# Optimizing a Trainium2 kernel written in Bass

```python
import math
import jax, jax.numpy as jnp
from jax import lax
import numpy as np

'''One inference step (DEPTH layers) of a hybrid decoder: parallel gated branches
(short gated convolution | gated DeltaNet | memory cross-attention) merged by
per-channel sigmoid gates, followed by a PEER product-key expert FFN.

Inputs:
  x_prompt (BATCH, SEQ, D_MODEL), x_sample (DEC_BATCH, DEC_SEQ, D_MODEL)
  mem_prompt (BATCH, MEM_TOKENS, D_MODEL)
  cache_mem_k, cache_mem_v (DEPTH, DEC_BATCH, MEM_TOKENS, MEM_HEADS, MEM_HEAD_DIM)
  state_conv (DEPTH, DEC_BATCH, CONV_K-1, CONV_WIDTH)
  state_gdn_conv (DEPTH, DEC_BATCH, GDN_CONV_K-1, GDN_CONV_CH)
  state_gdn (DEPTH, DEC_BATCH, GDN_HEADS, GDN_DK, GDN_DV)
  + weights.
Returns tuple:
  y_prompt (BATCH, SEQ, D_MODEL), y_sample (DEC_BATCH, DEC_SEQ, D_MODEL),
  new_mem_k_prompt, new_mem_v_prompt (DEPTH, BATCH, MEM_TOKENS, MEM_HEADS, MEM_HEAD_DIM),
  new_state_conv_prompt (DEPTH, BATCH, CONV_K-1, CONV_WIDTH),
  new_state_gdn_conv_prompt (DEPTH, BATCH, GDN_CONV_K-1, GDN_CONV_CH),
  new_state_gdn_prompt (DEPTH, BATCH, GDN_HEADS, GDN_DK, GDN_DV),
  new_state_conv_sample (DEPTH, DEC_BATCH, CONV_K-1, CONV_WIDTH),
  new_state_gdn_conv_sample (DEPTH, DEC_BATCH, GDN_CONV_K-1, GDN_CONV_CH),
  new_state_gdn_sample (DEPTH, DEC_BATCH, GDN_HEADS, GDN_DK, GDN_DV).
'''

D_MODEL = 1024
BATCH = 1
SEQ = 1024
DEPTH = 1
DEC_BATCH = 8
DEC_SEQ = 4
PAST_LEN = 8192
PAGE_SIZE = 128

CONV_WIDTH = D_MODEL
CONV_K = 3
GDN_HEADS = 8
GDN_DK = 128
GDN_DV = 128
GDN_CONV_K = 4
GDN_CHUNK = 64
GDN_QK = GDN_HEADS * GDN_DK
GDN_V = GDN_HEADS * GDN_DV
GDN_CONV_CH = 2 * GDN_QK + GDN_V
MEM_TOKENS = 256
MEM_HEADS = 4
MEM_HEAD_DIM = D_MODEL // MEM_HEADS
MEM_Q = MEM_HEADS * MEM_HEAD_DIM
PEER_HEADS = 8
PEER_N_KEYS = 128
PEER_N_EXPERTS = PEER_N_KEYS * PEER_N_KEYS
PEER_D_KEY = 256
PEER_D_HALF = PEER_D_KEY // 2
PEER_TOPK = 16
PEER_BLOCK = 256

N_BRANCHES = 3
EPS = 1e-6
SPLITS = (CONV_WIDTH, CONV_WIDTH, CONV_WIDTH,
          GDN_QK, GDN_QK, GDN_V, GDN_V, GDN_HEADS, GDN_HEADS,
          MEM_Q, N_BRANCHES * D_MODEL)
IN_COLS = 3 * CONV_WIDTH + 2 * GDN_QK + 2 * GDN_V + 2 * GDN_HEADS + MEM_Q + N_BRANCHES * D_MODEL

kernel_name = 'hybrid_conv_gdn_mem_peer_step'

def _split_cols(p):
    outs = []
    start = 0
    for width in SPLITS:
        outs.append(p[..., start:start + width])
        start += width
    return outs

def rmsnorm(x, g):
    xf = x.astype(jnp.float32)
    r = lax.rsqrt(jnp.mean(xf * xf, axis=-1, keepdims=True) + EPS)
    return (xf * r).astype(x.dtype) * g

def l2norm(x):
    xf = x.astype(jnp.float32)
    return xf * lax.rsqrt(jnp.sum(xf * xf, axis=-1, keepdims=True) + EPS)

def causal_dwconv(u, buf, w):
    K = w.shape[0]
    T = u.shape[1]
    full = jnp.concatenate([buf.astype(u.dtype), u], axis=1)
    y = sum(full[:, j:j + T] * w[j] for j in range(K))
    return y, full[:, T:]

def gated_delta_chunked(q, k, v, g, beta, S0):
    Bsz, T, H, dk = q.shape
    dv = v.shape[-1]
    C = math.gcd(T, GDN_CHUNK)
    N = T // C

    def to_chunks(a):
        a = a.astype(jnp.float32).reshape((Bsz, N, C, H) + a.shape[3:])
        return jnp.moveaxis(a, (1, 3), (0, 2))

    qc, kc, vc = to_chunks(q), to_chunks(k), to_chunks(v)
    gc = jnp.cumsum(to_chunks(g), axis=-1)
    bc = to_chunks(beta)
    tri_incl = jnp.tril(jnp.ones((C, C), dtype=bool))
    tri_strict = jnp.tril(jnp.ones((C, C), dtype=bool), -1)
    diff = gc[..., :, None] - gc[..., None, :]
    decay = jnp.exp(jnp.where(tri_incl, diff, -jnp.inf))
    kb = kc * bc[..., None]
    L = jnp.where(tri_strict, jnp.einsum('nbhid,nbhjd->nbhij', kb, kc) * decay, 0.0)
    eye = jnp.eye(C, dtype=jnp.float32)
    Tm = lax.linalg.triangular_solve(eye + L, jnp.broadcast_to(eye, L.shape), left_side=True, lower=True)
    u_val = jnp.einsum('nbhij,nbhjd->nbhid', Tm, vc * bc[..., None])
    w_k = jnp.einsum('nbhij,nbhjd->nbhid', Tm, kb * jnp.exp(gc)[..., None])
    attn = jnp.where(tri_incl, jnp.einsum('nbhid,nbhjd->nbhij', qc, kc) * decay, 0.0)
    q_dec = qc * jnp.exp(gc)[..., None]
    k_dec = kc * jnp.exp(gc[..., -1:] - gc)[..., None]
    g_last = jnp.exp(gc[..., -1])

    def step(S, inp):
        u_i, w_i, a_i, qd_i, kd_i, gl_i = inp
        v_new = u_i - jnp.einsum('bhcd,bhde->bhce', w_i, S)
        o = jnp.einsum('bhcd,bhde->bhce', qd_i, S) + jnp.einsum('bhij,bhje->bhie', a_i, v_new)
        S = S * gl_i[..., None, None] + jnp.einsum('bhcd,bhce->bhde', kd_i, v_new)
        return S, o

    S, o = lax.scan(step, S0.astype(jnp.float32), (u_val, w_k, attn, q_dec, k_dec, g_last))
    o = jnp.moveaxis(o, (0, 2), (1, 3)).reshape(Bsz, T, H, dv)
    return o, S

def mem_kv(mem, g, w_mem_kv):
    kv = rmsnorm(mem, g) @ w_mem_kv
    Bsz, M, _ = mem.shape
    mk = kv[..., :MEM_Q].reshape(Bsz, M, MEM_HEADS, MEM_HEAD_DIM)
    mv = kv[..., MEM_Q:].reshape(Bsz, M, MEM_HEADS, MEM_HEAD_DIM)
    return mk, mv

def mem_attend(q, mk, mv):
    s = jnp.einsum('bthd,bmhd->bhtm', q, mk.astype(q.dtype)).astype(jnp.float32) * (MEM_HEAD_DIM ** -0.5)
    p = jax.nn.softmax(s, axis=-1).astype(q.dtype)
    o = jnp.einsum('bhtm,bmhd->bthd', p, mv.astype(q.dtype))
    return o.reshape(q.shape[0], q.shape[1], MEM_Q)

def peer(x, w_q, sub_keys, u_tab, v_tab):
    Bsz, T, D = x.shape
    n = Bsz * T
    blk = math.gcd(n, PEER_BLOCK)

    def block(xb):
        q = (xb @ w_q).reshape(blk, PEER_HEADS, 2, PEER_D_HALF)
        s = jnp.einsum('nhpd,phkd->nhpk', q, sub_keys).astype(jnp.float32)
        sv, si = lax.top_k(s, PEER_TOPK)
        cand = (sv[:, :, 0, :, None] + sv[:, :, 1, None, :]).reshape(blk, PEER_HEADS, PEER_TOPK * PEER_TOPK)
        cidx = (si[:, :, 0, :, None] * PEER_N_KEYS + si[:, :, 1, None, :]).reshape(blk, PEER_HEADS, PEER_TOPK * PEER_TOPK)
        tv, ti = lax.top_k(cand, PEER_TOPK)
        eidx = jnp.take_along_axis(cidx, ti, axis=-1)
        gates = jax.nn.softmax(tv, axis=-1)
        u = jnp.take(u_tab, eidx, axis=0)
        act = jax.nn.gelu(jnp.einsum('nd,nhkd->nhk', xb, u).astype(jnp.float32), approximate=False)
        coef = (gates * act).astype(xb.dtype)
        return jnp.einsum('nhk,nhkd->nd', coef, jnp.take(v_tab, eidx, axis=0))

    y = lax.map(block, x.reshape(n // blk, blk, D))
    return y.reshape(Bsz, T, D)

def layer(x, mk, mv, conv_buf, gdn_buf, gdn_S,
          norm_mix_g, w_in, conv_w, gdn_conv_w, gdn_a_log, gdn_dt_bias, gdn_norm_g,
          w_br_conv, w_br_gdn, w_br_mem, w_out, norm_ffn_g, peer_w_q, peer_sub_keys, peer_u, peer_v):
    Bsz, T, _ = x.shape
    h = rmsnorm(x, norm_mix_g)
    (a_u, a_b, a_c, g_q, g_k, g_v, g_z, g_a, g_b, m_q, br_gates) = _split_cols(h @ w_in)
    ya, conv_buf_new = causal_dwconv(a_c * a_u, conv_buf, conv_w)
    ya = a_b * ya
    qkv, gdn_buf_new = causal_dwconv(jnp.concatenate([g_q, g_k, g_v], axis=-1), gdn_buf, gdn_conv_w)
    qkv = jax.nn.silu(qkv)
    q = l2norm(qkv[..., :GDN_QK].reshape(Bsz, T, GDN_HEADS, GDN_DK)) * (GDN_DK ** -0.5)
    k = l2norm(qkv[..., GDN_QK:2 * GDN_QK].reshape(Bsz, T, GDN_HEADS, GDN_DK))
    v = qkv[..., 2 * GDN_QK:].reshape(Bsz, T, GDN_HEADS, GDN_DV)
    beta = jax.nn.sigmoid(g_b.astype(jnp.float32))
    g_log = -jnp.exp(gdn_a_log.astype(jnp.float32)) * jax.nn.softplus(g_a.astype(jnp.float32) + gdn_dt_bias)
    o, S_new = gated_delta_chunked(q, k, v, g_log, beta, gdn_S)
    z = g_z.reshape(Bsz, T, GDN_HEADS, GDN_DV)
    yb = (rmsnorm(o.astype(x.dtype), gdn_norm_g) * jax.nn.silu(z)).reshape(Bsz, T, GDN_V)
    ym = mem_attend(m_q.reshape(Bsz, T, MEM_HEADS, MEM_HEAD_DIM), mk, mv)
    gates = jax.nn.sigmoid(br_gates).reshape(Bsz, T, N_BRANCHES, D_MODEL)
    merged = (gates[:, :, 0] * (ya @ w_br_conv) + gates[:, :, 1] * (yb @ w_br_gdn)
              + gates[:, :, 2] * (ym @ w_br_mem))
    x = x + merged @ w_out
    x = x + peer(rmsnorm(x, norm_ffn_g), peer_w_q, peer_sub_keys, peer_u, peer_v)
    return x, conv_buf_new, gdn_buf_new, S_new

def setup_inputs(seed: int = 0) -> dict:
    key = jax.random.key(seed)
    ks = jax.random.split(key, 32)
    f32 = jnp.float32

    def nrm(k, shape, s):
        return jax.random.normal(k, shape, f32) * s

    return {
        'x_prompt': nrm(ks[0], (BATCH, SEQ, D_MODEL), 1.0),
        'x_sample': nrm(ks[1], (DEC_BATCH, DEC_SEQ, D_MODEL), 1.0),
        'mem_prompt': nrm(ks[2], (BATCH, MEM_TOKENS, D_MODEL), 1.0),
        'cache_mem_k': nrm(ks[3], (DEPTH, DEC_BATCH, MEM_TOKENS, MEM_HEADS, MEM_HEAD_DIM), 1.0),
        'cache_mem_v': nrm(ks[4], (DEPTH, DEC_BATCH, MEM_TOKENS, MEM_HEADS, MEM_HEAD_DIM), 1.0),
        'state_conv': nrm(ks[5], (DEPTH, DEC_BATCH, CONV_K - 1, CONV_WIDTH), 1.0),
        'state_gdn_conv': nrm(ks[6], (DEPTH, DEC_BATCH, GDN_CONV_K - 1, GDN_CONV_CH), 1.0),
        'state_gdn': nrm(ks[7], (DEPTH, DEC_BATCH, GDN_HEADS, GDN_DK, GDN_DV), 0.1),
        'norm_mix_g': 1.0 + nrm(ks[8], (DEPTH, D_MODEL), 0.02),
        'w_in': nrm(ks[9], (DEPTH, D_MODEL, IN_COLS), D_MODEL ** -0.5),
        'conv_w': nrm(ks[10], (DEPTH, CONV_K, CONV_WIDTH), CONV_K ** -0.5),
        'gdn_conv_w': nrm(ks[11], (DEPTH, GDN_CONV_K, GDN_CONV_CH), GDN_CONV_K ** -0.5),
        'gdn_a_log': jnp.log(jax.random.uniform(ks[12], (DEPTH, GDN_HEADS), f32, 1.0, 16.0)),
        'gdn_dt_bias': nrm(ks[13], (DEPTH, GDN_HEADS), 0.1),
        'gdn_norm_g': 1.0 + nrm(ks[14], (DEPTH, GDN_DV), 0.02),
        'mem_norm_g': 1.0 + nrm(ks[15], (DEPTH, D_MODEL), 0.02),
        'w_mem_kv': nrm(ks[16], (DEPTH, D_MODEL, 2 * MEM_Q), D_MODEL ** -0.5),
        'w_br_conv': nrm(ks[17], (DEPTH, CONV_WIDTH, D_MODEL), CONV_WIDTH ** -0.5),
        'w_br_gdn': nrm(ks[18], (DEPTH, GDN_V, D_MODEL), GDN_V ** -0.5),
        'w_br_mem': nrm(ks[19], (DEPTH, MEM_Q, D_MODEL), MEM_Q ** -0.5),
        'w_out': nrm(ks[20], (DEPTH, D_MODEL, D_MODEL), D_MODEL ** -0.5),
        'norm_ffn_g': 1.0 + nrm(ks[21], (DEPTH, D_MODEL), 0.02),
        'peer_w_q': nrm(ks[22], (DEPTH, D_MODEL, PEER_HEADS * PEER_D_KEY), D_MODEL ** -0.5),
        'peer_sub_keys': nrm(ks[23], (DEPTH, 2, PEER_HEADS, PEER_N_KEYS, PEER_D_HALF), PEER_D_HALF ** -0.5),
        'peer_u': nrm(ks[24], (DEPTH, PEER_N_EXPERTS, D_MODEL), D_MODEL ** -0.5),
        'peer_v': nrm(ks[25], (DEPTH, PEER_N_EXPERTS, D_MODEL), PEER_HEADS ** -0.5),
        'final_norm_g': 1.0 + nrm(ks[26], (D_MODEL,), 0.02),
    }

def reference(x_prompt, x_sample, mem_prompt, cache_mem_k, cache_mem_v, state_conv, state_gdn_conv, state_gdn,
              norm_mix_g, w_in, conv_w, gdn_conv_w, gdn_a_log, gdn_dt_bias, gdn_norm_g, mem_norm_g, w_mem_kv,
              w_br_conv, w_br_gdn, w_br_mem, w_out, norm_ffn_g, peer_w_q, peer_sub_keys, peer_u, peer_v,
              final_norm_g):
    xp, xs = x_prompt, x_sample
    mk_p_l, mv_p_l, cb_p_l, gb_p_l, S_p_l = [], [], [], [], []
    cb_s_l, gb_s_l, S_s_l = [], [], []
    for l in range(DEPTH):
        params = (norm_mix_g[l], w_in[l], conv_w[l], gdn_conv_w[l], gdn_a_log[l], gdn_dt_bias[l], gdn_norm_g[l],
                  w_br_conv[l], w_br_gdn[l], w_br_mem[l], w_out[l], norm_ffn_g[l], peer_w_q[l], peer_sub_keys[l],
                  peer_u[l], peer_v[l])
        mk_p, mv_p = mem_kv(mem_prompt, mem_norm_g[l], w_mem_kv[l])
        zero_cb = jnp.zeros((xp.shape[0], CONV_K - 1, CONV_WIDTH), xp.dtype)
        zero_gb = jnp.zeros((xp.shape[0], GDN_CONV_K - 1, GDN_CONV_CH), xp.dtype)
        zero_S = jnp.zeros((xp.shape[0], GDN_HEADS, GDN_DK, GDN_DV), jnp.float32)
        xp, cb_p, gb_p, S_p = layer(xp, mk_p, mv_p, zero_cb, zero_gb, zero_S, *params)
        xs, cb_s, gb_s, S_s = layer(xs, cache_mem_k[l], cache_mem_v[l], state_conv[l], state_gdn_conv[l],
                                    state_gdn[l], *params)
        mk_p_l.append(mk_p); mv_p_l.append(mv_p); cb_p_l.append(cb_p); gb_p_l.append(gb_p); S_p_l.append(S_p)
        cb_s_l.append(cb_s); gb_s_l.append(gb_s); S_s_l.append(S_s)
    y_prompt = rmsnorm(xp, final_norm_g)
    y_sample = rmsnorm(xs, final_norm_g)
    new_mem_k_prompt = jnp.stack(mk_p_l)
    new_mem_v_prompt = jnp.stack(mv_p_l)
    new_state_conv_prompt = jnp.stack(cb_p_l)
    new_state_gdn_conv_prompt = jnp.stack(gb_p_l)
    new_state_gdn_prompt = jnp.stack(S_p_l)
    new_state_conv_sample = jnp.stack(cb_s_l)
    new_state_gdn_conv_sample = jnp.stack(gb_s_l)
    new_state_gdn_sample = jnp.stack(S_s_l)
    return (y_prompt, y_sample, new_mem_k_prompt, new_mem_v_prompt, new_state_conv_prompt,
            new_state_gdn_conv_prompt, new_state_gdn_prompt, new_state_conv_sample,
            new_state_gdn_conv_sample, new_state_gdn_sample)


_drawn_inputs = setup_inputs


def setup_inputs(seed=0):
    import zlib

    import numpy as np

    out = dict(_drawn_inputs(seed))
    spreads = {}
    factors = {'gdn_dt_bias': 4.249,
     'gdn_norm_g': 13.827,
     'mem_norm_g': 8.043,
     'final_norm_g': 21.554,
     'norm_ffn_g': 11.214,
     'cache_mem_k': 3.65,
     'cache_mem_v': 2.807}
    for name, (base, spread) in spreads.items():
        noise = np.random.default_rng([zlib.crc32(name.encode()), seed]).standard_normal(out[name].shape)
        drawn = base * np.exp(spread * noise) if base else spread * noise
        out[name] = __import__('jax').numpy.asarray(drawn.astype(out[name].dtype))
    for name, factor in factors.items():
        out[name] = (out[name] * factor).astype(out[name].dtype)
    return out
```

```python
from contextlib import ExitStack

import concourse.bass as bass
from concourse import mybir

P = 128
F32 = mybir.dt.float32
F32R = mybir.dt.float32r
I32 = mybir.dt.int32
U32 = mybir.dt.uint32
ALU = mybir.AluOpType
ACT = mybir.ActivationFunctionType
X = mybir.AxisListType.X
ds = bass.ds

D = 1024
KT = D // P
TP = 1024
NB, TS = 8, 4
NS = NB * TS
N = TP + NS
NCH = 3
CH = N // NCH
NT = 9
CK, GK = 3, 4
H = 8
M = 256
MT = M // P
MH = 4
TOPK = 16
NE = 16384
EPS = 1e-6

COL_U, COL_B, COL_C, COL_QKV, COL_Z, COL_AB = 0, D, 2 * D, 3 * D, 6 * D, 7 * D
COL_MQ = COL_AB + 2 * H
COL_GATE = COL_MQ + D

A_TAP = NB * (CK - 1)
A_GAIN = A_TAP + CK
A_ROWS = A_GAIN + 4
MIX, FFN, FINAL, MEM = range(4)
G_TAP = NB * (GK - 1)
G_ROWS = G_TAP + GK
A_OUT = (NB + 1) * (CK - 1)
G_OUT = (NB + 1) * (GK - 1)


def chunk(c):
    return slice(c * CH, (c + 1) * CH)


def make_constants(nc, k, io):
    with ExitStack() as ctx:
        rows_a = ctx.enter_context(nc.sbuf_tensor("rows_a", [A_ROWS, D], F32))
        rows_g = ctx.enter_context(nc.sbuf_tensor("rows_g", [G_ROWS, 3 * D], F32))
        ps = ctx.enter_context(nc.psum_tensor("ps_const", [P, 2, 512], F32))
        rows_in = nc.alloc_semaphore("rows_in")
        small_in = nc.alloc_semaphore("small_in")
        filled = nc.alloc_semaphore("filled")
        made = nc.alloc_semaphore("made")
        turned = nc.alloc_semaphore("turned")
        kept = nc.alloc_semaphore("kept")
        block = ctx.enter_context(nc.Block())

        @block.sync
        def _(sp):
            sp.dma_start(rows_a[0:A_TAP, :], io["state_conv"].rearrange("b t c -> (b t) c")).then_inc(rows_in, 16)
            sp.dma_start(rows_a[A_TAP:A_GAIN, :], io["conv_w"]).then_inc(rows_in, 16)
            for n, name in enumerate(("norm_mix_g", "norm_ffn_g", "final_norm_g", "mem_norm_g")):
                sp.dma_start(rows_a[A_GAIN + n:A_GAIN + n + 1, :], io[name]).then_inc(rows_in, 16)
            sp.dma_start(rows_g[0:G_TAP, :], io["state_gdn_conv"].rearrange("b t c -> (b t) c")).then_inc(rows_in, 16)
            sp.dma_start(rows_g[G_TAP:G_ROWS, :], io["gdn_conv_w"]).then_inc(rows_in, 16)
            sp.dma_start(k["gdn_gain"][:, :], io["gdn_norm_g"].rearrange("(p o) -> p o", o=1)).then_inc(small_in, 16)
            sp.dma_start(k["dt_bias"][:, :], io["gdn_dt_bias"].partition_broadcast(P)).then_inc(small_in, 16)
            sp.dma_start(k["a_log"][:, :], io["gdn_a_log"].partition_broadcast(P)).then_inc(small_in, 16)
            sp.wait_ge(small_in, 48)

        @block.gpsimd
        def _(pool):
            pool.memset(k["ones"][:, :], 1.0).then_inc(filled, 1)
            pool.memset(k["eps"][:, :], EPS).then_inc(filled, 1)
            pool.memset(k["ident"][:, :], 0.0).then_inc(filled, 1)
            pool.iota(k["iota_i"][:, :], [[1, P]], base=0, channel_multiplier=0).then_inc(filled, 1)
            pool.wait_ge(filled, 4)
            pool.tensor_copy(k["iota"][:, :], k["iota_i"][:, :]).then_inc(made, 1)
            pool.affine_select(out=k["ident"][:, :], in_=k["ident"][:, :], compare_op=ALU.not_equal, fill=1.0,
                               base=0, pattern=[[-1, P]], channel_multiplier=1).then_inc(made, 1)
            pool.affine_select(out=k["upto"][:, :], in_=k["ones"][:, :], compare_op=ALU.is_ge, fill=0.0,
                               base=0, pattern=[[1, P]], channel_multiplier=-1).then_inc(made, 1)
            pool.affine_select(out=k["after"][:, :], in_=k["ones"][:, :], compare_op=ALU.is_ge, fill=0.0,
                               base=-1, pattern=[[-1, P]], channel_multiplier=1).then_inc(made, 1)
            sb = k["same_seq"]
            v = sb[:, :].rearrange("p (b t) -> p b t", t=TS)
            pool.affine_select(out=v, in_=k["ones"][0:NS, 0:NS].rearrange("p (b t) -> p b t", t=TS),
                               compare_op=ALU.is_ge, fill=0.0, base=0, pattern=[[-TS, NB], [0, TS]],
                               channel_multiplier=1).then_inc(made, 1)
            pool.wait_ge(made, 5)
            pool.affine_select(out=v, in_=v, compare_op=ALU.is_ge, fill=0.0, base=TS - 1,
                               pattern=[[TS, NB], [0, TS]], channel_multiplier=-1).then_inc(made, 1)
            pool.wait_ge(made, 6)

        @block.tensor
        def _(pe):
            pe.wait_ge(rows_in, 16 * 8)
            pe.wait_ge(made, 2)
            for t in range(KT):
                pe.transpose(ps[:, 0, 32 * t:32 * t + A_ROWS], rows_a[:, t * P:(t + 1) * P],
                             k["ident"][0:A_ROWS, 0:A_ROWS]).then_inc(turned, 1)
            for g in range(3):
                if g:
                    pe.wait_ge(kept, g + 1)
                for t in range(KT):
                    c = g * KT + t
                    pe.transpose(ps[:, 1, 32 * t:32 * t + G_ROWS], rows_g[:, c * P:(c + 1) * P],
                                 k["ident"][0:G_ROWS, 0:G_ROWS]).then_inc(turned, 1)

        @block.vector
        def _(dve):
            for g in range(4):
                dve.wait_ge(turned, KT * (g + 1))
                dst = k["chan_a"][:, :, :] if g == 0 else k["chan_g"][:, (g - 1) * KT:g * KT, :]
                rows = A_ROWS if g == 0 else G_ROWS
                src = ps[:, min(g, 1), 0:32 * KT].rearrange("p (t r) -> p t r", r=32)
                dve.tensor_copy(dst[:, :, 0:rows], src[:, :, 0:rows]).then_inc(kept, 1)
            dve.wait_ge(kept, 4)


def turn_rows(nc, k, rows_dram, xT, n_tiles, name, save=None):
    total = rows_dram.shape[0]
    with ExitStack() as ctx:
        rows = ctx.enter_context(nc.sbuf_tensor(name + "_rows", [P, 2, D], F32))
        ps = ctx.enter_context(nc.psum_tensor(name + "_ps", [P, 2, 2, 512], F32))
        landed = [nc.alloc_semaphore(f"{name}_landed{s}") for s in range(2)]
        turned = nc.alloc_semaphore(name + "_turned")
        kept = nc.alloc_semaphore(name + "_kept")
        saved = nc.alloc_semaphore(name + "_saved")
        block = ctx.enter_context(nc.Block())
        size = [min(P, total - t * P) for t in range(n_tiles)]

        @block.sync
        def _(sp):
            for t in range(n_tiles):
                if t >= 2:
                    sp.wait_ge(turned, t - 1)
                sp.dma_start(rows[0:size[t], t % 2, :], rows_dram[t * P:t * P + size[t], :]).then_inc(landed[t % 2], 16)
            if save is not None:
                sp.wait_ge(kept, n_tiles)
                sp.dma_start(save, xT[:, :, :]).then_inc(saved, 16)
                sp.wait_ge(saved, 16)

        @block.tensor
        def _(pe):
            for t in range(n_tiles):
                pe.wait_ge(landed[t % 2], 16 * (t // 2 + 1))
                if t >= 2:
                    pe.wait_ge(kept, t - 1)
                for c in range(KT):
                    last = pe.transpose(ps[:, t % 2, c // 4, (c % 4) * P:(c % 4) * P + size[t]],
                                        rows[0:size[t], t % 2, c * P:(c + 1) * P],
                                        k["ident"][0:size[t], 0:size[t]])
                last.then_inc(turned, 1)

        @block.scalar
        def _(act):
            for t in range(n_tiles):
                act.wait_ge(turned, t + 1)
                for b in range(2):
                    src = ps[:, t % 2, b, :].rearrange("p (c n) -> p c n", n=P)[:, :, 0:size[t]]
                    last = act.copy(xT[:, 4 * b:4 * b + 4, t * P:t * P + size[t]], src)
                last.then_inc(kept, 1)


def norm_channels(nc, k, xT, gain, width, name, high=None, low=None, out=None):
    nch = max(1, -(-width // 512))
    w = width // nch
    with ExitStack() as ctx:
        sq = ctx.enter_context(nc.sbuf_tensor(name + "_sq", [P, 2, width], F32))
        root = ctx.enter_context(nc.sbuf_tensor(name + "_root", [P, width], F32))
        rinv = ctx.enter_context(nc.sbuf_tensor(name + "_rinv", [P, width], F32))
        full = out if out is not None else ctx.enter_context(nc.sbuf_tensor(name + "_full", [P, 2, width], F32))
        ps = ctx.enter_context(nc.psum_tensor(name + "_ps", [P, nch, 512], F32))
        squared = nc.alloc_semaphore(name + "_squared")
        summed = nc.alloc_semaphore(name + "_summed")
        rooted = nc.alloc_semaphore(name + "_rooted")
        inverted = nc.alloc_semaphore(name + "_inverted")
        normed = nc.alloc_semaphore(name + "_normed")
        high_made = nc.alloc_semaphore(name + "_high")
        low_made = nc.alloc_semaphore(name + "_low")
        block = ctx.enter_context(nc.Block())
        ring = out is None

        def full_of(c):
            return full[:, c % 2, :] if ring else full[:, c, :]

        @block.scalar
        def _(act):
            for c in range(KT):
                if c >= 2:
                    act.wait_ge(summed, c - 1)
                act.activation(sq[:, c % 2, :], xT[:, c, :], ACT.Square).then_inc(squared, 1)
            act.wait_ge(summed, KT)
            for c in range(nch):
                act.activation(root[:, c * w:(c + 1) * w], ps[:, c, 0:w], ACT.Sqrt, bias=k["eps"][:, 0:1],
                               scale=1.0 / D).then_inc(rooted, 1)
            if ring:
                for c in range(KT):
                    act.wait_ge(normed, c + 1)
                    act.copy(high[:, c, :], full_of(c)).then_inc(high_made, 1)

        @block.tensor
        def _(pe):
            for c in range(KT):
                pe.wait_ge(squared, c + 1)
                for n in range(nch):
                    last = pe.matmul(ps[:, n, 0:w], k["ones"][:, :], sq[:, c % 2, n * w:(n + 1) * w],
                                     start=(c == 0), stop=(c == KT - 1))
                last.then_inc(summed, 1)

        @block.vector
        def _(dve):
            dve.wait_ge(rooted, nch)
            dve.reciprocal(rinv[:, :], root[:, :]).then_inc(inverted, 1)
            dve.wait_ge(inverted, 1)
            for c in range(KT):
                if ring and c >= 2:
                    dve.wait_ge(low_made, c - 1)
                dve.scalar_tensor_tensor(out=full_of(c), in0=xT[:, c, :], scalar=gain[:, c, :], in1=rinv[:, :],
                                         op0=ALU.mult, op1=ALU.mult).then_inc(normed, 1)
                if ring:
                    dve.wait_ge(high_made, c + 1)
                    dve.tensor_tensor(low[:, c, :], full_of(c), high[:, c, :].bitcast(F32),
                                      ALU.subtract).then_inc(low_made, 1)


class Weights:

    def __init__(self, nc, ctx, name):
        def sem(n):
            return nc.alloc_semaphore(f"{name}_{n}")

        self.raw = ctx.enter_context(nc.sbuf_tensor(name + "_raw", [P, 2, KT, P], F32))
        self.high = [ctx.enter_context(nc.sbuf_tensor(f"{name}_high{s}", [P, KT, P], F32R)) for s in range(2)]
        self.low = [ctx.enter_context(nc.sbuf_tensor(f"{name}_low{s}", [P, KT, P], F32R)) for s in range(2)]
        self.landed = [sem("landed0"), sem("landed1")]
        self.high_made = sem("high_made")
        self.low_made = sem("low_made")
        self.product_done = sem("product_done")
        self.passed = sem("passed")


def load_weights(sp, wt, dram, column, w, s, first=False):
    if not first:
        sp.wait_ge(wt.low_made, w - 1)
    sp.dma_start(wt.raw[:, s, :, :], dram[:, ds(column, P)].rearrange("(k p) c -> p k c", p=P)).then_inc(wt.landed[s], 16)


def pass_waits(eng, passed):
    eng.sem_inc(passed, 1)


def cut_weights(pool, wt, s, turn, w, first=False):
    pool.wait_ge(wt.landed[s], 16 * turn + 16)
    if not first:
        pool.wait_ge(wt.product_done, w - 1)
        pass_waits(pool, wt.passed)
    pool.tensor_copy(wt.high[s][:, :, :], wt.raw[:, s, :, :]).then_inc(wt.high_made, 1)
    pool.wait_ge(wt.high_made, w + 1)
    pool.tensor_tensor(wt.low[s][:, :, :], wt.raw[:, s, :, :], wt.high[s][:, :, :].bitcast(F32),
                       ALU.subtract).then_inc(wt.low_made, 1)


def multiply(pe, wt, high, low, banks, s, rows=P):
    for n in range(NCH):
        for kk in range(KT):
            for a, b in ((wt.high[s], high), (wt.high[s], low), (wt.low[s], high)):
                last = pe.matmul(banks[0:rows, n, 0:CH], a[:, kk, 0:rows], b[:, kk, chunk(n)],
                                 start=(kk == 0 and a is wt.high[s] and b is high),
                                 stop=(kk == KT - 1 and a is wt.low[s]))
        if n == NCH - 1:
            last.then_inc(wt.product_done, 1)


class Steps:

    def __init__(self, eng, sem, base=0):
        self.eng, self.sem, self.base, self.n = eng, sem, base, 0

    def did(self, instruction):
        instruction.then_inc(self.sem, 1)
        self.n += 1

    def wait(self):
        self.eng.wait_ge(self.sem, self.base + self.n)


RUNS = (("conv", 3 * KT, 6), ("qkv", 3 * KT, 2), ("z", KT, 2), ("mq", KT, 2), ("gate", 3 * KT, 2))


def run_column(name, pair, u):
    if name == "conv":
        return (COL_U, COL_B, COL_C)[u % 3] + (pair * 2 + u // 3) * P
    return {"qkv": COL_QKV, "z": COL_Z, "mq": COL_MQ, "gate": COL_GATE}[name] + (pair * 2 + u) * P


def project_in(nc, k, io, tmp, high, low):
    starts, total = {}, 0
    for name, tiles, _ in RUNS:
        starts[name] = total
        total += tiles
    conv_steps = 3 + 1 + CK - 1 + 1
    qkv_steps = 1 + GK - 1
    with ExitStack() as ctx:
        def sb(name, shape, dt=F32):
            return ctx.enter_context(nc.sbuf_tensor(name, shape, dt))

        def sem(name):
            return nc.alloc_semaphore(name)

        wt = Weights(nc, ctx, "w_in")
        ps = ctx.enter_context(nc.psum_tensor("p_in", [P, 2, 4, 512], F32))
        plain = sb("plain", [P, 2, N])
        gate_u, gate_b, gate_c = (sb(n, [P, 2, N]) for n in ("gate_u", "gate_b", "gate_c"))
        conv_in = sb("conv_in", [P, 2, GK - 1 + TP])
        conv_in_s = sb("conv_in_s", [P, 2, NB, GK - 1 + TS])
        conv_out = sb("conv_out", [P, 2, N])
        tap_now = sb("tap_now", [P, 2, GK])
        new_a = sb("new_a", [P, KT, A_OUT])
        new_g = sb("new_g", [P, 3 * KT, G_OUT])
        w_ab = sb("w_ab", [P, KT, 2 * H])
        w_ab_high = sb("w_ab_high", [P, KT, 2 * H], F32R)
        w_ab_low = sb("w_ab_low", [P, KT, 2 * H], F32R)
        ab = sb("ab", [2 * H, NT * P])
        ab_rows = sb("ab_rows", [P, NT, 2 * H])
        soft = sb("soft", [P, 4, NT, H])
        state_rows_g = sb("state_rows_g", [G_OUT, 3 * D])
        state_rows_a = sb("state_rows_a", [A_OUT, D])
        evacuated = sem("evacuated")
        conv_step = sem("conv_step")
        convolved = sem("convolved")
        ready = sem("ready")
        stored = [sem("stored0"), sem("stored1")]
        ab_in, ab_cut, ab_done, ab_kept = sem("ab_in"), sem("ab_cut"), sem("ab_done"), sem("ab_kept")
        rows_done, soft_step, soft_act = sem("rows_done"), sem("soft_step"), sem("soft_act")
        states_turned, states_kept, states_out = sem("states_turned"), sem("states_kept"), sem("states_out")
        block = ctx.enter_context(nc.Block())

        @block.sync
        def _(sp):
            sp.dma_start(w_ab[:, :, :], io["w_in"][:, COL_AB:COL_AB + 2 * H].rearrange("(k p) c -> p k c", p=P)).then_inc(ab_in, 16)
            for name, tiles, per in RUNS:
                if name == "conv":
                    for u in range(per):
                        load_weights(sp, wt, io["w_in"], run_column(name, 0, u), u, u % 2, first=u < 2)
                with sp.Fori(1 if name == "conv" else 0, tiles // per) as i:
                    for u in range(per):
                        w = starts[name] + i * per + u
                        load_weights(sp, wt, io["w_in"], run_column(name, i, u), w, u % 2)
            sp.wait_ge(states_kept, 8)
            for dst, src in ((io["out_conv_p"], state_rows_a[0:CK - 1, :]), (io["out_conv_s"], state_rows_a[CK - 1:A_OUT, :]),
                             (io["out_gconv_p"], state_rows_g[0:GK - 1, :]), (io["out_gconv_s"], state_rows_g[GK - 1:G_OUT, :])):
                sp.dma_start(dst, src).then_inc(states_out, 16)
            sp.wait_ge(states_out, 64)

        @block.gpsimd
        def _(pool):
            for u in range(2):
                cut_weights(pool, wt, u, 0, u, first=True)
            with pool.Fori(1, total // 2) as i:
                for u in range(2):
                    cut_weights(pool, wt, u, i, 2 * i + u)

        @block.tensor
        def _(pe):
            def tile(s, w, first=False):
                pe.wait_ge(wt.low_made, w + 1)
                if not first:
                    pe.wait_ge(evacuated, w - 1)
                multiply(pe, wt, high, low, ps[:, s, :, :], s)

            pe.wait_ge(ab_cut, 2)
            for n in range(NCH):
                if n:
                    pe.wait_ge(ab_kept, n + 1)
                for kk in range(KT):
                    for a, b in ((w_ab_high, high), (w_ab_high, low), (w_ab_low, high)):
                        last = pe.matmul(ps[0:2 * H, 0, 3, 0:CH], a[:, kk, :], b[:, kk, chunk(n)],
                                         start=(kk == 0 and a is w_ab_high and b is high),
                                         stop=(kk == KT - 1 and a is w_ab_low))
                last.then_inc(ab_done, 1)
            pe.wait_ge(ab_kept, NCH + 1)
            for t in range(NT):
                last = pe.transpose(ps[:, 1, 3, t * 2 * H:(t + 1) * 2 * H], ab[:, t * P:(t + 1) * P],
                                    k["ident"][0:2 * H, 0:2 * H])
            last.then_inc(rows_done, 1)
            for s in range(2):
                tile(s, s, first=True)
            with pe.Fori(1, total // 2) as i:
                for s in range(2):
                    tile(s, 2 * i + s)
            pe.wait_ge(convolved, 4 * KT)
            for q in range(8):
                g, half = q // 2, q % 2
                if q:
                    pe.wait_ge(states_kept, q)
                for t in range(4):
                    c = 4 * half + t
                    src = new_a[:, c, :] if g == 0 else new_g[:, (g - 1) * KT + c, :]
                    rows = A_OUT if g == 0 else G_OUT
                    last = pe.transpose(ps[0:rows, 0, 3, t * P:(t + 1) * P], src, k["ident"][:, :])
                last.then_inc(states_turned, 1)

        @block.scalar
        def _(act):
            act.wait_ge(soft_step, 4)
            act.activation(soft[:, 1, :, :], soft[:, 1, :, :], ACT.Exp, scale=-1.0).then_inc(soft_act, 1)
            act.activation(k["a_log"][:, :], k["a_log"][:, :], ACT.Exp).then_inc(soft_act, 1)
            act.wait_ge(soft_act, 1)
            act.activation(soft[:, 1, :, :], soft[:, 1, :, :], ACT.Ln, bias=k["ones"][:, 0:1]).then_inc(soft_act, 1)
            act.activation(k["beta"][:, :, :], ab_rows[:, :, H:2 * H], ACT.Sigmoid).then_inc(soft_act, 1)

            def conv_turn(i, first=False):
                for v in range(2):
                    if not first:
                        act.wait_ge(convolved, 2 * i + v - 1)
                    for j, dst in enumerate((gate_u, gate_b, gate_c)):
                        u = 3 * v + j
                        act.wait_ge(wt.product_done, 6 * i + u + 1)
                        for n in range(NCH):
                            last = act.copy(dst[:, v, chunk(n)], ps[:, u % 2, n, 0:CH])
                        last.then_inc(evacuated, 1)
                    act.wait_ge(convolved, 2 * i + v + 1)
                    act.dma_start(tmp["ya"][:, ds(2 * i + v, 1), :], plain[:, v:v + 1, :]).then_inc(stored[v], 16)

            conv_turn(0, first=True)
            with act.Fori(1, KT // 2) as i:
                conv_turn(i)

            with act.Fori(0, 3 * KT // 2) as i:
                for s in range(2):
                    act.wait_ge(wt.product_done, starts["qkv"] + 2 * i + s + 1)
                    src = ps[:, s, :, :]
                    act.copy(conv_in[:, s, GK - 1:GK - 1 + CH], src[:, 0, 0:CH])
                    act.copy(conv_in[:, s, GK - 1 + CH:GK - 1 + 2 * CH], src[:, 1, 0:CH])
                    act.copy(conv_in[:, s, GK - 1 + 2 * CH:GK - 1 + TP], src[:, 2, 0:TP - 2 * CH])
                    act.copy(conv_in_s[:, s, :, GK - 1:GK - 1 + TS],
                             src[:, 2, TP - 2 * CH:CH].rearrange("p (b t) -> p b t", t=TS)).then_inc(evacuated, 1)
                    act.wait_ge(convolved, KT + 2 * i + s + 1)
                    act.wait_ge(stored[s], 16 * (KT // 2) + 16 * i)
                    act.activation(plain[:, s, :], conv_out[:, s, :], ACT.Silu).then_inc(ready, 1)
                    act.wait_ge(ready, 2 * i + s + 1)
                    act.dma_start(tmp["qkv"][:, ds(2 * i + s, 1), :], plain[:, s:s + 1, :]).then_inc(stored[s], 16)
            n_stored = 2 * KT
            for name, tiles, func in (("z", KT, ACT.Silu), ("mq", KT, ACT.Copy), ("gate", 3 * KT, ACT.Sigmoid)):
                with act.Fori(0, tiles // 2) as i:
                    for s in range(2):
                        w = starts[name] + 2 * i + s
                        act.wait_ge(stored[s], 16 * n_stored + 16 * i)
                        act.wait_ge(wt.product_done, w + 1)
                        for n in range(NCH):
                            last = act.activation(plain[:, s, chunk(n)], ps[:, s, n, 0:CH], func)
                        last.then_inc(evacuated, 1)
                        act.wait_ge(evacuated, w + 1)
                        act.dma_start(tmp[name][:, ds(2 * i + s, 1), :], plain[:, s:s + 1, :]).then_inc(stored[s], 16)
                n_stored += tiles // 2
            for s in range(2):
                act.wait_ge(stored[s], 16 * n_stored)

        @block.vector
        def _(dve):
            dve.wait_ge(ab_in, 16)
            dve.tensor_copy(w_ab_high[:, :, :], w_ab[:, :, :]).then_inc(ab_cut, 1)
            dve.memset(ab[:, N:NT * P], 0.0).then_inc(ab_kept, 1)
            dve.memset(conv_in[:, :, 0:GK - 1], 0.0)
            dve.wait_ge(ab_cut, 1)
            dve.tensor_tensor(w_ab_low[:, :, :], w_ab[:, :, :], w_ab_high[:, :, :].bitcast(F32),
                              ALU.subtract).then_inc(ab_cut, 1)
            for n in range(NCH):
                dve.wait_ge(ab_done, n + 1)
                dve.tensor_copy(ab[:, chunk(n)], ps[0:2 * H, 0, 3, 0:CH]).then_inc(ab_kept, 1)
            dve.wait_ge(rows_done, 1)
            own = Steps(dve, soft_step)
            own.did(dve.tensor_copy(ab_rows[:, :, :], ps[:, 1, 3, 0:NT * 2 * H].rearrange("p (t c) -> p t c", c=2 * H)))
            own.wait()
            bias = k["dt_bias"][:, :].unsqueeze(1).broadcast_to([P, NT, H])
            own.did(dve.tensor_tensor(soft[:, 0, :, :], ab_rows[:, :, 0:H], bias, ALU.add))
            own.wait()
            own.did(dve.tensor_scalar(soft[:, 2, :, :], soft[:, 0, :, :], 0.0, None, ALU.max))
            own.wait()
            own.did(dve.scalar_tensor_tensor(out=soft[:, 1, :, :], in0=soft[:, 2, :, :], scalar=2.0,
                                             in1=soft[:, 0, :, :], op0=ALU.mult, op1=ALU.subtract))
            own.wait()
            dve.wait_ge(soft_act, 3)
            own.did(dve.tensor_tensor(soft[:, 3, :, :], soft[:, 1, :, :], soft[:, 2, :, :], ALU.add))
            own.wait()
            rate = k["a_log"][:, :].unsqueeze(1).broadcast_to([P, NT, H])
            own.did(dve.tensor_tensor(soft[:, 0, :, :], soft[:, 3, :, :], rate, ALU.mult))
            own.wait()
            dve.tensor_scalar(k["glog"][:, :, :], soft[:, 0, :, :], -1.0, None, ALU.mult)

            def taps(own, s, kk):
                prompt = conv_in[:, s, GK - kk:GK - 1 + TP]
                samples = conv_in_s[:, s, :, GK - kk:GK - 1 + TS]
                out_s = conv_out[:, s, TP:N].rearrange("p (b t) -> p b t", t=TS)
                for j in range(kk):
                    a, b, tap = prompt[:, j:j + TP], samples[:, :, j:j + TS], tap_now[:, s, j:j + 1]
                    if j == 0:
                        dve.tensor_scalar(conv_out[:, s, 0:TP], a, tap, None, ALU.mult)
                        last = dve.tensor_scalar(out_s, b, tap, None, ALU.mult)
                    else:
                        own.wait()
                        dve.scalar_tensor_tensor(out=conv_out[:, s, 0:TP], in0=a, scalar=tap,
                                                 in1=conv_out[:, s, 0:TP], op0=ALU.mult, op1=ALU.add)
                        last = dve.scalar_tensor_tensor(out=out_s, in0=b, scalar=tap, in1=out_s,
                                                        op0=ALU.mult, op1=ALU.add)
                    if j < kk - 1:
                        own.did(last)
                return last

            def load_taps(own, s, c, chan, state, kk):
                own.did(dve.tensor_copy(conv_in_s[:, s, :, GK - kk:GK - 1],
                                        chan[:, ds(c, 1), 0:state].rearrange("p o (b t) -> p (o b) t", t=kk - 1)))
                own.did(dve.tensor_copy(tap_now[:, s:s + 1, 0:kk], chan[:, ds(c, 1), state:state + kk]))

            def keep_state(s, c, new, kk):
                dve.tensor_copy(new[:, ds(c, 1), 0:kk - 1], conv_in[:, s:s + 1, TP + GK - kk:TP + GK - 1])
                return dve.tensor_copy(new[:, ds(c, 1), kk - 1:(NB + 1) * (kk - 1)].rearrange("p o (b t) -> p (o b) t", t=kk - 1),
                                       conv_in_s[:, s, :, TS + GK - kk:TS + GK - 1])

            def conv_turn(i, first=False):
                for v in range(2):
                    own = Steps(dve, conv_step, (2 * i + v) * conv_steps)
                    load_taps(own, v, 2 * i + v, k["chan_a"], A_TAP, CK)
                    dve.wait_ge(evacuated, 6 * i + 3 * v + 3)
                    dve.tensor_tensor(conv_in[:, v, GK - 1:GK - 1 + TP], gate_c[:, v, 0:TP], gate_u[:, v, 0:TP], ALU.mult)
                    own.did(dve.tensor_tensor(conv_in_s[:, v, :, GK - 1:GK - 1 + TS],
                                              gate_c[:, v, TP:N].rearrange("p (b t) -> p b t", t=TS),
                                              gate_u[:, v, TP:N].rearrange("p (b t) -> p b t", t=TS), ALU.mult))
                    own.wait()
                    own.did(keep_state(v, 2 * i + v, new_a, CK))
                    own.did(taps(own, v, CK))
                    own.wait()
                    assert own.n == conv_steps
                    if not first:
                        dve.wait_ge(stored[v], 16 * i)
                    dve.tensor_tensor(plain[:, v, :], conv_out[:, v, :], gate_b[:, v, :], ALU.mult).then_inc(convolved, 1)

            conv_turn(0, first=True)
            with dve.Fori(1, KT // 2) as i:
                conv_turn(i)

            def qkv_turn(i, first=False):
                for s in range(2):
                    own = Steps(dve, conv_step, KT * conv_steps + (2 * i + s) * (qkv_steps + 2))
                    load_taps(own, s, 2 * i + s, k["chan_g"], G_TAP, GK)
                    if not first:
                        dve.wait_ge(ready, 2 * i + s - 1)
                    dve.wait_ge(evacuated, starts["qkv"] + 2 * i + s + 1)
                    own.wait()
                    own.did(keep_state(s, 2 * i + s, new_g, GK))
                    taps(own, s, GK).then_inc(convolved, 1)
                    assert own.n == qkv_steps + 2

            qkv_turn(0, first=True)
            with dve.Fori(1, 3 * KT // 2) as i:
                qkv_turn(i)
            for q in range(8):
                g, half = q // 2, q % 2
                dve.wait_ge(states_turned, q + 1)
                rows = A_OUT if g == 0 else G_OUT
                dst = state_rows_a if g == 0 else state_rows_g
                at = (max(g - 1, 0) * KT + 4 * half) * P
                dve.tensor_copy(dst[:, at:at + 512], ps[0:rows, 0, 3, :]).then_inc(states_kept, 1)


def memory_kv(nc, k, io, memn, kT, v_rows):
    with ExitStack() as ctx:
        def sem(name):
            return nc.alloc_semaphore(name)

        w = ctx.enter_context(nc.sbuf_tensor("w_kv", [P, 4, KT, P], F32))
        vT = ctx.enter_context(nc.sbuf_tensor("vT", [P, KT, M], F32))
        k_rows = ctx.enter_context(nc.sbuf_tensor("k_rows", [P, MT, D], F32))
        ps = ctx.enter_context(nc.psum_tensor("kv_ps", [P, 4, 512], F32))
        landed = [sem(f"kv_landed{s}") for s in range(4)]
        product_done, kept, turned, rows_kept, out_done = (sem("kv_" + n) for n in ("product", "kept", "turned", "rows", "out"))
        block = ctx.enter_context(nc.Block())
        tiles = 2 * KT

        @block.sync
        def _(sp):
            for t in range(tiles):
                if t >= 4:
                    sp.wait_ge(product_done, t - 3)
                sp.dma_start(w[:, t % 4, :, :], io["w_mem_kv"][:, t * P:(t + 1) * P].rearrange("(k p) c -> p k c", p=P)).then_inc(landed[t % 4], 16)
            sp.wait_ge(rows_kept, KT)
            sp.dma_start(io["out_mem_k"].rearrange("(t p) c -> p t c", p=P), k_rows[:, :, :]).then_inc(out_done, 16)
            sp.wait_ge(rows_kept, tiles)
            sp.dma_start(io["out_mem_v"].rearrange("(t p) c -> p t c", p=P), v_rows[:, :, :]).then_inc(out_done, 16)
            sp.wait_ge(out_done, 32)

        @block.tensor
        def _(pe):
            def turn(t):
                pe.wait_ge(kept, t + 1)
                if t >= 2:
                    pe.wait_ge(rows_kept, t - 1)
                src = (kT if t < KT else vT)[:, t % KT, :]
                for m in range(MT):
                    last = pe.transpose(ps[:, 2 + t % 2, m * P:(m + 1) * P], src[:, m * P:(m + 1) * P], k["ident"][:, :])
                last.then_inc(turned, 1)

            for t in range(tiles):
                pe.wait_ge(landed[t % 4], 16 * (t // 4 + 1))
                if t >= 2:
                    pe.wait_ge(kept, t - 1)
                for kk in range(KT):
                    last = pe.matmul(ps[:, t % 2, 0:M], w[:, t % 4, kk, :], memn[:, kk, :],
                                     start=(kk == 0), stop=(kk == KT - 1))
                last.then_inc(product_done, 1)
                if t:
                    turn(t - 1)
            turn(tiles - 1)

        @block.scalar
        def _(act):
            for t in range(tiles):
                act.wait_ge(product_done, t + 1)
                act.copy((kT if t < KT else vT)[:, t % KT, :], ps[:, t % 2, 0:M]).then_inc(kept, 1)

        @block.vector
        def _(dve):
            for t in range(tiles):
                dve.wait_ge(turned, t + 1)
                dst = (k_rows if t < KT else v_rows)[:, :, (t % KT) * P:(t % KT + 1) * P]
                dve.tensor_copy(dst, ps[:, 2 + t % 2, 0:M].rearrange("p (m c) -> p m c", c=P)).then_inc(rows_kept, 1)


SCALE = (D // MH) ** -0.5


def attend_prompt(nc, k, tmp, kT, v_rows):
    tiles = TP // P
    with ExitStack() as ctx:
        def sb(name, shape, dt=F32):
            return ctx.enter_context(nc.sbuf_tensor(name, shape, dt))

        def sem(name):
            return nc.alloc_semaphore("ap_" + name)

        q = sb("ap_q", [P, 2, KT, P])
        probs = sb("ap_probs", [P, 2, MH, M])
        top, bias, total, inv = (sb("ap_" + n, [P, 2, MH]) for n in ("top", "bias", "total", "inv"))
        pT = sb("ap_pT", [P, 2, MH * MT, P])
        o = sb("ap_o", [P, 2, KT, P])
        ps_s = ctx.enter_context(nc.psum_tensor("ap_s", [P, MH, M], F32))
        ps_t = ctx.enter_context(nc.psum_tensor("ap_t", [P, MH * MT, P], F32))
        ps_o = ctx.enter_context(nc.psum_tensor("ap_o_ps", [P, KT, P], F32))
        landed = [sem("landed0"), sem("landed1")]
        stored = [sem("stored0"), sem("stored1")]
        scored, topped, biased, raised, own, normed, turned, kept, summed, out_kept = (
            sem(n) for n in ("scored", "topped", "biased", "raised", "own", "normed", "turned", "kept", "summed", "out_kept"))
        block = ctx.enter_context(nc.Block())

        @block.sync
        def _(sp):
            def load(t, s, first=False):
                if not first:
                    sp.wait_ge(scored, t - 1)
                sp.dma_start(q[:, s, :, :], tmp["mq"][:, :, ds(t * P, P)]).then_inc(landed[s], 16)

            for s in range(2):
                load(s, s, first=True)
            with sp.Fori(1, tiles // 2) as i:
                for s in range(2):
                    load(2 * i + s, s)

        @block.gpsimd
        def _(pool):
            with pool.Fori(0, tiles // 2) as i:
                for s in range(2):
                    pool.wait_ge(out_kept, 2 * i + s + 1)
                    pool.dma_start(tmp["ym"][:, :, ds((2 * i + s) * P, P)], o[:, s, :, :]).then_inc(stored[s], 16)
            for s in range(2):
                pool.wait_ge(stored[s], 16 * (tiles // 2))

        @block.tensor
        def _(pe):
            def scores(i, s, first=False):
                t = 2 * i + s
                pe.wait_ge(landed[s], 16 * i + 16)
                if not first:
                    pe.wait_ge(raised, t)
                for h in range(MH):
                    for c in range(2):
                        last = pe.matmul(ps_s[:, h, :], q[:, s, 2 * h + c, :], kT[:, 2 * h + c, :],
                                         start=(c == 0), stop=(c == 1))
                last.then_inc(scored, 1)

            def values(i, s):
                t = 2 * i + s
                pe.wait_ge(normed, t + 1)
                for b in range(MH * MT):
                    last = pe.transpose(ps_t[:, b, :], probs[:, s, b // MT, (b % MT) * P:(b % MT + 1) * P], k["ident"][:, :])
                last.then_inc(turned, 1)
                pe.wait_ge(kept, t + 1)
                for c in range(KT):
                    for m in range(MT):
                        last = pe.matmul(ps_o[:, c, :], v_rows[:, m, c * P:(c + 1) * P], pT[:, s, (c // 2) * MT + m, :],
                                         start=(m == 0), stop=(m == MT - 1))
                last.then_inc(summed, 1)

            scores(0, 0, first=True)
            scores(0, 1)
            values(0, 0)
            with pe.Fori(1, tiles // 2) as i:
                scores(i, 0)
                values(i - 1, 1)
                scores(i, 1)
                values(i, 0)
            values(tiles // 2 - 1, 1)

        @block.scalar
        def _(act):
            def keep(t, s, first=False):
                act.wait_ge(turned, t + 1)
                if not first:
                    act.wait_ge(out_kept, t)
                act.copy(pT[:, s, 0:4, :], ps_t[:, 0:4, :])
                act.copy(pT[:, s, 4:8, :], ps_t[:, 4:8, :]).then_inc(kept, 1)

            def turn(i, first=False):
                for s in range(2):
                    t = 2 * i + s
                    act.wait_ge(topped, t + 1)
                    act.mul(bias[:, s, :], top[:, s, :], -SCALE).then_inc(biased, 1)
                    act.wait_ge(biased, t + 1)
                    for h in range(MH):
                        last = act.activation(probs[:, s, h, :], ps_s[:, h, :], ACT.Exp, bias=bias[:, s, h:h + 1],
                                              scale=SCALE, accum_out=total[:, s, h:h + 1])
                    last.then_inc(raised, 1)
                    if not (first and s == 0):
                        keep(t - 1, 1 - s, first=first)

            turn(0, first=True)
            with act.Fori(1, tiles // 2) as i:
                turn(i)
            keep(tiles - 1, 1)

        @block.vector
        def _(dve):
            def norm(t, s):
                dve.wait_ge(raised, t + 1)
                dve.reciprocal(inv[:, s, :], total[:, s, :]).then_inc(own, 1)
                dve.wait_ge(own, t + 1)
                for h in range(MH):
                    last = dve.tensor_scalar(probs[:, s, h, :], probs[:, s, h, :], inv[:, s, h:h + 1], None, ALU.mult)
                last.then_inc(normed, 1)

            def outputs(i, t, s, first=False):
                dve.wait_ge(summed, t + 1)
                if not first:
                    dve.wait_ge(stored[s], 16 * i)
                dve.tensor_copy(o[:, s, :, :], ps_o[:, :, :]).then_inc(out_kept, 1)

            def turn(i, kind=None):
                for s in range(2):
                    t = 2 * i + s
                    dve.wait_ge(scored, t + 1)
                    dve.reduce_max(top[:, s, :], ps_s[:, :, :], X).then_inc(topped, 1)
                    norm(t, s)
                    if s == 1:
                        outputs(i, t - 1, 0, first=(kind == "first"))
                    elif kind != "first":
                        outputs(i - 1, t - 1, 1, first=(kind == "second"))

            turn(0, "first")
            turn(1, "second")
            with dve.Fori(2, tiles // 2) as i:
                turn(i)
            outputs(tiles // 2 - 1, tiles - 1, 1)


def attend_samples(nc, k, io, tmp):
    R = MH * TS
    with ExitStack() as ctx:
        def sb(name, shape, dt=F32):
            return ctx.enter_context(nc.sbuf_tensor(name, shape, dt))

        def sem(name):
            return nc.alloc_semaphore("as_" + name)

        q = sb("as_q", [P, KT, NS])
        qpad = sb("as_qpad", [P, NB, KT, P])
        keys = sb("as_keys", [P, 3, MT, D])
        kT = sb("as_kT", [P, 2, KT, M])
        probs = sb("as_probs", [P, M])
        top, bias, total, inv = (sb("as_" + n, [P, 1]) for n in ("top", "bias", "total", "inv"))
        pT = sb("as_pT", [P, MT, P])
        o = sb("as_o", [P, KT, NS])
        ps_t = ctx.enter_context(nc.psum_tensor("as_t", [P, 4, 4, P], F32))
        ps_s = ctx.enter_context(nc.psum_tensor("as_s", [P, 512], F32))
        ps_o = ctx.enter_context(nc.psum_tensor("as_o_ps", [P, KT, NS], F32))
        landed = [sem(f"landed{s}") for s in range(3)]
        q_in, zeroed, padded, turned, kept, kept_act, scored, used, summed, out_kept, stored = (
            sem(n) for n in ("q_in", "zeroed", "padded", "turned", "kept", "kept_act", "scored", "used", "summed", "out_kept", "stored"))
        soft = sem("soft")
        block = ctx.enter_context(nc.Block())

        @block.sync
        def _(sp):
            sp.dma_start(q[:, :, :], tmp["mq"][:, :, TP:N]).then_inc(q_in, 16)
            for j in range(2 * NB):
                if 3 <= j < NB + 3:
                    sp.wait_ge(turned, 4 * (j - 2))
                elif j >= 3:
                    sp.wait_ge(used, j - 2 - NB)
                src = io["cache_mem_k" if j < NB else "cache_mem_v"][j % NB].rearrange("(t p) h d -> p t (h d)", p=P)
                sp.dma_start(keys[:, j % 3, :, :], src).then_inc(landed[j % 3], 16)
            sp.wait_ge(out_kept, 1)
            sp.dma_start(tmp["ym"][:, :, TP:N], o[:, :, :]).then_inc(stored, 16)
            sp.wait_ge(stored, 16)

        @block.vector
        def _(dve):
            dve.memset(qpad[:, :, :, :], 0.0).then_inc(zeroed, 1)
            dve.wait_ge(zeroed, 1)
            dve.wait_ge(q_in, 16)
            for b in range(NB):
                for h in range(MH):
                    row = b * R + h * TS
                    last = dve.tensor_copy(qpad[:, b, 2 * h:2 * h + 2, row:row + TS], q[:, 2 * h:2 * h + 2, b * TS:(b + 1) * TS])
                last.then_inc(padded, 1)
            for g in range(1, 4 * NB, 2):
                dve.wait_ge(turned, g + 1)
                if g >= 8:
                    dve.wait_ge(scored, g // 4 - 1)
                dve.tensor_copy(kT[:, (g // 4) % 2, 4 * (g % 2):4 * (g % 2) + 4, (g // 2 % 2) * P:(g // 2 % 2 + 1) * P],
                                ps_t[:, g % 4, :, :]).then_inc(kept, 1)
            dve.wait_ge(scored, NB)
            dve.reduce_max(top[:, :], ps_s[:, 0:M], X).then_inc(soft, 1)
            dve.wait_ge(soft, 3)
            dve.reciprocal(inv[:, :], total[:, :]).then_inc(soft, 1)
            dve.wait_ge(soft, 4)
            dve.tensor_scalar(probs[:, :], probs[:, :], inv[:, 0:1], None, ALU.mult).then_inc(soft, 1)
            dve.wait_ge(turned, 4 * NB + 1)
            dve.tensor_copy(pT[:, :, :], ps_t[:, 0, 0:MT, :]).then_inc(soft, 1)
            dve.wait_ge(summed, 1)
            dve.tensor_copy(o[:, :, :], ps_o[:, :, :]).then_inc(out_kept, 1)

        @block.scalar
        def _(act):
            for g in range(0, 4 * NB, 2):
                act.wait_ge(turned, g + 1)
                if g >= 8:
                    act.wait_ge(scored, g // 4 - 1)
                act.copy(kT[:, (g // 4) % 2, 4 * (g % 2):4 * (g % 2) + 4, (g // 2 % 2) * P:(g // 2 % 2 + 1) * P],
                         ps_t[:, g % 4, :, :]).then_inc(kept_act, 1)
            act.wait_ge(soft, 1)
            act.mul(bias[:, :], top[:, :], -SCALE).then_inc(soft, 1)
            act.wait_ge(soft, 2)
            act.activation(probs[:, :], ps_s[:, 0:M], ACT.Exp, bias=bias[:, 0:1], scale=SCALE,
                           accum_out=total[:, 0:1]).then_inc(soft, 1)

        @block.tensor
        def _(pe):
            def turn(b):
                pe.wait_ge(landed[b % 3], 16 * (b // 3 + 1))
                for g in range(4 * b, 4 * b + 4):
                    if g >= 4:
                        pe.wait_ge(kept if g % 2 else kept_act, (g - 4) // 2 + 1)
                    for c in range(4):
                        at = (4 * (g % 2) + c) * P
                        last = pe.transpose(ps_t[:, g % 4, c, :], keys[:, b % 3, g // 2 % 2, at:at + P], k["ident"][:, :])
                    last.then_inc(turned, 1)

            def scores(b):
                pe.wait_ge(padded, b + 1)
                pe.wait_ge(kept, 2 * b + 2)
                pe.wait_ge(kept_act, 2 * b + 2)
                for c in range(KT):
                    last = pe.matmul(ps_s[:, 0:M], qpad[:, b, c, :], kT[:, b % 2, c, :],
                                     start=(b == 0 and c == 0), stop=(b == NB - 1 and c == KT - 1))
                last.then_inc(scored, 1)

            turn(0)
            for b in range(NB):
                if b + 1 < NB:
                    turn(b + 1)
                scores(b)
            pe.wait_ge(soft, 5)
            for m in range(MT):
                last = pe.transpose(ps_t[:, 0, m, :], probs[:, m * P:(m + 1) * P], k["ident"][:, :])
            last.then_inc(turned, 1)
            pe.wait_ge(soft, 6)
            for b in range(NB):
                j = NB + b
                pe.wait_ge(landed[j % 3], 16 * (j // 3 + 1))
                for c in range(KT):
                    row = b * R + (c // 2) * TS
                    for m in range(MT):
                        last = pe.matmul(ps_o[:, c, b * TS:(b + 1) * TS], keys[:, j % 3, m, c * P:(c + 1) * P],
                                         pT[:, m, row:row + TS], start=(m == 0), stop=(m == MT - 1))
                last.then_inc(used if b < NB - 1 else summed, 1)


HG = H // 2
LEVELS = (1, 2, 4, 8, 16, 32, 64)


def over_heads(mask, heads=HG):
    return mask.unsqueeze(1).broadcast_to([mask.shape[0], heads, mask.shape[1]])


def over_columns(values, columns=P):
    return values.unsqueeze(2).broadcast_to([values.shape[0], values.shape[1], columns])


def decay_sums(nc, k):
    with ExitStack() as ctx:
        def sem(name):
            return nc.alloc_semaphore("sums_" + name)

        ps = ctx.enter_context(nc.psum_tensor("sums_ps", [P, 3, NT * H], F32))
        summed, masked, done = sem("summed"), sem("masked"), sem("done")
        block = ctx.enter_context(nc.Block())

        @block.tensor
        def _(pe):
            for n, mask in enumerate(("upto", "after", "ones")):
                last = pe.matmul(ps[:, n, :], k[mask][:, :], k["glog"][:, :, :], start=True, stop=True)
            last.then_inc(summed, 1)

        @block.scalar
        def _(act):
            act.wait_ge(summed, 1)
            act.activation(k["decays"][:, :, :, :], ps[:, :, :], ACT.Exp).then_inc(done, 1)

        @block.vector
        def _(dve):
            dve.wait_ge(done, 1)
            dve.tensor_tensor(k["beta_decay"][:, :, :], k["beta"][:, :, :], k["decays"][:, 0, :, :], ALU.mult)

        @block.gpsimd
        def _(pool):
            for n, s in enumerate(LEVELS):
                m = k["level"][:, n, :].rearrange("p (c e j) -> p c e j", e=2, j=s)
                pool.memset(k["level"][:, n, :], 0.0).then_inc(masked, 1)
                pool.wait_ge(masked, 3 * n + 1)
                lower = m[:, :, 0, :]
                pool.affine_select(out=lower, in_=k["ones"][:, 0:P // 2].rearrange("p (c j) -> p c j", j=s),
                                   compare_op=ALU.is_ge, fill=0.0, base=-s, pattern=[[-2 * s, P // (2 * s)], [0, s]],
                                   channel_multiplier=1).then_inc(masked, 1)
                pool.wait_ge(masked, 3 * n + 2)
                pool.affine_select(out=lower, in_=lower, compare_op=ALU.is_ge, fill=0.0, base=2 * s - 1,
                                   pattern=[[2 * s, P // (2 * s)], [0, s]], channel_multiplier=-1).then_inc(masked, 1)


def delta_prompt(nc, k, io, tmp):
    chunks = TP // P
    NL = len(LEVELS)
    with ExitStack() as ctx:
        def sb(name, dt=F32):
            return [ctx.enter_context(nc.sbuf_tensor(f"dp_{name}{g}", [P, HG, P], dt)) for g in range(2)]

        def sem(name):
            return nc.alloc_semaphore("dp_" + name)

        qkv = ctx.enter_context(nc.sbuf_tensor("dp_qkv", [P, 2, 3, H, P], F32))
        z = ctx.enter_context(nc.sbuf_tensor("dp_z", [P, 2, H, P], F32))
        S = ctx.enter_context(nc.sbuf_tensor("dp_S", [P, H, P], F32))
        y = ctx.enter_context(nc.sbuf_tensor("dp_y", [P, 2, HG, P], F32))
        sq_q, sq_k, root_q, root_k, r_q, r_k = (sb(n) for n in ("sq_q", "sq_k", "root_q", "root_k", "r_q", "r_k"))
        g_upto, decay, decayT, weight, weightT = (sb(n) for n in ("g_upto", "decay", "decayT", "weight", "weightT"))
        L, attnT, inv, invT, R = (sb(n) for n in ("L", "attnT", "inv", "invT", "R"))
        Lm = [ctx.enter_context(nc.sbuf_tensor(f"dp_Lm{g}", [P, NL, HG, P], F32)) for g in range(2)]
        k_in, v_in, k_out, wT, v_new, o_state, o, o_sq = (
            sb(n) for n in ("k_in", "v_in", "k_out", "wT", "v_new", "o_state", "o", "o_sq"))
        o_ss, o_root, o_r = ([ctx.enter_context(nc.sbuf_tensor(f"dp_{n}{g}", [P, HG], F32)) for g in range(2)]
                             for n in ("o_ss", "o_root", "o_r"))
        banks = ctx.enter_context(nc.psum_tensor("dp_ps", [P, 2, 4, HG, P], F32))
        landed = [sem("landed0"), sem("landed1")]
        stored = [sem("stored0"), sem("stored1")]
        names = ("squared q_summed k_summed q_rooted k_rooted q_ready k_ready g_ready q_inverted k_inverted diffed raised weighted gram attn_done L_ready "
                 "masked turned1 inv_ready r_done r_kept grown krow_done krow_kept vrow_done vrow_kept "
                 "w_done w_kept v_done v_kept state_done intra_done grow_done S_ready o_part o_ready o_squared "
                 "o_rooted o_inv o_normed o_turned y_ready zeroed S_out S_part").split()
        m = {n: sem(n) for n in names}
        block = ctx.enter_context(nc.Block())

        def q_of(g, s):
            return qkv[:, s, 0, g * HG:(g + 1) * HG, :]

        def k_of(g, s):
            return qkv[:, s, 1, g * HG:(g + 1) * HG, :]

        def v_of(g, s):
            return qkv[:, s, 2, g * HG:(g + 1) * HG, :]

        def S_of(g):
            return S[:, g * HG:(g + 1) * HG, :]

        def level_at(t, lv, g, per=NL):
            return (t * per + lv) * 2 + g + 1

        @block.sync
        def _(sp):
            def load(i, s):
                t = 2 * i + s
                sp.dma_start(qkv[:, s, :, :, :], tmp["qkv"][:, :, ds(t * P, P)].rearrange("p (a h) n -> p a h n", h=H)).then_inc(landed[s], 16)
                sp.dma_start(z[:, s, :, :], tmp["z"][:, :, ds(t * P, P)]).then_inc(landed[s], 16)

            def store(i, s):
                t = 2 * i + s
                for g in range(2):
                    sp.wait_ge(m["y_ready"], 2 * t + g + 1)
                    sp.dma_start(tmp["yb"][:, g * HG:(g + 1) * HG, ds(t * P, P)], y[:, g, :, :]).then_inc(stored[g], 16)

            for s in range(2):
                load(0, s)
            with sp.Fori(0, chunks // 2 - 1) as i:
                for s in range(2):
                    store(i, s)
                    load(i + 1, s)
            for s in range(2):
                store(chunks // 2 - 1, s)
            for g in range(2):
                sp.wait_ge(stored[g], 16 * chunks)
            sp.wait_ge(m["S_ready"], 2 * chunks)
            sp.dma_start(io["out_gdn_p"].rearrange("h d e -> d h e"), S[:, :, :]).then_inc(m["S_out"], 16)
            sp.wait_ge(m["S_out"], 16)

        @block.tensor
        def _(pe):
            def heads(out, lhsT, rhs, start=True, stop=True, fixed=None):
                for h in range(HG):
                    last = pe.matmul(out[:, h, :], lhsT[:, h, :], fixed if fixed is not None else rhs[:, h, :],
                                     start=start, stop=stop)
                return last

            def turn(out, src):
                for h in range(HG):
                    last = pe.transpose(out[:, h, :], src[:, h, :], k["ident"][:, :])
                return last

            def B(g, b):
                return banks[:, g, b, :, :]

            def sum_q(n, g):
                pe.wait_ge(m["squared"], n + 1)
                pe.matmul(B(g, 2), k["ones"][:, :], sq_q[g][:, :, :], start=True, stop=True).then_inc(m["q_summed"], 1)

            def sum_k(n, g):
                pe.wait_ge(m["q_rooted"], n + 1)
                pe.matmul(B(g, 2), k["ones"][:, :], sq_k[g][:, :, :], start=True, stop=True).then_inc(m["k_summed"], 1)

            def differences(n, g):
                pe.wait_ge(m["g_ready"], n + 1)
                pe.wait_ge(m["k_rooted"], n + 1)
                heads(B(g, 2), g_upto[g], None, fixed=k["after"][:, :])
                pe.matmul(B(g, 0), k["after"][:, :], g_upto[g][:, :, :], start=True, stop=True).then_inc(m["diffed"], 1)

            def turn_output(n, g):
                pe.wait_ge(m["o_normed"], n + 1)
                pe.wait_ge(m["S_ready"], n + 1)
                turn(B(g, 3), o[g]).then_inc(m["o_turned"], 1)

            def chunk_turn(i, s, first=False, last=False):
                t = 2 * i + s
                for g in range(2):
                    n = 2 * t + g
                    pe.wait_ge(m["raised"], n + 1)
                    pe.wait_ge(m["k_ready"], n + 1)
                    heads(B(g, 0), k_of(g, s), k_of(g, s)).then_inc(m["gram"], 1)
                    pe.wait_ge(m["q_ready"], n + 1)
                    if not first:
                        pe.wait_ge(m["o_part"], n - 1)
                    heads(B(g, 1), k_of(g, s), q_of(g, s)).then_inc(m["attn_done"], 1)
                if not first:
                    for g in range(2):
                        turn_output(2 * t + g - 2, g)
                for g in range(2):
                    n = 2 * t + g
                    if not first:
                        pe.wait_ge(m["o_ready"], n - 1)
                    pe.wait_ge(m["masked"], level_at(t, 0, g))
                    turn(B(g, 2), Lm[g][:, 0, :, :]).then_inc(m["turned1"], 1)
                for lv in range(1, NL):
                    for g in range(2):
                        n = 2 * t + g
                        pe.wait_ge(m["masked"], level_at(t, lv, g))
                        pe.wait_ge(m["inv_ready"], level_at(t, lv - 1, g))
                        if lv == 1 and not first:
                            pe.wait_ge(m["y_ready"], n - 1)
                        heads(B(g, 3), Lm[g][:, lv, :, :], invT[g]).then_inc(m["r_done"], 1)
                        if lv == 1:
                            turn(B(g, 2), k_of(g, s)).then_inc(m["krow_done"], 1)
                        if lv == 3:
                            pe.wait_ge(m["krow_kept"], n + 1)
                            turn(B(g, 2), v_of(g, s)).then_inc(m["vrow_done"], 1)
                        if lv == 4:
                            pe.wait_ge(m["vrow_kept"], n + 1)
                        if not last:
                            if lv == 4:
                                sum_q(n + 2, g)
                            if lv == 5:
                                sum_k(n + 2, g)
                            if lv == 6:
                                differences(n + 2, g)
                    for g in range(2):
                        pe.wait_ge(m["r_kept"], level_at(t, lv - 1, g, NL - 1))
                        if lv < NL - 1:
                            heads(B(g, 0), R[g], inv[g])
                        heads(B(g, 1), inv[g], R[g]).then_inc(m["grown"], 1)
                for g in range(2):
                    pe.wait_ge(m["inv_ready"], level_at(t, NL - 1, g))
                    heads(B(g, 3), k_in[g], invT[g]).then_inc(m["w_done"], 1)
                for g in range(2):
                    n = 2 * t + g
                    pe.wait_ge(m["w_kept"], n + 1)
                    if not last:
                        pe.wait_ge(m["raised"], n + 3)
                    for h in range(HG):
                        pe.matmul(B(g, 0)[:, h, :], invT[g][:, h, :], v_in[g][:, h, :], start=True, stop=False)
                        done = pe.matmul(B(g, 0)[:, h, :], wT[g][:, h, :], S_of(g)[:, h, :], start=False, stop=True)
                    done.then_inc(m["v_done"], 1)
                    heads(B(g, 1), q_of(g, s), S_of(g)).then_inc(m["state_done"], 1)
                for g in range(2):
                    n = 2 * t + g
                    pe.wait_ge(m["v_kept"], n + 1)
                    heads(B(g, 3), k_out[g], v_new[g]).then_inc(m["grow_done"], 1)
                    heads(B(g, 2), attnT[g], v_new[g]).then_inc(m["intra_done"], 1)

            for step in (sum_q, sum_k, differences):
                for g in range(2):
                    step(g, g)
            pe.wait_ge(m["zeroed"], 1)
            chunk_turn(0, 0, first=True)
            chunk_turn(0, 1)
            with pe.Fori(1, chunks // 2 - 1) as i:
                for s in range(2):
                    chunk_turn(i, s)
            chunk_turn(chunks // 2 - 1, 0)
            chunk_turn(chunks // 2 - 1, 1, last=True)
            for g in range(2):
                turn_output(2 * chunks - 2 + g, g)

        @block.scalar
        def _(act):
            def B(g, b):
                return banks[:, g, b, :, :]

            def square(i, s):
                act.wait_ge(landed[s], 32 * i + 32)
                for g in range(2):
                    act.activation(sq_q[g][:, :, :], q_of(g, s), ACT.Square)
                    act.activation(sq_k[g][:, :, :], k_of(g, s), ACT.Square).then_inc(m["squared"], 1)

            def root(n, g, summed, rooted, out):
                act.wait_ge(m[summed], n + 1)
                act.activation(out[g][:, :, :], B(g, 2), ACT.Sqrt, bias=k["eps"][:, 0:1]).then_inc(m[rooted], 1)

            def raise_decays(n, g):
                act.wait_ge(m["diffed"], n + 1)
                act.activation(decay[g][:, :, :], B(g, 2), ACT.Exp)
                act.activation(decayT[g][:, :, :], B(g, 0), ACT.Exp).then_inc(m["raised"], 1)

            def chunk_turn(i, s, last=False):
                t = 2 * i + s
                for lv in range(1, NL):
                    for g in range(2):
                        act.wait_ge(m["r_done"], level_at(t, lv - 1, g, NL - 1))
                        act.copy(R[g][:, :, :], B(g, 3)).then_inc(m["r_kept"], 1)
                    if not last:
                        if lv == 3:
                            square(i + s, 1 - s)
                        for g in range(2):
                            n = 2 * t + 2 + g
                            if lv == 4:
                                root(n, g, "q_summed", "q_rooted", root_q)
                            if lv == 5:
                                root(n, g, "k_summed", "k_rooted", root_k)
                            if lv == 6:
                                raise_decays(n, g)
                for g in range(2):
                    n = 2 * t + g
                    act.wait_ge(m["w_done"], n + 1)
                    act.mul(wT[g][:, :, :], B(g, 3), -1.0).then_inc(m["w_kept"], 1)
                for g in range(2):
                    n = 2 * t + g
                    act.wait_ge(m["v_done"], n + 1)
                    act.copy(v_new[g][:, :, :], B(g, 0)).then_inc(m["v_kept"], 1)
                for g in range(2):
                    n = 2 * t + g
                    act.wait_ge(m["o_ready"], n + 1)
                    for h in range(HG):
                        done = act.activation(o_sq[g][:, h, :], o[g][:, h, :], ACT.Square, accum_out=o_ss[g][:, h:h + 1])
                    done.then_inc(m["o_squared"], 1)
                for g in range(2):
                    n = 2 * t + g
                    act.wait_ge(m["o_squared"], n + 1)
                    act.activation(o_root[g][:, :], o_ss[g][:, :], ACT.Sqrt, bias=k["eps"][:, 0:1], scale=1.0 / P).then_inc(m["o_rooted"], 1)

            square(0, 0)
            for g in range(2):
                root(g, g, "q_summed", "q_rooted", root_q)
            for g in range(2):
                root(g, g, "k_summed", "k_rooted", root_k)
            for g in range(2):
                raise_decays(g, g)
            with act.Fori(0, chunks // 2 - 1) as i:
                for s in range(2):
                    chunk_turn(i, s)
            chunk_turn(chunks // 2 - 1, 0)
            chunk_turn(chunks // 2 - 1, 1, last=True)

        @block.gpsimd
        def _(pool):
            def weights(t, first=False):
                for g in range(2):
                    n = 2 * t + g
                    beta = k["beta"][:, ds(t, 1), g * HG:(g + 1) * HG].rearrange("p o h -> p (o h)")
                    own = Steps(pool, m["weighted"], 3 * n)
                    if not first:
                        pool.wait_ge(m["inv_ready"], level_at(t - 1, 0, g))
                    own.did(pool.tensor_tensor(weight[g][:, :, :], over_heads(k["after"][:, :]), over_columns(beta), ALU.mult))
                    pool.wait_ge(m["raised"], n + 1)
                    own.wait()
                    own.did(pool.tensor_tensor(weight[g][:, :, :], weight[g][:, :, :], decay[g][:, :, :], ALU.mult))
                    own.did(pool.tensor_tensor(weightT[g][:, :, :], over_heads(k["upto"][:, :]), decayT[g][:, :, :], ALU.mult))

            def chunk_turn(i, s, last=False):
                t = 2 * i + s
                for lv in range(NL):
                    for g in range(2):
                        if lv == 0:
                            pool.wait_ge(m["L_ready"], 2 * t + g + 1)
                        pool.tensor_tensor(Lm[g][:, lv, :, :], L[g][:, :, :], over_heads(k["level"][:, lv, :]), ALU.mult).then_inc(m["masked"], 1)
                if not last:
                    weights(t + 1)

            weights(0, first=True)
            with pool.Fori(0, chunks // 2 - 1) as i:
                for s in range(2):
                    chunk_turn(i, s)
            chunk_turn(chunks // 2 - 1, 0)
            chunk_turn(chunks // 2 - 1, 1, last=True)

        @block.vector
        def _(dve):
            def B(g, b):
                return banks[:, g, b, :, :]

            def of(name, t, g):
                return k[name][:, ds(t, 1), g * HG:(g + 1) * HG].rearrange("p o h -> p (o h)")

            def decays(n, t, g):
                return k["decays"][:, n:n + 1, ds(t, 1), g * HG:(g + 1) * HG].rearrange("p a o h -> p (a o h)")

            def gates(t):
                for g in range(2):
                    dve.tensor_tensor(g_upto[g][:, :, :], over_heads(k["upto"][:, :]), over_columns(of("glog", t, g)), ALU.mult).then_inc(m["g_ready"], 1)

            def norm_q(n, g, s):
                dve.wait_ge(m["q_rooted"], n + 1)
                dve.reciprocal(r_q[g][:, :, :], root_q[g][:, :, :]).then_inc(m["q_inverted"], 1)
                dve.wait_ge(m["q_inverted"], n + 1)
                dve.scalar_tensor_tensor(out=q_of(g, s), in0=q_of(g, s), scalar=float(P) ** -0.5, in1=r_q[g][:, :, :],
                                         op0=ALU.mult, op1=ALU.mult).then_inc(m["q_ready"], 1)

            def norm_k(n, g, s):
                dve.wait_ge(m["k_rooted"], n + 1)
                dve.reciprocal(r_k[g][:, :, :], root_k[g][:, :, :]).then_inc(m["k_inverted"], 1)
                dve.wait_ge(m["k_inverted"], n + 1)
                dve.tensor_tensor(k_of(g, s), k_of(g, s), r_k[g][:, :, :], ALU.mult).then_inc(m["k_ready"], 1)

            def norm_output(n, g):
                dve.wait_ge(m["o_rooted"], n + 1)
                dve.reciprocal(o_r[g][:, :], o_root[g][:, :]).then_inc(m["o_inv"], 1)
                dve.wait_ge(m["o_inv"], n + 1)
                dve.tensor_tensor(o[g][:, :, :], o[g][:, :, :], over_columns(o_r[g][:, :]), ALU.mult).then_inc(m["o_normed"], 1)

            def finish_output(t, g, s, first=False):
                dve.wait_ge(m["o_turned"], 2 * t + g + 1)
                if not first:
                    dve.wait_ge(stored[g], 16 * t)
                dve.scalar_tensor_tensor(out=y[:, g, :, :], in0=B(g, 3), scalar=k["gdn_gain"][:, 0:1],
                                         in1=z[:, s, g * HG:(g + 1) * HG, :], op0=ALU.mult, op1=ALU.mult).then_inc(m["y_ready"], 1)

            def chunk_turn(i, s, kind=None):
                t = 2 * i + s
                first, last = kind == "first", kind == "last"
                for g in range(2):
                    n = 2 * t + g
                    dve.wait_ge(m["gram"], n + 1)
                    dve.wait_ge(m["weighted"], 3 * n + 3)
                    dve.tensor_tensor(L[g][:, :, :], B(g, 0), weight[g][:, :, :], ALU.mult).then_inc(m["L_ready"], 1)
                if not first:
                    for g in range(2):
                        norm_output(2 * t + g - 2, g)
                for g in range(2):
                    n = 2 * t + g
                    dve.wait_ge(m["attn_done"], n + 1)
                    dve.tensor_tensor(attnT[g][:, :, :], B(g, 1), weightT[g][:, :, :], ALU.mult)
                    dve.wait_ge(m["masked"], level_at(t, 0, g))
                    dve.tensor_tensor(inv[g][:, :, :], over_heads(k["ident"][:, :]), Lm[g][:, 0, :, :], ALU.subtract)
                    dve.wait_ge(m["turned1"], n + 1)
                    dve.tensor_tensor(invT[g][:, :, :], over_heads(k["ident"][:, :]), B(g, 2), ALU.subtract).then_inc(m["inv_ready"], 1)
                if not first:
                    for g in range(2):
                        finish_output(t - 1, g, 1 - s, first=(kind == "second"))
                for lv in range(1, NL):
                    for g in range(2):
                        n = 2 * t + g
                        dve.wait_ge(m["grown"], level_at(t, lv - 1, g, NL - 1))
                        if lv < NL - 1:
                            dve.tensor_tensor(inv[g][:, :, :], inv[g][:, :, :], B(g, 0), ALU.subtract)
                        dve.tensor_tensor(invT[g][:, :, :], invT[g][:, :, :], B(g, 1), ALU.subtract).then_inc(m["inv_ready"], 1)
                        if lv == 1:
                            dve.wait_ge(m["krow_done"], n + 1)
                            dve.tensor_tensor(k_in[g][:, :, :], B(g, 2), over_columns(of("beta_decay", t, g)), ALU.mult)
                            dve.tensor_tensor(k_out[g][:, :, :], B(g, 2), over_columns(decays(1, t, g)), ALU.mult).then_inc(m["krow_kept"], 1)
                        if lv == 3:
                            dve.wait_ge(m["vrow_done"], n + 1)
                            dve.tensor_tensor(v_in[g][:, :, :], B(g, 2), over_columns(of("beta", t, g)), ALU.mult).then_inc(m["vrow_kept"], 1)
                    if not last:
                        if lv == 2:
                            gates(t + 1)
                        for g in range(2):
                            if lv == 5:
                                norm_q(2 * t + 2 + g, g, 1 - s)
                            if lv == 6:
                                norm_k(2 * t + 2 + g, g, 1 - s)
                for g in range(2):
                    n = 2 * t + g
                    dve.wait_ge(m["state_done"], n + 1)
                    dve.tensor_tensor(o_state[g][:, :, :], B(g, 1), over_columns(decays(0, t, g)), ALU.mult).then_inc(m["o_part"], 1)
                for g in range(2):
                    n = 2 * t + g
                    dve.tensor_tensor(S_of(g), S_of(g), over_columns(decays(2, t, g)), ALU.mult).then_inc(m["S_part"], 1)
                    dve.wait_ge(m["S_part"], n + 1)
                    dve.wait_ge(m["grow_done"], n + 1)
                    dve.tensor_tensor(S_of(g), S_of(g), B(g, 3), ALU.add).then_inc(m["S_ready"], 1)
                    dve.wait_ge(m["o_part"], n + 1)
                    dve.wait_ge(m["intra_done"], n + 1)
                    dve.tensor_tensor(o[g][:, :, :], o_state[g][:, :, :], B(g, 2), ALU.add).then_inc(m["o_ready"], 1)

            dve.memset(S[:, :, :], 0.0).then_inc(m["zeroed"], 1)
            gates(0)
            for step in (norm_q, norm_k):
                for g in range(2):
                    step(g, g, 0)
            chunk_turn(0, 0, "first")
            chunk_turn(0, 1, "second")
            with dve.Fori(1, chunks // 2 - 1) as i:
                for s in range(2):
                    chunk_turn(i, s)
            chunk_turn(chunks // 2 - 1, 0)
            chunk_turn(chunks // 2 - 1, 1, "last")
            for g in range(2):
                norm_output(2 * chunks - 2 + g, g)
            for g in range(2):
                finish_output(chunks - 1, g, 1)


def delta_samples(nc, k, io, tmp):
    levels = [s for s in LEVELS if s < TS]
    last_tile = NT - 1
    with ExitStack() as ctx:
        def sb(name, shape, dt=F32):
            return ctx.enter_context(nc.sbuf_tensor("ds_" + name, shape, dt))

        def sem(name):
            return nc.alloc_semaphore("ds_" + name)

        qkv = sb("qkv", [P, 3, H, NS])
        z = sb("z", [P, H, NS])
        S = sb("S", [P, NB, H, P])
        upto, after = sb("upto", [NS, NS]), sb("after", [NS, NS])
        sq, root, rinv = sb("sq", [P, 2, H, NS]), sb("root", [P, 2, H, NS]), sb("rinv", [P, 2, H, NS])
        glog, beta = k["glog"][0:NS, last_tile, :], k["beta"][0:NS, last_tile, :]
        g_upto, g_seq = sb("g_upto", [NS, H, NS]), sb("g_seq", [NS, NB, H])
        decay, decayT = sb("decay", [NS, H, NS]), sb("decayT", [NS, H, NS])
        weight, weightT = sb("weight", [NS, H, NS]), sb("weightT", [NS, H, NS])
        sums, beta_decay = sb("sums", [NS, 2, H]), sb("beta_decay", [NS, H])
        keep = sb("keep", [P, NB, H])
        L, Lm, attnT = sb("L", [NS, H, NS]), sb("Lm", [NS, len(levels), H, NS]), sb("attnT", [NS, H, NS])
        inv, invT, R = sb("inv", [NS, H, NS]), sb("invT", [NS, H, NS]), sb("R", [NS, H, NS])
        k_in, k_out, v_in, v_new = (sb(n, [NS, H, P]) for n in ("k_in", "k_out", "v_in", "v_new"))
        wT, v_newT, o_stateT = (sb(n, [P, H, NS]) for n in ("wT", "v_newT", "o_stateT"))
        v_seq = sb("v_seq", [NS, 2, NB, P])
        o_state, o, o_sq = (sb(n, [NS, H, P]) for n in ("o_state", "o", "o_sq"))
        o_ss, o_root, o_r = (sb(n, [NS, H]) for n in ("o_ss", "o_root", "o_r"))
        y = sb("y", [P, H, NS])
        ps = ctx.enter_context(nc.psum_tensor("ds_ps", [P, 8, 512], F32))
        landed, made, did_pe, did_act, stored, S_step = (
            sem(n) for n in ("landed", "dve_step", "pe_step", "act_step", "stored", "S_step"))
        v_masked, grow_done = sem("v_masked"), sem("grow_done")
        block = ctx.enter_context(nc.Block())

        def cols(b, rows=P, n=NS):
            return ps[0:rows, b, 0:H * n].rearrange("p (h n) -> p h n", n=n)

        def wide(b, rows=NS):
            return ps[0:rows, b:b + 2, :].rearrange("p b (h n) -> p (b h) n", n=P)

        mask4 = k["same_seq"][:, :].rearrange("p (b t) -> p b t", t=TS)[:, :, 0]

        @block.sync
        def _(sp):
            sp.dma_start(qkv[:, :, :, :], tmp["qkv"][:, :, TP:N].rearrange("p (a h) n -> p a h n", h=H)).then_inc(landed, 16)
            sp.dma_start(z[:, :, :], tmp["z"][:, :, TP:N]).then_inc(landed, 16)
            for b in range(NB):
                sp.dma_start(S[:, b, :, :], io["state_gdn"][b].rearrange("h d e -> d h e")).then_inc(landed, 16)
            sp.wait_ge(made, 20)
            sp.dma_start(tmp["yb"][:, :, TP:N], y[:, :, :]).then_inc(stored, 16)
            sp.wait_ge(S_step, 3 * H)
            for b in range(NB):
                sp.dma_start(io["out_gdn_s"][b].rearrange("h d e -> d h e"), S[:, b, :, :]).then_inc(stored, 16)
            sp.wait_ge(stored, 16 * (NB + 1))

        @block.vector
        def _(dve):
            own = Steps(dve, made)
            own.did(dve.tensor_tensor(upto[:, :], k["upto"][0:NS, 0:NS], k["same_seq"][:, :], ALU.mult))
            own.did(dve.tensor_tensor(after[:, :], k["after"][0:NS, 0:NS], k["same_seq"][:, :], ALU.mult))
            own.wait()
            own.did(dve.tensor_tensor(g_upto[:, :, :], over_heads(upto[:, :], H), over_columns(glog, NS), ALU.mult))
            own.did(dve.tensor_tensor(g_seq[:, :, :], over_heads(glog, NB), over_columns(mask4, H), ALU.mult))
            dve.tensor_tensor(weight[:, :, :], over_heads(after[:, :], H), over_columns(beta, NS), ALU.mult)
            dve.wait_ge(did_act, 2)
            own.did(dve.reciprocal(rinv[:, :, :, :], root[:, :, :, :]))
            own.wait()
            dve.scalar_tensor_tensor(out=qkv[:, 0, :, :], in0=qkv[:, 0, :, :], scalar=float(P) ** -0.5,
                                     in1=rinv[:, 0, :, :], op0=ALU.mult, op1=ALU.mult)
            own.did(dve.tensor_tensor(qkv[:, 1, :, :], qkv[:, 1, :, :], rinv[:, 1, :, :], ALU.mult))
            dve.wait_ge(did_act, 3)
            dve.tensor_tensor(weight[:, :, :], weight[:, :, :], decay[:, :, :], ALU.mult)
            dve.tensor_tensor(weightT[:, :, :], over_heads(upto[:, :], H), decayT[:, :, :], ALU.mult)
            own.did(dve.tensor_tensor(beta_decay[:, :], beta, sums[:, 0, :], ALU.mult))
            own.wait()
            dve.wait_ge(did_pe, 3)
            dve.tensor_tensor(attnT[:, :, :], cols(5, NS), weightT[:, :, :], ALU.mult)
            own.did(dve.tensor_tensor(L[:, :, :], cols(4, NS), weight[:, :, :], ALU.mult))
            own.wait()
            for n in range(len(levels)):
                last = dve.tensor_tensor(Lm[:, n, :, :], L[:, :, :], over_heads(k["level"][0:NS, n, 0:NS], H), ALU.mult)
            own.did(last)
            own.wait()
            dve.tensor_tensor(inv[:, :, :], over_heads(k["ident"][0:NS, 0:NS], H), Lm[:, 0, :, :], ALU.subtract)
            dve.wait_ge(did_pe, 4)
            own.did(dve.tensor_tensor(invT[:, :, :], over_heads(k["ident"][0:NS, 0:NS], H), cols(6, NS), ALU.subtract))
            own.wait()
            dve.wait_ge(did_pe, 5)
            own.did(dve.tensor_copy(R[:, :, :], cols(7, NS)))
            dve.wait_ge(did_pe, 6)
            own.did(dve.tensor_tensor(invT[:, :, :], invT[:, :, :], cols(6, NS), ALU.subtract))
            dve.wait_ge(did_pe, 7)
            dve.tensor_tensor(k_in[:, :, :], wide(0), over_columns(beta_decay[:, :]), ALU.mult)
            dve.tensor_tensor(k_out[:, :, :], wide(0), over_columns(sums[:, 1, :]), ALU.mult)
            own.did(dve.tensor_tensor(v_in[:, :, :], wide(2), over_columns(beta), ALU.mult))
            dve.wait_ge(did_pe, 8)
            own.did(dve.tensor_scalar(wT[:, :, :], cols(4), -1.0, None, ALU.mult))
            dve.wait_ge(did_pe, 9)
            dve.tensor_copy(v_newT[:, :, :], cols(5))
            own.did(dve.tensor_copy(o_stateT[:, :, :], cols(6)))
            dve.wait_ge(did_pe, 10)
            dve.tensor_copy(v_new[:, :, :], wide(0))
            own.did(dve.tensor_tensor(o_state[:, :, :], wide(2), over_columns(sums[:, 0, :]), ALU.mult))
            own.wait()
            dve.wait_ge(did_pe, 11)
            own.did(dve.tensor_tensor(o[:, :, :], wide(4), o_state[:, :, :], ALU.add))
            dve.wait_ge(did_act, 5)
            own.did(dve.reciprocal(o_r[:, :], o_root[:, :]))
            own.wait()
            own.did(dve.tensor_tensor(o[:, :, :], o[:, :, :], over_columns(o_r[:, :]), ALU.mult))
            dve.wait_ge(did_pe, 12)
            own.did(dve.scalar_tensor_tensor(out=y[:, :, :], in0=cols(6), scalar=k["gdn_gain"][:, 0:1], in1=z[:, :, :],
                                             op0=ALU.mult, op1=ALU.mult))
            for h in range(H):
                if h >= 2:
                    dve.wait_ge(grow_done, h - 1)
                dve.tensor_tensor(v_seq[:, h % 2, :, :], over_heads(v_new[:, h, :], NB), over_columns(mask4), ALU.mult).then_inc(v_masked, 1)
                scale = keep[:, :, h]
                dve.tensor_tensor(S[:, :, h, :], S[:, :, h, :], over_columns(scale), ALU.mult).then_inc(S_step, 1)
                dve.wait_ge(S_step, 3 * h + 1)
                dve.wait_ge(grow_done, h + 1)
                for half in range(2):
                    bs = slice(half * NB // 2, (half + 1) * NB // 2)
                    src = ps[:, 2 * (h % 2) + half, :].rearrange("p (b e) -> p b e", e=P)
                    dve.tensor_tensor(S[:, bs, h, :], S[:, bs, h, :], src, ALU.add).then_inc(S_step, 1)

        @block.scalar
        def _(act):
            act.wait_ge(landed, 16 * (NB + 2))
            act.activation(sq[:, :, :, :], qkv[:, 0:2, :, :], ACT.Square).then_inc(did_act, 1)
            act.wait_ge(did_pe, 1)
            act.activation(root[:, :, :, :], ps[:, 0, :].rearrange("p (a h n) -> p a h n", a=2, h=H), ACT.Sqrt, bias=k["eps"][:, 0:1]).then_inc(did_act, 1)
            act.wait_ge(did_pe, 2)
            act.activation(decay[:, :, :], cols(1, NS), ACT.Exp)
            act.activation(decayT[:, :, :], cols(2, NS), ACT.Exp)
            act.activation(sums[:, :, :], ps[0:NS, 3, 0:2 * H].rearrange("p (a h) -> p a h", h=H), ACT.Exp)
            act.activation(keep[:, :, :], ps[:, 6, 0:NB * H].rearrange("p (b h) -> p b h", h=H), ACT.Exp).then_inc(did_act, 1)
            act.wait_ge(made, 17)
            for h in range(H):
                last = act.activation(o_sq[:, h, :], o[:, h, :], ACT.Square, accum_out=o_ss[:, h:h + 1])
            last.then_inc(did_act, 1)
            act.wait_ge(did_act, 4)
            act.activation(o_root[:, :], o_ss[:, :], ACT.Sqrt, bias=k["eps"][0:NS, 0:1], scale=1.0 / P).then_inc(did_act, 1)

        @block.tensor
        def _(pe):
            own = Steps(pe, did_pe)

            def heads(out, lhsT, rhs):
                for h in range(H):
                    last = pe.matmul(out[:, h, :], lhsT[:, h, :], rhs[:, h, :], start=True, stop=True)
                return last

            def turn(out, src, n):
                for h in range(H):
                    last = pe.transpose(out[:, h, :], src[:, h, :], k["ident"][0:n, 0:n])
                return last

            pe.wait_ge(did_act, 1)
            own.did(pe.matmul(ps[:, 0, :], k["ones"][:, :], sq[:, :, :, :], start=True, stop=True))
            pe.wait_ge(made, 4)
            for h in range(H):
                pe.matmul(cols(1, NS)[:, h, :], g_upto[:, h, :], after[:, :], start=True, stop=True)
            pe.matmul(ps[0:NS, 2, 0:H * NS], after[:, :], g_upto[:, :, :], start=True, stop=True)
            pe.matmul(ps[0:NS, 3, 0:H], upto[:, :], glog, start=True, stop=True)
            pe.matmul(ps[0:NS, 3, H:2 * H], after[:, :], glog, start=True, stop=True)
            own.did(pe.matmul(ps[:, 6, 0:NB * H], k["ones"][0:NS, :], g_seq[:, :, :], start=True, stop=True))
            pe.wait_ge(made, 6)
            heads(cols(4, NS), qkv[:, 1, :, :], qkv[:, 1, :, :])
            own.did(heads(cols(5, NS), qkv[:, 1, :, :], qkv[:, 0, :, :]))
            pe.wait_ge(made, 9)
            pe.wait_ge(did_act, 3)
            own.did(turn(cols(6, NS), Lm[:, 0, :, :], NS))
            pe.wait_ge(made, 10)
            own.did(heads(cols(7, NS), Lm[:, 1, :, :], invT))
            pe.wait_ge(made, 11)
            own.did(heads(cols(6, NS), inv, R))
            turn(wide(0), qkv[:, 1, :, :], P)
            own.did(turn(wide(2), qkv[:, 2, :, :], P))
            pe.wait_ge(made, 13)
            own.did(heads(cols(4), k_in, invT))
            pe.wait_ge(made, 14)
            for h in range(H):
                pe.matmul(cols(5)[:, h, :], v_in[:, h, :], invT[:, h, :], start=True, stop=True)
                for b in range(NB):
                    at = slice(b * TS, (b + 1) * TS)
                    pe.matmul(cols(5)[:, h, at], S[:, b, h, :], wT[:, h, at], start=False, stop=True,
                              skip_group_check=True)
            for h in range(H):
                for b in range(NB):
                    at = slice(b * TS, (b + 1) * TS)
                    last = pe.matmul(cols(6)[:, h, at], S[:, b, h, :], qkv[:, 0, h, at], start=True, stop=True)
            own.did(last)
            pe.wait_ge(made, 15)
            turn(wide(0), v_newT, P)
            own.did(turn(wide(2), o_stateT, P))
            pe.wait_ge(made, 16)
            own.did(heads(wide(4), attnT, v_new))
            pe.wait_ge(made, 19)
            own.did(turn(cols(6), o, NS))
            for h in range(H):
                pe.wait_ge(v_masked, h + 1)
                if h >= 2:
                    pe.wait_ge(S_step, 3 * (h - 2) + 3)
                for half in range(2):
                    bs = slice(half * NB // 2, (half + 1) * NB // 2)
                    last = pe.matmul(ps[:, 2 * (h % 2) + half, :], k_out[:, h, :], v_seq[:, h % 2, bs, :], start=True, stop=True)
                last.then_inc(grow_done, 1)


def merge_branches(nc, k, io, tmp, x2T, high, low):
    stages = (("ya", "w_br_conv"), ("yb", "w_br_gdn"), ("ym", "w_br_mem"), (None, "w_out"))
    with ExitStack() as ctx:
        def sb(name, shape, dt=F32):
            return ctx.enter_context(nc.sbuf_tensor("mb_" + name, shape, dt))

        def sem(name):
            return nc.alloc_semaphore("mb_" + name)

        wt = Weights(nc, ctx, "w_mb")
        ps = ctx.enter_context(nc.psum_tensor("mb_ps", [P, 2, 4, 512], F32))
        raw = sb("raw", [P, KT, N])
        gate = sb("gate", [P, 2, N])
        part = sb("part", [P, 2, N])
        merged = x2T
        raw_in = sem("raw_in")
        gate_in = [sem("gate_in0"), sem("gate_in1")]
        high_made, low_made, gated, merged_done = sem("high_made"), sem("low_made"), sem("gated"), sem("merged_done")
        x2_out = sem("x2_out")
        block = ctx.enter_context(nc.Block())

        @block.sync
        def _(sp):
            sp.dma_start(raw[:, :, :], tmp["ya"]).then_inc(raw_in, 16)
            for st, (_, name) in enumerate(stages):
                if st == 0:
                    for u in range(2):
                        load_weights(sp, wt, io[name], u * P, u, u, first=True)
                with sp.Fori(1 if st == 0 else 0, KT // 2) as i:
                    for u in range(2):
                        load_weights(sp, wt, io[name], (2 * i + u) * P, st * KT + 2 * i + u, u)
                if st < 3:
                    sp.wait_ge(low_made, KT * (st + 1))
                    sp.dma_start(raw[:, :, :], tmp[stages[st + 1][0]] if st < 2 else tmp["xT"]).then_inc(raw_in, 16)
            sp.wait_ge(gated, 4 * KT)
            sp.dma_start(tmp["x2T"], x2T[:, :, :]).then_inc(x2_out, 16)
            sp.wait_ge(x2_out, 16)

        @block.gpsimd
        def _(pool):
            for u in range(2):
                cut_weights(pool, wt, u, 0, u, first=True)
            with pool.Fori(1, 4 * KT // 2) as i:
                for u in range(2):
                    cut_weights(pool, wt, u, i, 2 * i + u)

        @block.tensor
        def _(pe):
            for st in range(4):
                pe.wait_ge(low_made, KT * (st + 1))
                if st == 0:
                    for s in range(2):
                        pe.wait_ge(wt.low_made, s + 1)
                        multiply(pe, wt, high, low, ps[:, s, :, :], s)
                with pe.Fori(1 if st == 0 else 0, KT // 2) as i:
                    for s in range(2):
                        w = st * KT + 2 * i + s
                        pe.wait_ge(wt.low_made, w + 1)
                        pe.wait_ge(gated, w - 1)
                        multiply(pe, wt, high, low, ps[:, s, :, :], s)

        @block.scalar
        def _(act):
            for st in range(4):
                for c in range(KT):
                    if c == 0:
                        if st < 3:
                            act.wait_ge(raw_in, 16 * (st + 1))
                        else:
                            act.wait_ge(merged_done, 2 * KT)
                        if st:
                            act.wait_ge(wt.product_done, st * KT)
                    act.copy(high[:, c, :], raw[:, c, :] if st < 3 else merged[:, c, :]).then_inc(high_made, 1)
                if st == 3:
                    break
                if st == 0:
                    for s in range(2):
                        act.dma_start(gate[:, s, :], tmp["gate"][:, s, :]).then_inc(gate_in[s], 16)
                with act.Fori(1 if st == 0 else 0, KT // 2) as i:
                    for s in range(2):
                        w = st * KT + 2 * i + s
                        act.wait_ge(gated, w - 1)
                        act.dma_start(gate[:, s:s + 1, :], tmp["gate"][:, ds(w, 1), :]).then_inc(gate_in[s], 16)

        @block.vector
        def _(dve):
            for st in range(4):
                for c in range(KT):
                    dve.wait_ge(high_made, st * KT + c + 1)
                    src = raw[:, c, :] if st < 3 else merged[:, c, :]
                    dve.tensor_tensor(low[:, c, :], src, high[:, c, :].bitcast(F32), ALU.subtract).then_inc(low_made, 1)
                if st == 3:
                    dve.wait_ge(raw_in, 64)
                    dve.wait_ge(low_made, 4 * KT)
                with dve.Fori(0, KT // 2) as i:
                    for s in range(2):
                        c = 2 * i + s
                        w = st * KT + c
                        dve.wait_ge(wt.product_done, w + 1)
                        if st < 3:
                            dve.wait_ge(gate_in[s], 16 * (st * (KT // 2)) + 16 * i + 16)
                        for n in range(NCH):
                            at = merged[:, ds(c, 1), chunk(n)].rearrange("p o n -> p (o n)")
                            if st == 0:
                                last = dve.tensor_tensor(at, ps[:, s, n, 0:CH], gate[:, s, chunk(n)], ALU.mult)
                            elif st < 3:
                                last = dve.tensor_tensor(part[:, s, chunk(n)], ps[:, s, n, 0:CH], gate[:, s, chunk(n)], ALU.mult)
                            else:
                                x_at = raw[:, ds(c, 1), chunk(n)].rearrange("p o n -> p (o n)")
                                last = dve.tensor_tensor(at, ps[:, s, n, 0:CH], x_at, ALU.add)
                        last.then_inc(gated, 1)
                        if st in (1, 2):
                            dve.wait_ge(gated, w + 1)
                            dve.tensor_tensor(merged[:, ds(c, 1), :], merged[:, ds(c, 1), :], part[:, s:s + 1, :], ALU.add).then_inc(merged_done, 1)


def top_keys(nc, k, io, high, low, best, where):
    tiles = 2 * KT
    with ExitStack() as ctx:
        def sb(name, shape, dt=F32):
            return ctx.enter_context(nc.sbuf_tensor("tk_" + name, shape, dt))

        def sem(name):
            return nc.alloc_semaphore("tk_" + name)

        wt = Weights(nc, ctx, "w_tk")
        ps = ctx.enter_context(nc.psum_tensor("tk_ps", [P, 8, 512], F32))
        keys = sb("keys", [P, 2, P])
        keysT = sb("keysT", [P, tiles, P])
        qT = [sb(f"qT{s}", [P, NT * P]) for s in range(2)]
        score = [sb(f"score{s}", [P, NT, P]) for s in range(2)]
        rest = sb("rest", [P, NT, P])
        top = [sb(f"top{s}", [P, NT, TOPK]) for s in range(2)]
        at = [sb(f"at{s}", [P, NT, TOPK], U32) for s in range(2)]
        keys_in = [sem("keys_in0"), sem("keys_in1")]
        turned, keysT_kept, padded = sem("turned"), sem("keysT_kept"), sem("padded")
        evacuated, scored, score_kept, found, taken = (sem(n) for n in ("evacuated", "scored", "score_kept", "found", "taken"))
        step, passed = sem("step"), sem("passed")
        block = ctx.enter_context(nc.Block())

        @block.sync
        def _(sp):
            for w in range(tiles):
                if w >= 2:
                    sp.wait_ge(turned, w - 1)
                sp.dma_start(keys[:, w % 2, :], io["peer_sub_keys"][w % 2, w // 2]).then_inc(keys_in[w % 2], 16)
            for u in range(2):
                load_weights(sp, wt, io["peer_w_q"], u * P, u, u, first=True)
            with sp.Fori(1, tiles // 2) as i:
                for u in range(2):
                    load_weights(sp, wt, io["peer_w_q"], (2 * i + u) * P, 2 * i + u, u)

        @block.gpsimd
        def _(pool):
            for s in range(2):
                pool.memset(qT[s][:, N:NT * P], 0.0).then_inc(padded, 1)
            for u in range(2):
                cut_weights(pool, wt, u, 0, u, first=True)
            with pool.Fori(1, tiles // 2) as i:
                for u in range(2):
                    cut_weights(pool, wt, u, i, 2 * i + u)

        def product_banks(s):
            return ps[:, 3 * s:3 * s + NCH, :]

        def score_bank(s, t):
            return ps[:, 6 + t // 4, (t % 4) * P:(t % 4 + 1) * P] if t < NT - 1 else ps[:, 3 * s, CH:CH + P]

        @block.tensor
        def _(pe):
            for w in range(tiles):
                pe.wait_ge(keys_in[w % 2], 16 * (w // 2 + 1))
                if w >= 2:
                    pe.wait_ge(keysT_kept, w - 1)
                pe.transpose(ps[:, w % 2, 0:P], keys[:, w % 2, :], k["ident"][:, :]).then_inc(turned, 1)
            pe.wait_ge(keysT_kept, tiles)
            pe.wait_ge(padded, 2)

            def product(w, s, first=False):
                pe.wait_ge(wt.low_made, w + 1)
                if not first:
                    pe.wait_ge(evacuated, w - 1)
                    pe.wait_ge(score_kept, w - 1)
                multiply(pe, wt, high, low, product_banks(s), s)

            def scores(w, s, first=False):
                pe.wait_ge(evacuated, w + 1)
                if not first:
                    pe.wait_ge(score_kept, w)
                for t in range(NT):
                    last = pe.matmul(score_bank(s, t), qT[s][:, t * P:(t + 1) * P],
                                     keysT[:, ds(w, 1), :].rearrange("p o k -> p (o k)"), start=True, stop=True)
                last.then_inc(scored, 1)

            product(0, 0, first=True)
            product(1, 1, first=True)
            scores(0, 0, first=True)
            with pe.Fori(1, tiles // 2) as i:
                product(2 * i, 0)
                scores(2 * i - 1, 1)
                product(2 * i + 1, 1)
                scores(2 * i, 0)
            scores(tiles - 1, 1)

        @block.scalar
        def _(act):
            def keep_scores(w, s, first=False):
                act.wait_ge(scored, w + 1)
                if not first:
                    act.wait_ge(found, w - 1)
                for b in range(2):
                    act.copy(score[s][:, 4 * b:4 * b + 4, :], ps[:, 6 + b, :].rearrange("p (t k) -> p t k", k=P))
                act.copy(score[s][:, NT - 1, :], score_bank(s, NT - 1)).then_inc(score_kept, 1)

            def keep_q(w, s):
                act.wait_ge(wt.product_done, w + 1)
                for n in range(NCH):
                    last = act.copy(qT[s][:, chunk(n)], product_banks(s)[:, n, 0:CH])
                last.then_inc(evacuated, 1)

            keep_q(0, 0)
            keep_q(1, 1)
            keep_scores(0, 0, first=True)
            keep_q(2, 0)
            keep_scores(1, 1, first=True)
            keep_q(3, 1)
            keep_scores(2, 0)
            with act.Fori(2, tiles // 2) as i:
                keep_q(2 * i, 0)
                keep_scores(2 * i - 1, 1)
                keep_q(2 * i + 1, 1)
                keep_scores(2 * i, 0)
            keep_scores(tiles - 1, 1)

        @block.vector
        def _(dve):
            for w in range(tiles):
                dve.wait_ge(turned, w + 1)
                dve.tensor_copy(keysT[:, w, :], ps[:, w % 2, 0:P]).then_inc(keysT_kept, 1)

            with dve.Fori(0, tiles // 2) as i:
                for s in range(2):
                    w = 2 * i + s
                    dve.wait_ge(score_kept, w + 1)
                    pass_waits(dve, passed)
                    own = Steps(dve, step, w * 4)
                    for t in range(NT):
                        last = dve.max(out=top[s][:, t, 0:8], in_=score[s][:, t, :])
                    own.did(last)
                    own.wait()
                    pass_waits(dve, passed)
                    for t in range(NT):
                        dve.max_index(out=at[s][:, t, 0:8], in_max=top[s][:, t, 0:8], in_values=score[s][:, t, :])
                        last = dve.match_replace(out=rest[:, t, :], in_to_replace=top[s][:, t, 0:8],
                                                 in_values=score[s][:, t, :], imm_value=LOWEST)
                    own.did(last)
                    own.wait()
                    pass_waits(dve, passed)
                    for t in range(NT):
                        last = dve.max(out=top[s][:, t, 8:16], in_=rest[:, t, :])
                    own.did(last)
                    own.wait()
                    pass_waits(dve, passed)
                    for t in range(NT):
                        last = dve.max_index(out=at[s][:, t, 8:16], in_max=top[s][:, t, 8:16], in_values=rest[:, t, :])
                    last.then_inc(found, 1)
                    dve.wait_ge(found, w + 1)
                    dve.tensor_copy(best[:, :, ds(w, 1), :].rearrange("p t o k -> p t (o k)"), top[s][:, :, :])
                    own.did(dve.tensor_copy(where[:, :, ds(w, 1), :].rearrange("p t o k -> p t (o k)"), at[s][:, :, :]))
                    assert own.n == 4


LOWEST = -3.4028234663852886e38
PAIRS = TOPK * TOPK


def top_experts(nc, k, best, where, chosen):
    HK = H * TOPK
    with ExitStack() as ctx:
        def sb(name, shape, dt=F32):
            return ctx.enter_context(nc.sbuf_tensor("te_" + name, shape, dt))

        def sem(name):
            return nc.alloc_semaphore("te_" + name)

        ps = ctx.enter_context(nc.psum_tensor("te_ps", [P, 3, P], F32))
        cand, rest = sb("cand", [P, H, TOPK, TOPK]), sb("rest", [P, H, PAIRS])
        top = sb("top", [P, H, TOPK])
        at = sb("at", [P, H, TOPK], U32)
        rank_i = sb("rank_i", [P, 2, HK], U32)
        rank = sb("rank", [P, 2, HK])
        is_rank = [sb(f"is_rank{p}", [P, HK, TOPK]) for p in range(2)]
        rows = sb("rows", [P, 3, HK])
        shifted, total, inv = sb("shifted", [P, H, TOPK]), sb("total", [P, H]), sb("inv", [P, H])
        step, ranked, second_done, raised, turned, kept = (
            sem(n) for n in ("step", "ranked", "second_done", "raised", "turned", "kept"))
        shifted_done, passed = sem("shifted_done"), sem("passed")
        steps = 14
        block = ctx.enter_context(nc.Block())

        def of_tile(x, t, p):
            return x[:, ds(t, 1), :, :].rearrange("p o (h a) k -> p (o h) a k", a=2)[:, :, p, :]

        iota16 = k["iota"][:, 0:TOPK]

        def is_equal(p):
            return nc.vector.tensor_tensor(is_rank[p][:, :, :], over_heads(iota16, HK), over_columns(rank[:, p, :], TOPK), ALU.is_equal)

        def pick(eng, t, p):
            keys = of_tile(where, t, p).unsqueeze(2).broadcast_to([P, H, TOPK, TOPK])
            v = is_rank[p][:, :, :].rearrange("p (h k) a -> p h k a", h=H)
            return eng.tensor_tensor(v, v, keys, ALU.mult)

        @block.vector
        def _(dve):
            def tile(t, first=False):
                own = Steps(dve, step, t * steps)
                one = of_tile(best, t, 0).unsqueeze(3).broadcast_to([P, H, TOPK, TOPK])
                two = of_tile(best, t, 1).unsqueeze(2).broadcast_to([P, H, TOPK, TOPK])
                own.did(dve.tensor_tensor(cand[:, :, :, :], one, two, ALU.add))
                own.wait()
                pass_waits(dve, passed)
                flat = cand[:, :, :, :].rearrange("p h a b -> p h (a b)")
                for h in range(H):
                    last = dve.max(out=top[:, h, 0:8], in_=flat[:, h, :])
                own.did(last)
                own.wait()
                pass_waits(dve, passed)
                for h in range(H):
                    dve.max_index(out=at[:, h, 0:8], in_max=top[:, h, 0:8], in_values=flat[:, h, :])
                    last = dve.match_replace(out=rest[:, h, :], in_to_replace=top[:, h, 0:8], in_values=flat[:, h, :],
                                             imm_value=LOWEST)
                own.did(last)
                own.wait()
                pass_waits(dve, passed)
                for h in range(H):
                    last = dve.max(out=top[:, h, 8:16], in_=rest[:, h, :])
                own.did(last)
                own.wait()
                if not first:
                    dve.wait_ge(raised, t)
                dve.tensor_tensor(shifted[:, :, :], top[:, :, :], over_columns(top[:, :, 0], TOPK), ALU.subtract).then_inc(shifted_done, 1)
                for h in range(H):
                    last = dve.max_index(out=at[:, h, 8:16], in_max=top[:, h, 8:16], in_values=rest[:, h, :])
                own.did(last)
                own.wait()
                flat_at = at[:, :, :].rearrange("p h k -> p (h k)")
                dve.tensor_scalar(rank_i[:, 0, :], flat_at, 4, None, ALU.logical_shift_right)
                own.did(dve.tensor_scalar(rank_i[:, 1, :], flat_at, TOPK - 1, None, ALU.bitwise_and))
                own.wait()
                own.did(dve.tensor_copy(rank[:, :, :], rank_i[:, :, :]))
                own.wait()
                is_equal(1).then_inc(ranked, 1)
                own.did(is_equal(0))
                own.wait()
                own.did(pick(dve, t, 0))
                own.wait()
                if not first:
                    dve.wait_ge(turned, t)
                own.did(dve.tensor_reduce(rows[:, 0, :], is_rank[0][:, :, :], X, ALU.add))
                dve.wait_ge(raised, t + 1)
                own.did(dve.tensor_reduce(total[:, :], shifted[:, :, :], X, ALU.add))
                own.wait()
                own.did(dve.reciprocal(inv[:, :], total[:, :]))
                own.wait()
                own.did(dve.tensor_tensor(rows[:, 2, :].rearrange("p (h k) -> p h k", h=H), shifted[:, :, :],
                                          over_columns(inv[:, :], TOPK), ALU.mult))
                dve.wait_ge(second_done, t + 1)
                own.did(dve.tensor_reduce(rows[:, 1, :], is_rank[1][:, :, :], X, ALU.add))
                assert own.n == steps
                dve.wait_ge(turned, t + 1)
                dve.tensor_copy(chosen[:, :, ds(t * P, P)], ps[:, :, :]).then_inc(kept, 1)

            tile(0, first=True)
            with dve.Fori(1, NT) as t:
                tile(t)

        @block.gpsimd
        def _(pool):
            with pool.Fori(0, NT) as t:
                pool.wait_ge(ranked, t + 1)
                pick(pool, t, 1).then_inc(second_done, 1)

        @block.scalar
        def _(act):
            with act.Fori(0, NT) as t:
                act.wait_ge(shifted_done, t + 1)
                act.activation(shifted[:, :, :], shifted[:, :, :], ACT.Exp).then_inc(raised, 1)

        @block.tensor
        def _(pe):
            def turn(t, first=False):
                pe.wait_ge(step, (t + 1) * steps)
                if not first:
                    pe.wait_ge(kept, t)
                for r in range(3):
                    last = pe.transpose(ps[:, r, :], rows[:, r, :], k["ident"][:, :])
                last.then_inc(turned, 1)

            turn(0, first=True)
            with pe.Fori(1, NT) as t:
                turn(t)


def spread_gates(nc, k, tmp, chosen):
    UN = 8
    BT = 88
    per = BT // UN
    blocks = N // BT
    with ExitStack() as ctx:
        def sb(name, shape, dt=F32):
            return ctx.enter_context(nc.sbuf_tensor("sg_" + name, shape, dt))

        def sem(name):
            return nc.alloc_semaphore("sg_" + name)

        first_key = [sb(f"first{s}", [P, UN, P]) for s in range(2)]
        weighted = [sb(f"weighted{s}", [P, UN, P]) for s in range(2)]
        second_key = [sb(f"second{s}", [P, UN, P]) for s in range(2)]
        out = [sb(f"out{s}", [P, P, BT]) for s in range(2)]
        ps = ctx.enter_context(nc.psum_tensor("sg_ps", [P, 8, 4, P], F32))
        first_made, second_made, weights_on, spread, kept = (
            sem(n) for n in ("first_made", "second_made", "weights_on", "spread", "kept"))
        stored = [sem("stored0"), sem("stored1")]
        block = ctx.enter_context(nc.Block())

        def all_turns(turn, eng):
            def two_blocks(i, first=False):
                for bs in range(2):
                    for r in range(per):
                        q = 2 * i * per + bs * per + r
                        turn(q, (bs * per + r) % 2, first and bs * per + r < 2)

            two_blocks(0, first=True)
            with eng.Fori(1, blocks // 2) as i:
                two_blocks(i)

        @block.vector
        def _(dve):
            def turn(q, s, first):
                for made, n, used, hot in ((first_made, 0, weights_on, first_key), (second_made, 1, spread, second_key)):
                    if not first:
                        dve.wait_ge(used, q - 1)
                    dve.tensor_tensor(hot[s][:, :, :], over_heads(k["iota"][:, :], UN),
                                      over_columns(chosen[:, n, ds(q * UN, UN)]), ALU.is_equal).then_inc(made, 1)

            all_turns(turn, dve)

        @block.gpsimd
        def _(pool):
            def turn(q, s, first):
                pool.wait_ge(first_made, q + 1)
                if not first:
                    pool.wait_ge(spread, q - 1)
                pool.tensor_tensor(weighted[s][:, :, :], first_key[s][:, :, :],
                                   over_columns(chosen[:, 2, ds(q * UN, UN)]), ALU.mult).then_inc(weights_on, 1)

            all_turns(turn, pool)

        @block.tensor
        def _(pe):
            def turn(q, s, first):
                pe.wait_ge(weights_on, q + 1)
                pe.wait_ge(second_made, q + 1)
                if not first:
                    pe.wait_ge(kept, q - 1)
                for u in range(UN):
                    last = pe.matmul(ps[:, 4 * s + u // 4, u % 4, :], second_key[s][:, u, :], weighted[s][:, u, :],
                                     start=True, stop=True)
                last.then_inc(spread, 1)

            all_turns(turn, pe)

        @block.scalar
        def _(act):
            def keep(q, bs, r):
                act.wait_ge(spread, q + 1)
                for b in range(UN // 4):
                    at = r * UN + 4 * b
                    last = act.copy(out[bs][:, :, at:at + 4], ps[:, 4 * ((bs * per + r) % 2) + b, :, :].rearrange("p n i -> p i n"))
                last.then_inc(kept, 1)

            def two_blocks(i, first=False):
                for bs in range(2):
                    if not first:
                        act.wait_ge(stored[bs], 16 * i)
                    for r in range(per):
                        keep((2 * i + bs) * per + r, bs, r)

            two_blocks(0, first=True)
            with act.Fori(1, blocks // 2) as i:
                two_blocks(i)

        @block.sync
        def _(sp):
            with sp.Fori(0, blocks // 2) as i:
                for bs in range(2):
                    sp.wait_ge(kept, (2 * i + bs) * per + per)
                    sp.dma_start(tmp["gates"][:, :, ds((2 * i + bs) * BT, BT)].rearrange("i j n -> j i n"), out[bs][:, :, :]).then_inc(stored[bs], 16)
            for bs in range(2):
                sp.wait_ge(stored[bs], 16 * (blocks // 2))


def experts(nc, k, io, tmp, h_high, h_low, yT):
    tiles = NE // P
    groups = tiles // 2
    with ExitStack() as ctx:
        def sb(name, shape, dt=F32):
            return ctx.enter_context(nc.sbuf_tensor("ex_" + name, shape, dt))

        def sem(name):
            return nc.alloc_semaphore("ex_" + name)

        u_raw, v_raw = sb("u_raw", [P, 2, D]), sb("v_raw", [P, 2, D])
        uT_high = [sb(f"uT_high{s}", [P, KT, P], F32R) for s in range(2)]
        uT_low = [sb(f"uT_low{s}", [P, KT, P], F32R) for s in range(2)]
        v_high = [sb(f"v_high{s}", [P, D], F32R) for s in range(2)]
        v_low = [sb(f"v_low{s}", [P, D], F32R) for s in range(2)]
        gate = sb("gate", [P, 2, N])
        coef = sb("coef", [P, N])
        c_high = [[sb(f"c_high{a}{s}", [P, N], F32R) for s in range(2)] for a in range(2)]
        c_low = [[sb(f"c_low{a}{s}", [P, N], F32R) for s in range(2)] for a in range(2)]
        ps_t = ctx.enter_context(nc.psum_tensor("ex_t", [P, 2, 4, P], F32))
        ps_a = ctx.enter_context(nc.psum_tensor("ex_a", [P, NCH, 512], F32))
        ps_y = ctx.enter_context(nc.psum_tensor("ex_y", [P, 3, 512], F32))
        names = "x2_in u_turned uT_high_made uT_low_made acted gelu_done weighted coef_high coef_low v_high_made v_low_made multiplied summed".split()
        m = {n: sem(n) for n in names}
        u_in, v_in, g_in = ([sem(f"{n}{s}") for s in range(2)] for n in ("u_in", "v_in", "g_in"))
        units = KT * NCH
        block = ctx.enter_context(nc.Block())

        @block.sync
        def _(sp):
            def load(g, first=False):
                for s in range(2):
                    e = 2 * g + s
                    if not first:
                        sp.wait_ge(m["u_turned"], e - 1)
                    sp.dma_start(u_raw[:, s, :], io["peer_u"][ds(e * P, P), :]).then_inc(u_in[s], 16)
                for s in range(2):
                    e = 2 * g + s
                    if not first:
                        sp.wait_ge(m["weighted"], e - 1)
                    sp.dma_start(gate[:, s, :], tmp["gates"][ds(e, 1), :, :].rearrange("o j n -> j (o n)")).then_inc(g_in[s], 16)
                    if not first:
                        sp.wait_ge(m["v_low_made"], e - 1)
                    sp.dma_start(v_raw[:, s, :], io["peer_v"][ds(e * P, P), :]).then_inc(v_in[s], 16)

            load(0, first=True)
            sp.dma_start(yT[:, :, :], tmp["x2T"]).then_inc(m["x2_in"], 16)
            with sp.Fori(1, groups) as g:
                load(g)

        @block.tensor
        def _(pe):
            def turn(g, s, first=False):
                e = 2 * g + s
                pe.wait_ge(u_in[s], 16 * g + 16)
                if not first:
                    pe.wait_ge(m["uT_low_made"], e)
                for c in range(KT):
                    last = pe.transpose(ps_t[:, c // 4, c % 4, :], u_raw[:, s, c * P:(c + 1) * P], k["ident"][:, :])
                last.then_inc(m["u_turned"], 1)

            def products(g, s, first=False):
                e = 2 * g + s
                pe.wait_ge(m["uT_low_made"], e + 1)
                if not first:
                    pe.wait_ge(m["gelu_done"], e)
                for n in range(NCH):
                    for c in range(KT):
                        for a, b in ((uT_high[s], h_high), (uT_high[s], h_low), (uT_low[s], h_high)):
                            last = pe.matmul(ps_a[:, n, 0:CH], a[:, c, :], b[:, c, chunk(n)],
                                             start=(c == 0 and a is uT_high[s] and b is h_high),
                                             stop=(c == KT - 1 and a is uT_low[s]))
                last.then_inc(m["acted"], 1)

            def values(g, a, first=False):
                pe.wait_ge(m["coef_low"], 2 * g + 2)
                pe.wait_ge(m["v_low_made"], 2 * g + 2)
                for c in range(KT):
                    for n in range(NCH):
                        q = c * NCH + n
                        if not first:
                            pe.wait_ge(m["summed"], g * units + q - 2)
                        elif q >= 3:
                            pe.wait_ge(m["summed"], q - 2)
                        for s in range(2):
                            for x, y in ((v_high[s], c_high[a][s]), (v_high[s], c_low[a][s]), (v_low[s], c_high[a][s])):
                                last = pe.matmul(ps_y[:, n, 0:CH], x[:, c * P:(c + 1) * P], y[:, chunk(n)],
                                                 start=(s == 0 and x is v_high[0] and y is c_high[a][0]),
                                                 stop=(s == 1 and x is v_low[1]))
                        last.then_inc(m["multiplied"], 1)

            turn(0, 0, first=True)
            turn(0, 1)
            products(0, 0, first=True)
            turn(1, 0)
            products(0, 1)
            turn(1, 1)
            products(1, 0)
            turn(2, 0)
            products(1, 1)
            values(0, 0, first=True)

            def pair(i, last=False):
                for a in range(2):
                    g = 2 * i + a
                    turn(g, 1)
                    products(g, 0)
                    if not (last and a == 1):
                        turn(g + 1, 0)
                    products(g, 1)
                    values(g - 1, 1 - a)

            with pe.Fori(1, groups // 2 - 1) as i:
                pair(i)
            pair(groups // 2 - 1, last=True)
            values(groups - 1, 1)

        @block.scalar
        def _(act):
            def turned(g, s, first=False):
                e = 2 * g + s
                act.wait_ge(m["u_turned"], e + 1)
                if not first:
                    act.wait_ge(m["acted"], e - 1)
                for b in range(2):
                    last = act.copy(uT_high[s][:, 4 * b:4 * b + 4, :], ps_t[:, b, :, :])
                last.then_inc(m["uT_high_made"], 1)

            def gelu(g, s, first=False):
                e = 2 * g + s
                act.wait_ge(m["acted"], e + 1)
                if not first:
                    act.wait_ge(m["coef_low"], e)
                for n in range(NCH):
                    last = act.activation(coef[:, chunk(n)], ps_a[:, n, 0:CH], ACT.Gelu)
                last.then_inc(m["gelu_done"], 1)

            def cut_v(g, first=False):
                for s in range(2):
                    act.wait_ge(v_in[s], 16 * g + 16)
                    if not first:
                        act.wait_ge(m["multiplied"], g * units)
                    act.copy(v_high[s][:, :], v_raw[:, s, :]).then_inc(m["v_high_made"], 1)

            def group(g, kind=None):
                turned(g, 1, first=(kind == "first"))
                if kind != "first":
                    cut_v(g - 1, first=(kind == "second"))
                gelu(g, 0, first=(kind == "first"))
                if kind != "last":
                    turned(g + 1, 0)
                gelu(g, 1)

            turned(0, 0, first=True)
            group(0, "first")
            group(1, "second")
            with act.Fori(1, groups // 2 - 1) as i:
                for a in range(2):
                    group(2 * i + a)
            group(groups - 2)
            group(groups - 1, "last")
            cut_v(groups - 1)

        @block.vector
        def _(dve):
            def turned(g, s):
                e = 2 * g + s
                dve.wait_ge(m["uT_high_made"], e + 1)
                for b in range(2):
                    last = dve.tensor_tensor(uT_low[s][:, 4 * b:4 * b + 4, :], ps_t[:, b, :, :],
                                             uT_high[s][:, 4 * b:4 * b + 4, :].bitcast(F32), ALU.subtract)
                last.then_inc(m["uT_low_made"], 1)

            def weigh(g, a, s):
                e = 2 * g + s
                dve.wait_ge(m["gelu_done"], e + 1)
                dve.wait_ge(g_in[s], 16 * g + 16)
                dve.tensor_tensor(coef[:, :], coef[:, :], gate[:, s, :], ALU.mult).then_inc(m["weighted"], 1)
                dve.wait_ge(m["weighted"], e + 1)
                dve.tensor_copy(c_high[a][s][:, :], coef[:, :]).then_inc(m["coef_high"], 1)
                dve.wait_ge(m["coef_high"], e + 1)
                dve.tensor_tensor(c_low[a][s][:, :], coef[:, :], c_high[a][s][:, :].bitcast(F32), ALU.subtract).then_inc(m["coef_low"], 1)

            def cut_v(g):
                for s in range(2):
                    dve.wait_ge(m["v_high_made"], 2 * g + s + 1)
                    dve.tensor_tensor(v_low[s][:, :], v_raw[:, s, :], v_high[s][:, :].bitcast(F32), ALU.subtract).then_inc(m["v_low_made"], 1)

            def sum_up(g):
                for c in range(KT):
                    for n in range(NCH):
                        dve.wait_ge(m["multiplied"], g * units + c * NCH + n + 1)
                        at = yT[:, c, chunk(n)]
                        dve.tensor_tensor(at, at, ps_y[:, n, 0:CH], ALU.add).then_inc(m["summed"], 1)

            def group(g, a, kind=None):
                turned(g, 1)
                if kind != "first":
                    cut_v(g - 1)
                    weigh(g - 1, 1 - a, 1)
                weigh(g, a, 0)
                if kind != "last":
                    turned(g + 1, 0)
                if kind != "first":
                    sum_up(g - 1)

            turned(0, 0)
            group(0, 0, "first")
            dve.wait_ge(m["x2_in"], 16)
            group(1, 1)
            with dve.Fori(1, groups // 2 - 1) as i:
                for a in range(2):
                    group(2 * i + a, a)
            group(groups - 2, 0)
            group(groups - 1, 1, "last")
            cut_v(groups - 1)
            weigh(groups - 1, 1, 1)
            sum_up(groups - 1)


def rows_out(nc, k, src, dram):
    with ExitStack() as ctx:
        def sem(name):
            return nc.alloc_semaphore("ro_" + name)

        rows = ctx.enter_context(nc.sbuf_tensor("ro_rows", [P, 2, D], F32))
        ps = ctx.enter_context(nc.psum_tensor("ro_ps", [P, 2, 2, 512], F32))
        turned, kept_a, kept_b = sem("turned"), sem("kept_a"), sem("kept_b")
        stored = [sem("stored0"), sem("stored1")]
        size = [min(P, N - t * P) for t in range(NT)]
        block = ctx.enter_context(nc.Block())

        @block.tensor
        def _(pe):
            for t in range(NT):
                if t >= 2:
                    pe.wait_ge(kept_a, t - 1)
                    pe.wait_ge(kept_b, t - 1)
                for c in range(KT):
                    last = pe.transpose(ps[0:size[t], t % 2, c // 4, (c % 4) * P:(c % 4 + 1) * P],
                                        src[:, c, t * P:t * P + size[t]], k["ident"][:, :])
                last.then_inc(turned, 1)

        @block.scalar
        def _(act):
            for t in range(NT):
                act.wait_ge(turned, t + 1)
                if t >= 2:
                    act.wait_ge(stored[t % 2], 16 * (t // 2))
                act.copy(rows[0:size[t], t % 2, 0:512], ps[0:size[t], t % 2, 0, :]).then_inc(kept_a, 1)

        @block.vector
        def _(dve):
            for t in range(NT):
                dve.wait_ge(turned, t + 1)
                if t >= 2:
                    dve.wait_ge(stored[t % 2], 16 * (t // 2))
                dve.tensor_copy(rows[0:size[t], t % 2, 512:D], ps[0:size[t], t % 2, 1, :]).then_inc(kept_b, 1)

        @block.sync
        def _(sp):
            for t in range(NT):
                sp.wait_ge(kept_a, t + 1)
                sp.wait_ge(kept_b, t + 1)
                sp.dma_start(dram[t * P:t * P + size[t], :], rows[0:size[t], t % 2, :]).then_inc(stored[t % 2], 16)
            sp.wait_ge(stored[0], 16 * ((NT + 1) // 2))
            sp.wait_ge(stored[1], 16 * (NT // 2))


SHAPES = dict(
    x=(N, D), mem=(M, D), cache_mem_k=(NB, M, MH, D // MH), cache_mem_v=(NB, M, MH, D // MH),
    state_conv=(NB, CK - 1, D), state_gdn_conv=(NB, GK - 1, 3 * D), state_gdn=(NB, H, P, P),
    norm_mix_g=(1, D), w_in=(D, COL_GATE + 3 * D), conv_w=(CK, D), gdn_conv_w=(GK, 3 * D),
    gdn_a_log=(H,), gdn_dt_bias=(H,), gdn_norm_g=(P,), mem_norm_g=(1, D), w_mem_kv=(D, 2 * D),
    w_br_conv=(D, D), w_br_gdn=(D, D), w_br_mem=(D, D), w_out=(D, D), norm_ffn_g=(1, D),
    peer_w_q=(D, 2 * D), peer_sub_keys=(2, H, P, P), peer_u=(NE, D), peer_v=(NE, D), final_norm_g=(1, D))
OUTS = dict(
    out_y=(N, D), out_mem_k=(M, D), out_mem_v=(M, D), out_conv_p=(CK - 1, D), out_gconv_p=(GK - 1, 3 * D),
    out_gdn_p=(H, P, P), out_conv_s=(NB * (CK - 1), D), out_gconv_s=(NB * (GK - 1), 3 * D),
    out_gdn_s=(NB, H, P, P))


def load_x2(nc, tmp, x2T):
    x2_in = nc.alloc_semaphore("x2_in")
    with nc.Block() as block:
        @block.sync
        def _(sp):
            sp.dma_start(x2T[:, :, :], tmp["x2T"]).then_inc(x2_in, 16)
            sp.wait_ge(x2_in, 16)


def load_given(nc, k, tmp):
    s = nc.alloc_semaphore("given_in")
    with nc.Block() as block:
        @block.sync
        def _(sp):
            sp.dma_start(k["glog"][:, :, :], tmp["glog"]).then_inc(s, 16)
            sp.dma_start(k["beta"][:, :, :], tmp["beta"]).then_inc(s, 16)
            sp.wait_ge(s, 32)


def build(nc, io, stages=(1, 2, 3, 4, 5, 6, 7), dump=(), given=()):
    tmp = {name: nc.dram_tensor("tmp_" + name, shape, F32, kind="ExternalOutput" if name in dump else "ExternalInput" if name in given else "Internal").ap()
           for name, shape in dict(
               xT=(P, KT, N), ya=(P, KT, N), qkv=(P, 3 * KT, N), z=(P, KT, N), mq=(P, KT, N), gate=(P, 3 * KT, N),
               ym=(P, KT, N), yb=(P, KT, N), x2T=(P, KT, N), gates=(P, P, N),
               glog=(P, NT, H), beta=(P, NT, H)).items()}
    with ExitStack() as ctx:
        def sb(name, shape, dt=F32):
            return ctx.enter_context(nc.sbuf_tensor(name, shape, dt))

        k = dict(ones=sb("ones", [P, P]), eps=sb("eps", [P, 1]), ident=sb("ident", [P, P]),
                 iota_i=sb("iota_i", [P, P], I32), iota=sb("iota", [P, P]), upto=sb("upto", [P, P]),
                 after=sb("after", [P, P]), same_seq=sb("same_seq", [NS, NS]), chan_a=sb("chan_a", [P, KT, 32]),
                 chan_g=sb("chan_g", [P, 3 * KT, 32]), gdn_gain=sb("gdn_gain", [P, 1]), dt_bias=sb("dt_bias", [P, H]),
                 a_log=sb("a_log", [P, H]), decays=sb("decays", [P, 3, NT, H]), beta_decay=sb("beta_decay", [P, NT, H]),
                 level=sb("level", [P, len(LEVELS), P]), glog=sb("glog", [P, NT, H]), beta=sb("beta", [P, NT, H]))

        def gain(n):
            return k["chan_a"][:, :, A_GAIN + n:A_GAIN + n + 1]

        with nc.cleanup_on_exit():
            make_constants(nc, k, io)
            if 1 in stages:
                with ExitStack() as part:
                    high = part.enter_context(nc.sbuf_tensor("h_high", [P, KT, N], F32R))
                    low = part.enter_context(nc.sbuf_tensor("h_low", [P, KT, N], F32R))
                    with nc.sbuf_tensor("xT", [P, KT, N], F32) as xT:
                        turn_rows(nc, k, io["x"], xT, NT, "x", save=tmp["xT"])
                        norm_channels(nc, k, xT, gain(MIX), N, "mix", high=high, low=low)
                    project_in(nc, k, io, tmp, high, low)
        if 2 in stages:
            with nc.cleanup_on_exit():
                with ExitStack() as part:
                    memT, memn, kT = (part.enter_context(nc.sbuf_tensor(n, [P, KT, M], F32)) for n in ("memT", "memn", "kT"))
                    v_rows = part.enter_context(nc.sbuf_tensor("v_rows", [P, MT, D], F32))
                    turn_rows(nc, k, io["mem"], memT, MT, "mem")
                    norm_channels(nc, k, memT, gain(MEM), M, "memn", out=memn)
                    memory_kv(nc, k, io, memn, kT, v_rows)
                    attend_prompt(nc, k, tmp, kT, v_rows)
                attend_samples(nc, k, io, tmp)
        if 3 in stages:
            with nc.cleanup_on_exit():
                if "glog" in given:
                    load_given(nc, k, tmp)
                decay_sums(nc, k)
                delta_prompt(nc, k, io, tmp)
                delta_samples(nc, k, io, tmp)
        with ExitStack() as part:
            high = part.enter_context(nc.sbuf_tensor("h2_high", [P, KT, N], F32R))
            low = part.enter_context(nc.sbuf_tensor("h2_low", [P, KT, N], F32R))
            with nc.sbuf_tensor("chosen", [P, 3, NT * P], F32) as chosen:
                with nc.cleanup_on_exit():
                    with nc.sbuf_tensor("x2T", [P, KT, N], F32) as x2T:
                        if 4 in stages:
                            merge_branches(nc, k, io, tmp, x2T, high, low)
                        else:
                            load_x2(nc, tmp, x2T)
                        if 5 in stages:
                            norm_channels(nc, k, x2T, gain(FFN), N, "ffn", high=high, low=low)
                if 5 in stages:
                    with nc.cleanup_on_exit():
                        with ExitStack() as keys:
                            best = keys.enter_context(nc.sbuf_tensor("best", [P, NT, 2 * H, TOPK], F32))
                            where = keys.enter_context(nc.sbuf_tensor("where", [P, NT, 2 * H, TOPK], F32))
                            top_keys(nc, k, io, high, low, best, where)
                            top_experts(nc, k, best, where, chosen)
                        spread_gates(nc, k, tmp, chosen)
            if 6 in stages:
                with nc.cleanup_on_exit(), nc.sbuf_tensor("yT", [P, KT, N], F32) as yT:
                    experts(nc, k, io, tmp, high, low, yT)
                    with nc.sbuf_tensor("outT", [P, KT, N], F32) as outT:
                        norm_channels(nc, k, yT, gain(FINAL), N, "final", out=outT)
                        rows_out(nc, k, outT, io["out_y"])


def kernel(**inputs):
    import numpy as _np
    import concourse.bacc as _bacc
    from concourse.bass_utils import run_bass_kernel_spmd as _run

    nc = _bacc.Bacc("TRN2", target_bir_lowering=False, num_devices=1)
    tokens = [_np.reshape(inputs[name], (-1, D)) for name in ("x_prompt", "x_sample")]
    named = dict(inputs, x=_np.concatenate(tokens), mem=inputs["mem_prompt"])
    io, arrays = {}, {}
    for name, shape in SHAPES.items():
        arrays["in_" + name] = _np.ascontiguousarray(_np.reshape(named[name], shape))
        io[name] = nc.dram_tensor("in_" + name, shape, F32, kind="ExternalInput").ap()
    for name, shape in OUTS.items():
        io[name] = nc.dram_tensor(name, shape, F32, kind="ExternalOutput").ap()
    build(nc, io)
    r = _run(nc, [arrays], core_ids=[0]).results[0]
    return (r["out_y"][:TP].reshape(1, TP, D), r["out_y"][TP:].reshape(NB, TS, D),
            r["out_mem_k"].reshape(1, 1, M, MH, D // MH), r["out_mem_v"].reshape(1, 1, M, MH, D // MH),
            r["out_conv_p"].reshape(1, 1, CK - 1, D), r["out_gconv_p"].reshape(1, 1, GK - 1, 3 * D),
            r["out_gdn_p"].reshape(1, 1, H, P, P), r["out_conv_s"].reshape(1, NB, CK - 1, D),
            r["out_gconv_s"].reshape(1, NB, GK - 1, 3 * D), r["out_gdn_s"].reshape(1, NB, H, P, P))
```

```python
from contextlib import ExitStack

import concourse.bass as bass
from concourse import mybir

P = 128
F32 = mybir.dt.float32
F32R = mybir.dt.float32r
I32 = mybir.dt.int32
U32 = mybir.dt.uint32
ALU = mybir.AluOpType
ACT = mybir.ActivationFunctionType
X = mybir.AxisListType.X
ds = bass.ds

D = 1024
KT = D // P
TP = 1024
NB, TS = 8, 4
NS = NB * TS
N = TP + NS
NCH = 3
CH = N // NCH
NT = 9
CK, GK = 3, 4
H = 8
M = 256
MT = M // P
MH = 4
TOPK = 16
NE = 16384
EPS = 1e-6

COL_U, COL_B, COL_C, COL_QKV, COL_Z, COL_AB = 0, D, 2 * D, 3 * D, 6 * D, 7 * D
COL_MQ = COL_AB + 2 * H
COL_GATE = COL_MQ + D

A_TAP = NB * (CK - 1)
A_GAIN = A_TAP + CK
A_ROWS = A_GAIN + 4
MIX, FFN, FINAL, MEM = range(4)
G_TAP = NB * (GK - 1)
G_ROWS = G_TAP + GK
A_OUT = (NB + 1) * (CK - 1)
G_OUT = (NB + 1) * (GK - 1)


def chunk(c):
    return slice(c * CH, (c + 1) * CH)


def make_constants(nc, k, io):
    with ExitStack() as ctx:
        rows_a = ctx.enter_context(nc.sbuf_tensor("rows_a", [A_ROWS, D], F32))
        rows_g = ctx.enter_context(nc.sbuf_tensor("rows_g", [G_ROWS, 3 * D], F32))
        ps = ctx.enter_context(nc.psum_tensor("ps_const", [P, 2, 512], F32))
        rows_in = nc.alloc_semaphore("rows_in")
        small_in = nc.alloc_semaphore("small_in")
        filled = nc.alloc_semaphore("filled")
        made = nc.alloc_semaphore("made")
        turned = nc.alloc_semaphore("turned")
        kept = nc.alloc_semaphore("kept")
        block = ctx.enter_context(nc.Block())

        @block.sync
        def _(sp):
            sp.dma_start(rows_a[0:A_TAP, :], io["state_conv"].rearrange("b t c -> (b t) c")).then_inc(rows_in, 16)
            sp.dma_start(rows_a[A_TAP:A_GAIN, :], io["conv_w"]).then_inc(rows_in, 16)
            for n, name in enumerate(("norm_mix_g", "norm_ffn_g", "final_norm_g", "mem_norm_g")):
                sp.dma_start(rows_a[A_GAIN + n:A_GAIN + n + 1, :], io[name]).then_inc(rows_in, 16)
            sp.dma_start(rows_g[0:G_TAP, :], io["state_gdn_conv"].rearrange("b t c -> (b t) c")).then_inc(rows_in, 16)
            sp.dma_start(rows_g[G_TAP:G_ROWS, :], io["gdn_conv_w"]).then_inc(rows_in, 16)
            sp.dma_start(k["gdn_gain"][:, :], io["gdn_norm_g"].rearrange("(p o) -> p o", o=1)).then_inc(small_in, 16)
            sp.dma_start(k["dt_bias"][:, :], io["gdn_dt_bias"].partition_broadcast(P)).then_inc(small_in, 16)
            sp.dma_start(k["a_log"][:, :], io["gdn_a_log"].partition_broadcast(P)).then_inc(small_in, 16)
            sp.wait_ge(small_in, 48)

        @block.gpsimd
        def _(pool):
            pool.memset(k["ones"][:, :], 1.0).then_inc(filled, 1)
            pool.memset(k["eps"][:, :], EPS).then_inc(filled, 1)
            pool.memset(k["ident"][:, :], 0.0).then_inc(filled, 1)
            pool.iota(k["iota_i"][:, :], [[1, P]], base=0, channel_multiplier=0).then_inc(filled, 1)
            pool.wait_ge(filled, 4)
            pool.tensor_copy(k["iota"][:, :], k["iota_i"][:, :]).then_inc(made, 1)
            pool.affine_select(out=k["ident"][:, :], in_=k["ident"][:, :], compare_op=ALU.not_equal, fill=1.0,
                               base=0, pattern=[[-1, P]], channel_multiplier=1).then_inc(made, 1)
            pool.affine_select(out=k["upto"][:, :], in_=k["ones"][:, :], compare_op=ALU.is_ge, fill=0.0,
                               base=0, pattern=[[1, P]], channel_multiplier=-1).then_inc(made, 1)
            pool.affine_select(out=k["after"][:, :], in_=k["ones"][:, :], compare_op=ALU.is_ge, fill=0.0,
                               base=-1, pattern=[[-1, P]], channel_multiplier=1).then_inc(made, 1)
            sb = k["same_seq"]
            v = sb[:, :].rearrange("p (b t) -> p b t", t=TS)
            pool.affine_select(out=v, in_=k["ones"][0:NS, 0:NS].rearrange("p (b t) -> p b t", t=TS),
                               compare_op=ALU.is_ge, fill=0.0, base=0, pattern=[[-TS, NB], [0, TS]],
                               channel_multiplier=1).then_inc(made, 1)
            pool.wait_ge(made, 5)
            pool.affine_select(out=v, in_=v, compare_op=ALU.is_ge, fill=0.0, base=TS - 1,
                               pattern=[[TS, NB], [0, TS]], channel_multiplier=-1).then_inc(made, 1)
            pool.wait_ge(made, 6)

        @block.tensor
        def _(pe):
            pe.wait_ge(rows_in, 16 * 8)
            pe.wait_ge(made, 2)
            for t in range(KT):
                pe.transpose(ps[:, 0, 32 * t:32 * t + A_ROWS], rows_a[:, t * P:(t + 1) * P],
                             k["ident"][0:A_ROWS, 0:A_ROWS]).then_inc(turned, 1)
            for g in range(3):
                if g:
                    pe.wait_ge(kept, g + 1)
                for t in range(KT):
                    c = g * KT + t
                    pe.transpose(ps[:, 1, 32 * t:32 * t + G_ROWS], rows_g[:, c * P:(c + 1) * P],
                                 k["ident"][0:G_ROWS, 0:G_ROWS]).then_inc(turned, 1)

        @block.vector
        def _(dve):
            for g in range(4):
                dve.wait_ge(turned, KT * (g + 1))
                dst = k["chan_a"][:, :, :] if g == 0 else k["chan_g"][:, (g - 1) * KT:g * KT, :]
                rows = A_ROWS if g == 0 else G_ROWS
                src = ps[:, min(g, 1), 0:32 * KT].rearrange("p (t r) -> p t r", r=32)
                dve.tensor_copy(dst[:, :, 0:rows], src[:, :, 0:rows]).then_inc(kept, 1)
            dve.wait_ge(kept, 4)


def turn_rows(nc, k, rows_dram, xT, n_tiles, name, save=None):
    total = rows_dram.shape[0]
    with ExitStack() as ctx:
        rows = ctx.enter_context(nc.sbuf_tensor(name + "_rows", [P, 2, D], F32))
        ps = ctx.enter_context(nc.psum_tensor(name + "_ps", [P, 2, 2, 512], F32))
        landed = [nc.alloc_semaphore(f"{name}_landed{s}") for s in range(2)]
        turned = nc.alloc_semaphore(name + "_turned")
        kept = nc.alloc_semaphore(name + "_kept")
        saved = nc.alloc_semaphore(name + "_saved")
        block = ctx.enter_context(nc.Block())
        size = [min(P, total - t * P) for t in range(n_tiles)]

        @block.sync
        def _(sp):
            for t in range(n_tiles):
                if t >= 2:
                    sp.wait_ge(turned, t - 1)
                sp.dma_start(rows[0:size[t], t % 2, :], rows_dram[t * P:t * P + size[t], :]).then_inc(landed[t % 2], 16)
            if save is not None:
                sp.wait_ge(kept, n_tiles)
                sp.dma_start(save, xT[:, :, :]).then_inc(saved, 16)
                sp.wait_ge(saved, 16)

        @block.tensor
        def _(pe):
            for t in range(n_tiles):
                pe.wait_ge(landed[t % 2], 16 * (t // 2 + 1))
                if t >= 2:
                    pe.wait_ge(kept, t - 1)
                for c in range(KT):
                    last = pe.transpose(ps[:, t % 2, c // 4, (c % 4) * P:(c % 4) * P + size[t]],
                                        rows[0:size[t], t % 2, c * P:(c + 1) * P],
                                        k["ident"][0:size[t], 0:size[t]])
                last.then_inc(turned, 1)

        @block.scalar
        def _(act):
            for t in range(n_tiles):
                act.wait_ge(turned, t + 1)
                for b in range(2):
                    src = ps[:, t % 2, b, :].rearrange("p (c n) -> p c n", n=P)[:, :, 0:size[t]]
                    last = act.copy(xT[:, 4 * b:4 * b + 4, t * P:t * P + size[t]], src)
                last.then_inc(kept, 1)


def norm_channels(nc, k, xT, gain, width, name, high=None, low=None, out=None, wt=None, first_tiles=()):
    nch = max(1, -(-width // 512))
    w = width // nch
    with ExitStack() as ctx:
        sq = ctx.enter_context(nc.sbuf_tensor(name + "_sq", [P, 2, width], F32))
        root = ctx.enter_context(nc.sbuf_tensor(name + "_root", [P, width], F32))
        rinv = ctx.enter_context(nc.sbuf_tensor(name + "_rinv", [P, width], F32))
        full = out if out is not None else ctx.enter_context(nc.sbuf_tensor(name + "_full", [P, 2, width], F32))
        ps = ctx.enter_context(nc.psum_tensor(name + "_ps", [P, nch, 512], F32))
        squared = nc.alloc_semaphore(name + "_squared")
        summed = nc.alloc_semaphore(name + "_summed")
        rooted = nc.alloc_semaphore(name + "_rooted")
        inverted = nc.alloc_semaphore(name + "_inverted")
        normed = nc.alloc_semaphore(name + "_normed")
        high_made = nc.alloc_semaphore(name + "_high")
        low_made = nc.alloc_semaphore(name + "_low")
        block = ctx.enter_context(nc.Block())
        ring = out is None

        def full_of(c):
            return full[:, c % 2, :] if ring else full[:, c, :]

        if wt:
            @block.sync
            def _(sp):
                for u in range(2):
                    load_weights(sp, wt, *first_tiles[u], u, u, first=True)

            @block.gpsimd
            def _(pool):
                for u in range(2):
                    cut_weights(pool, wt, u, 0, u, first=True)

        @block.scalar
        def _(act):
            for c in range(KT):
                if c >= 2:
                    act.wait_ge(summed, c - 1)
                act.activation(sq[:, c % 2, :], xT[:, c, :], ACT.Square).then_inc(squared, 1)
            act.wait_ge(summed, KT)
            for c in range(nch):
                act.activation(root[:, c * w:(c + 1) * w], ps[:, c, 0:w], ACT.Sqrt, bias=k["eps"][:, 0:1],
                               scale=1.0 / D).then_inc(rooted, 1)
            if ring:
                for c in range(KT):
                    act.wait_ge(normed, c + 1)
                    act.copy(high[:, c, :], full_of(c)).then_inc(high_made, 1)

        @block.tensor
        def _(pe):
            for c in range(KT):
                pe.wait_ge(squared, c + 1)
                for n in range(nch):
                    last = pe.matmul(ps[:, n, 0:w], k["ones"][:, :], sq[:, c % 2, n * w:(n + 1) * w],
                                     start=(c == 0), stop=(c == KT - 1))
                last.then_inc(summed, 1)

        @block.vector
        def _(dve):
            dve.wait_ge(rooted, nch)
            dve.reciprocal(rinv[:, :], root[:, :]).then_inc(inverted, 1)
            dve.wait_ge(inverted, 1)
            for c in range(KT):
                if ring and c >= 2:
                    dve.wait_ge(low_made, c - 1)
                dve.scalar_tensor_tensor(out=full_of(c), in0=xT[:, c, :], scalar=gain[:, c, :], in1=rinv[:, :],
                                         op0=ALU.mult, op1=ALU.mult).then_inc(normed, 1)
                if ring:
                    dve.wait_ge(high_made, c + 1)
                    dve.tensor_tensor(low[:, c, :], full_of(c), high[:, c, :].bitcast(F32),
                                      ALU.subtract).then_inc(low_made, 1)


class Weights:

    def __init__(self, nc, ctx, name, slots_of=None):
        def sem(n):
            return nc.alloc_semaphore(f"{name}_{n}")

        if slots_of:
            self.raw, self.high, self.low = slots_of.raw, slots_of.high, slots_of.low
        else:
            self.allocate(nc, ctx, name)
        self.landed = [sem("landed0"), sem("landed1")]
        self.high_made = sem("high_made")
        self.low_made = sem("low_made")
        self.product_done = sem("product_done")
        self.passed = sem("passed")

    def allocate(self, nc, ctx, name):
        self.raw = ctx.enter_context(nc.sbuf_tensor(name + "_raw", [P, 2, KT, P], F32))
        self.high = [ctx.enter_context(nc.sbuf_tensor(f"{name}_high{s}", [P, KT, P], F32R)) for s in range(2)]
        self.low = [ctx.enter_context(nc.sbuf_tensor(f"{name}_low{s}", [P, KT, P], F32R)) for s in range(2)]


def load_weights(sp, wt, dram, column, w, s, first=False):
    if not first:
        sp.wait_ge(wt.low_made, w - 1)
    sp.dma_start(wt.raw[:, s, :, :], dram[:, ds(column, P)].rearrange("(k p) c -> p k c", p=P)).then_inc(wt.landed[s], 16)


def pass_waits(eng, passed):
    eng.sem_inc(passed, 1)


def cut_weights(pool, wt, s, turn, w, first=False):
    pool.wait_ge(wt.landed[s], 16 * turn + 16)
    if not first:
        pool.wait_ge(wt.product_done, w - 1)
        pass_waits(pool, wt.passed)
    pool.tensor_copy(wt.high[s][:, :, :], wt.raw[:, s, :, :]).then_inc(wt.high_made, 1)
    pool.wait_ge(wt.high_made, w + 1)
    pool.tensor_tensor(wt.low[s][:, :, :], wt.raw[:, s, :, :], wt.high[s][:, :, :].bitcast(F32),
                       ALU.subtract).then_inc(wt.low_made, 1)


def multiply(pe, wt, high, low, banks, s, rows=P, cut=None):
    for n in range(NCH):
        for kk in range(KT):
            if cut and n == 0:
                pe.wait_ge(cut[0], cut[1] + kk + 1)
            for a, b in ((wt.high[s], high), (wt.high[s], low), (wt.low[s], high)):
                last = pe.matmul(banks[0:rows, n, 0:CH], a[:, kk, 0:rows], b[:, kk, chunk(n)],
                                 start=(kk == 0 and a is wt.high[s] and b is high),
                                 stop=(kk == KT - 1 and a is wt.low[s]))
        if n == NCH - 1:
            last.then_inc(wt.product_done, 1)


class Steps:

    def __init__(self, eng, sem, base=0):
        self.eng, self.sem, self.base, self.n = eng, sem, base, 0

    def did(self, instruction):
        instruction.then_inc(self.sem, 1)
        self.n += 1

    def wait(self):
        self.eng.wait_ge(self.sem, self.base + self.n)


RUNS = (("conv", 3 * KT, 6), ("qkv", 3 * KT, 2), ("z", KT, 2), ("mq", KT, 2), ("gate", 3 * KT, 2))


def run_column(name, pair, u):
    if name == "conv":
        return (COL_U, COL_B, COL_C)[u % 3] + (pair * 2 + u // 3) * P
    return {"qkv": COL_QKV, "z": COL_Z, "mq": COL_MQ, "gate": COL_GATE}[name] + (pair * 2 + u) * P


def project_in(nc, k, io, tmp, high, low, wt):
    starts, total = {}, 0
    for name, tiles, _ in RUNS:
        starts[name] = total
        total += tiles
    conv_steps = 3 + 1 + CK - 1 + 1
    qkv_steps = 1 + GK - 1
    with ExitStack() as ctx:
        def sb(name, shape, dt=F32):
            return ctx.enter_context(nc.sbuf_tensor(name, shape, dt))

        def sem(name):
            return nc.alloc_semaphore(name)

        ps = ctx.enter_context(nc.psum_tensor("p_in", [P, 2, 4, 512], F32))
        plain = sb("plain", [P, 2, N])
        gate_u, gate_b, gate_c = (sb(n, [P, 2, N]) for n in ("gate_u", "gate_b", "gate_c"))
        conv_in = sb("conv_in", [P, 2, GK - 1 + TP])
        conv_in_s = sb("conv_in_s", [P, 2, NB, GK - 1 + TS])
        conv_out = sb("conv_out", [P, 2, N])
        tap_now = sb("tap_now", [P, 2, GK])
        new_a = sb("new_a", [P, KT, A_OUT])
        new_g = sb("new_g", [P, 3 * KT, G_OUT])
        w_ab = sb("w_ab", [P, KT, 2 * H])
        w_ab_high = sb("w_ab_high", [P, KT, 2 * H], F32R)
        w_ab_low = sb("w_ab_low", [P, KT, 2 * H], F32R)
        ab = sb("ab", [2 * H, NT * P])
        ab_rows = sb("ab_rows", [P, NT, 2 * H])
        soft = sb("soft", [P, 4, NT, H])
        state_rows_g = sb("state_rows_g", [G_OUT, 3 * D])
        state_rows_a = sb("state_rows_a", [A_OUT, D])
        evacuated = sem("evacuated")
        conv_step = sem("conv_step")
        convolved = sem("convolved")
        ready = sem("ready")
        stored = [sem("stored0"), sem("stored1")]
        ab_in, ab_cut, ab_done, ab_kept = sem("ab_in"), sem("ab_cut"), sem("ab_done"), sem("ab_kept")
        rows_done, soft_step, soft_act = sem("rows_done"), sem("soft_step"), sem("soft_act")
        states_turned, states_kept, states_out = sem("states_turned"), sem("states_kept"), sem("states_out")
        block = ctx.enter_context(nc.Block())

        @block.sync
        def _(sp):
            sp.dma_start(w_ab[:, :, :], io["w_in"][:, COL_AB:COL_AB + 2 * H].rearrange("(k p) c -> p k c", p=P)).then_inc(ab_in, 16)
            for name, tiles, per in RUNS:
                if name == "conv":
                    for u in range(2, per):
                        load_weights(sp, wt, io["w_in"], run_column(name, 0, u), u, u % 2, first=u < 2)
                with sp.Fori(1 if name == "conv" else 0, tiles // per) as i:
                    for u in range(per):
                        w = starts[name] + i * per + u
                        load_weights(sp, wt, io["w_in"], run_column(name, i, u), w, u % 2)
            sp.wait_ge(states_kept, 8)
            for dst, src in ((io["out_conv_p"], state_rows_a[0:CK - 1, :]), (io["out_conv_s"], state_rows_a[CK - 1:A_OUT, :]),
                             (io["out_gconv_p"], state_rows_g[0:GK - 1, :]), (io["out_gconv_s"], state_rows_g[GK - 1:G_OUT, :])):
                sp.dma_start(dst, src).then_inc(states_out, 16)
            sp.wait_ge(states_out, 64)

        @block.gpsimd
        def _(pool):
            with pool.Fori(1, total // 2) as i:
                for u in range(2):
                    cut_weights(pool, wt, u, i, 2 * i + u)

        @block.tensor
        def _(pe):
            def tile(s, w, first=False):
                pe.wait_ge(wt.low_made, w + 1)
                if not first:
                    pe.wait_ge(evacuated, w - 1)
                multiply(pe, wt, high, low, ps[:, s, :, :], s)

            pe.wait_ge(ab_cut, 2)
            for n in range(NCH):
                if n:
                    pe.wait_ge(ab_kept, n + 1)
                for kk in range(KT):
                    for a, b in ((w_ab_high, high), (w_ab_high, low), (w_ab_low, high)):
                        last = pe.matmul(ps[0:2 * H, 0, 3, 0:CH], a[:, kk, :], b[:, kk, chunk(n)],
                                         start=(kk == 0 and a is w_ab_high and b is high),
                                         stop=(kk == KT - 1 and a is w_ab_low))
                last.then_inc(ab_done, 1)
            pe.wait_ge(ab_kept, NCH + 1)
            for t in range(NT):
                last = pe.transpose(ps[:, 1, 3, t * 2 * H:(t + 1) * 2 * H], ab[:, t * P:(t + 1) * P],
                                    k["ident"][0:2 * H, 0:2 * H])
            last.then_inc(rows_done, 1)
            for s in range(2):
                tile(s, s, first=True)
            with pe.Fori(1, total // 2) as i:
                for s in range(2):
                    tile(s, 2 * i + s)
            pe.wait_ge(convolved, 4 * KT)
            for q in range(8):
                g, half = q // 2, q % 2
                if q:
                    pe.wait_ge(states_kept, q)
                for t in range(4):
                    c = 4 * half + t
                    src = new_a[:, c, :] if g == 0 else new_g[:, (g - 1) * KT + c, :]
                    rows = A_OUT if g == 0 else G_OUT
                    last = pe.transpose(ps[0:rows, 0, 3, t * P:(t + 1) * P], src, k["ident"][:, :])
                last.then_inc(states_turned, 1)

        @block.scalar
        def _(act):
            act.wait_ge(soft_step, 4)
            act.activation(soft[:, 1, :, :], soft[:, 1, :, :], ACT.Exp, scale=-1.0).then_inc(soft_act, 1)
            act.activation(k["a_log"][:, :], k["a_log"][:, :], ACT.Exp).then_inc(soft_act, 1)
            act.wait_ge(soft_act, 1)
            act.activation(soft[:, 1, :, :], soft[:, 1, :, :], ACT.Ln, bias=k["ones"][:, 0:1]).then_inc(soft_act, 1)
            act.activation(k["beta"][:, :, :], ab_rows[:, :, H:2 * H], ACT.Sigmoid).then_inc(soft_act, 1)

            def conv_turn(i, first=False):
                for v in range(2):
                    if not first:
                        act.wait_ge(convolved, 2 * i + v - 1)
                    for j, dst in enumerate((gate_u, gate_b, gate_c)):
                        u = 3 * v + j
                        act.wait_ge(wt.product_done, 6 * i + u + 1)
                        for n in range(NCH):
                            last = act.copy(dst[:, v, chunk(n)], ps[:, u % 2, n, 0:CH])
                        last.then_inc(evacuated, 1)
                    act.wait_ge(convolved, 2 * i + v + 1)
                    act.dma_start(tmp["ya"][:, ds(2 * i + v, 1), :], plain[:, v:v + 1, :]).then_inc(stored[v], 16)

            conv_turn(0, first=True)
            with act.Fori(1, KT // 2) as i:
                conv_turn(i)

            with act.Fori(0, 3 * KT // 2) as i:
                for s in range(2):
                    act.wait_ge(wt.product_done, starts["qkv"] + 2 * i + s + 1)
                    src = ps[:, s, :, :]
                    act.copy(conv_in[:, s, GK - 1:GK - 1 + CH], src[:, 0, 0:CH])
                    act.copy(conv_in[:, s, GK - 1 + CH:GK - 1 + 2 * CH], src[:, 1, 0:CH])
                    act.copy(conv_in[:, s, GK - 1 + 2 * CH:GK - 1 + TP], src[:, 2, 0:TP - 2 * CH])
                    act.copy(conv_in_s[:, s, :, GK - 1:GK - 1 + TS],
                             src[:, 2, TP - 2 * CH:CH].rearrange("p (b t) -> p b t", t=TS)).then_inc(evacuated, 1)
                    act.wait_ge(convolved, KT + 2 * i + s + 1)
                    act.wait_ge(stored[s], 16 * (KT // 2) + 16 * i)
                    act.activation(plain[:, s, :], conv_out[:, s, :], ACT.Silu).then_inc(ready, 1)
                    act.wait_ge(ready, 2 * i + s + 1)
                    act.dma_start(tmp["qkv"][:, ds(2 * i + s, 1), :], plain[:, s:s + 1, :]).then_inc(stored[s], 16)
            n_stored = 2 * KT
            for name, tiles, func in (("z", KT, ACT.Silu), ("mq", KT, ACT.Copy), ("gate", 3 * KT, ACT.Sigmoid)):
                with act.Fori(0, tiles // 2) as i:
                    for s in range(2):
                        w = starts[name] + 2 * i + s
                        act.wait_ge(stored[s], 16 * n_stored + 16 * i)
                        act.wait_ge(wt.product_done, w + 1)
                        for n in range(NCH):
                            last = act.activation(plain[:, s, chunk(n)], ps[:, s, n, 0:CH], func)
                        last.then_inc(evacuated, 1)
                        act.wait_ge(evacuated, w + 1)
                        act.dma_start(tmp[name][:, ds(2 * i + s, 1), :], plain[:, s:s + 1, :]).then_inc(stored[s], 16)
                n_stored += tiles // 2
            for s in range(2):
                act.wait_ge(stored[s], 16 * n_stored)

        @block.vector
        def _(dve):
            dve.wait_ge(ab_in, 16)
            dve.tensor_copy(w_ab_high[:, :, :], w_ab[:, :, :]).then_inc(ab_cut, 1)
            dve.memset(ab[:, N:NT * P], 0.0).then_inc(ab_kept, 1)
            dve.memset(conv_in[:, :, 0:GK - 1], 0.0)
            dve.wait_ge(ab_cut, 1)
            dve.tensor_tensor(w_ab_low[:, :, :], w_ab[:, :, :], w_ab_high[:, :, :].bitcast(F32),
                              ALU.subtract).then_inc(ab_cut, 1)
            for n in range(NCH):
                dve.wait_ge(ab_done, n + 1)
                dve.tensor_copy(ab[:, chunk(n)], ps[0:2 * H, 0, 3, 0:CH]).then_inc(ab_kept, 1)
            dve.wait_ge(rows_done, 1)
            own = Steps(dve, soft_step)
            own.did(dve.tensor_copy(ab_rows[:, :, :], ps[:, 1, 3, 0:NT * 2 * H].rearrange("p (t c) -> p t c", c=2 * H)))
            own.wait()
            bias = k["dt_bias"][:, :].unsqueeze(1).broadcast_to([P, NT, H])
            own.did(dve.tensor_tensor(soft[:, 0, :, :], ab_rows[:, :, 0:H], bias, ALU.add))
            own.wait()
            own.did(dve.tensor_scalar(soft[:, 2, :, :], soft[:, 0, :, :], 0.0, None, ALU.max))
            own.wait()
            own.did(dve.scalar_tensor_tensor(out=soft[:, 1, :, :], in0=soft[:, 2, :, :], scalar=2.0,
                                             in1=soft[:, 0, :, :], op0=ALU.mult, op1=ALU.subtract))
            own.wait()
            dve.wait_ge(soft_act, 3)
            own.did(dve.tensor_tensor(soft[:, 3, :, :], soft[:, 1, :, :], soft[:, 2, :, :], ALU.add))
            own.wait()
            rate = k["a_log"][:, :].unsqueeze(1).broadcast_to([P, NT, H])
            own.did(dve.tensor_tensor(soft[:, 0, :, :], soft[:, 3, :, :], rate, ALU.mult))
            own.wait()
            dve.tensor_scalar(k["glog"][:, :, :], soft[:, 0, :, :], -1.0, None, ALU.mult)

            def taps(own, s, kk):
                prompt = conv_in[:, s, GK - kk:GK - 1 + TP]
                samples = conv_in_s[:, s, :, GK - kk:GK - 1 + TS]
                out_s = conv_out[:, s, TP:N].rearrange("p (b t) -> p b t", t=TS)
                for j in range(kk):
                    a, b, tap = prompt[:, j:j + TP], samples[:, :, j:j + TS], tap_now[:, s, j:j + 1]
                    if j == 0:
                        dve.tensor_scalar(conv_out[:, s, 0:TP], a, tap, None, ALU.mult)
                        last = dve.tensor_scalar(out_s, b, tap, None, ALU.mult)
                    else:
                        own.wait()
                        dve.scalar_tensor_tensor(out=conv_out[:, s, 0:TP], in0=a, scalar=tap,
                                                 in1=conv_out[:, s, 0:TP], op0=ALU.mult, op1=ALU.add)
                        last = dve.scalar_tensor_tensor(out=out_s, in0=b, scalar=tap, in1=out_s,
                                                        op0=ALU.mult, op1=ALU.add)
                    if j < kk - 1:
                        own.did(last)
                return last

            def load_taps(own, s, c, chan, state, kk):
                own.did(dve.tensor_copy(conv_in_s[:, s, :, GK - kk:GK - 1],
                                        chan[:, ds(c, 1), 0:state].rearrange("p o (b t) -> p (o b) t", t=kk - 1)))
                own.did(dve.tensor_copy(tap_now[:, s:s + 1, 0:kk], chan[:, ds(c, 1), state:state + kk]))

            def keep_state(s, c, new, kk):
                dve.tensor_copy(new[:, ds(c, 1), 0:kk - 1], conv_in[:, s:s + 1, TP + GK - kk:TP + GK - 1])
                return dve.tensor_copy(new[:, ds(c, 1), kk - 1:(NB + 1) * (kk - 1)].rearrange("p o (b t) -> p (o b) t", t=kk - 1),
                                       conv_in_s[:, s, :, TS + GK - kk:TS + GK - 1])

            def conv_turn(i, first=False):
                for v in range(2):
                    own = Steps(dve, conv_step, (2 * i + v) * conv_steps)
                    load_taps(own, v, 2 * i + v, k["chan_a"], A_TAP, CK)
                    dve.wait_ge(evacuated, 6 * i + 3 * v + 3)
                    dve.tensor_tensor(conv_in[:, v, GK - 1:GK - 1 + TP], gate_c[:, v, 0:TP], gate_u[:, v, 0:TP], ALU.mult)
                    own.did(dve.tensor_tensor(conv_in_s[:, v, :, GK - 1:GK - 1 + TS],
                                              gate_c[:, v, TP:N].rearrange("p (b t) -> p b t", t=TS),
                                              gate_u[:, v, TP:N].rearrange("p (b t) -> p b t", t=TS), ALU.mult))
                    own.wait()
                    own.did(keep_state(v, 2 * i + v, new_a, CK))
                    own.did(taps(own, v, CK))
                    own.wait()
                    assert own.n == conv_steps
                    if not first:
                        dve.wait_ge(stored[v], 16 * i)
                    dve.tensor_tensor(plain[:, v, :], conv_out[:, v, :], gate_b[:, v, :], ALU.mult).then_inc(convolved, 1)

            conv_turn(0, first=True)
            with dve.Fori(1, KT // 2) as i:
                conv_turn(i)

            def qkv_turn(i, first=False):
                for s in range(2):
                    own = Steps(dve, conv_step, KT * conv_steps + (2 * i + s) * (qkv_steps + 2))
                    load_taps(own, s, 2 * i + s, k["chan_g"], G_TAP, GK)
                    if not first:
                        dve.wait_ge(ready, 2 * i + s - 1)
                    dve.wait_ge(evacuated, starts["qkv"] + 2 * i + s + 1)
                    own.wait()
                    own.did(keep_state(s, 2 * i + s, new_g, GK))
                    taps(own, s, GK).then_inc(convolved, 1)
                    assert own.n == qkv_steps + 2

            qkv_turn(0, first=True)
            with dve.Fori(1, 3 * KT // 2) as i:
                qkv_turn(i)
            for q in range(8):
                g, half = q // 2, q % 2
                dve.wait_ge(states_turned, q + 1)
                rows = A_OUT if g == 0 else G_OUT
                dst = state_rows_a if g == 0 else state_rows_g
                at = (max(g - 1, 0) * KT + 4 * half) * P
                dve.tensor_copy(dst[:, at:at + 512], ps[0:rows, 0, 3, :]).then_inc(states_kept, 1)


def memory_kv(nc, k, io, memn, kT, v_rows):
    with ExitStack() as ctx:
        def sem(name):
            return nc.alloc_semaphore(name)

        w = ctx.enter_context(nc.sbuf_tensor("w_kv", [P, 4, KT, P], F32))
        vT = ctx.enter_context(nc.sbuf_tensor("vT", [P, KT, M], F32))
        k_rows = ctx.enter_context(nc.sbuf_tensor("k_rows", [P, MT, D], F32))
        ps = ctx.enter_context(nc.psum_tensor("kv_ps", [P, 4, 512], F32))
        landed = [sem(f"kv_landed{s}") for s in range(4)]
        product_done, kept, turned, rows_kept, out_done = (sem("kv_" + n) for n in ("product", "kept", "turned", "rows", "out"))
        block = ctx.enter_context(nc.Block())
        tiles = 2 * KT

        @block.sync
        def _(sp):
            for t in range(tiles):
                if t >= 4:
                    sp.wait_ge(product_done, t - 3)
                sp.dma_start(w[:, t % 4, :, :], io["w_mem_kv"][:, t * P:(t + 1) * P].rearrange("(k p) c -> p k c", p=P)).then_inc(landed[t % 4], 16)
            sp.wait_ge(rows_kept, KT)
            sp.dma_start(io["out_mem_k"].rearrange("(t p) c -> p t c", p=P), k_rows[:, :, :]).then_inc(out_done, 16)
            sp.wait_ge(rows_kept, tiles)
            sp.dma_start(io["out_mem_v"].rearrange("(t p) c -> p t c", p=P), v_rows[:, :, :]).then_inc(out_done, 16)
            sp.wait_ge(out_done, 32)

        @block.tensor
        def _(pe):
            def turn(t):
                pe.wait_ge(kept, t + 1)
                if t >= 2:
                    pe.wait_ge(rows_kept, t - 1)
                src = (kT if t < KT else vT)[:, t % KT, :]
                for m in range(MT):
                    last = pe.transpose(ps[:, 2 + t % 2, m * P:(m + 1) * P], src[:, m * P:(m + 1) * P], k["ident"][:, :])
                last.then_inc(turned, 1)

            for t in range(tiles):
                pe.wait_ge(landed[t % 4], 16 * (t // 4 + 1))
                if t >= 2:
                    pe.wait_ge(kept, t - 1)
                for kk in range(KT):
                    last = pe.matmul(ps[:, t % 2, 0:M], w[:, t % 4, kk, :], memn[:, kk, :],
                                     start=(kk == 0), stop=(kk == KT - 1))
                last.then_inc(product_done, 1)
                if t:
                    turn(t - 1)
            turn(tiles - 1)

        @block.scalar
        def _(act):
            for t in range(tiles):
                act.wait_ge(product_done, t + 1)
                act.copy((kT if t < KT else vT)[:, t % KT, :], ps[:, t % 2, 0:M]).then_inc(kept, 1)

        @block.vector
        def _(dve):
            for t in range(tiles):
                dve.wait_ge(turned, t + 1)
                dst = (k_rows if t < KT else v_rows)[:, :, (t % KT) * P:(t % KT + 1) * P]
                dve.tensor_copy(dst, ps[:, 2 + t % 2, 0:M].rearrange("p (m c) -> p m c", c=P)).then_inc(rows_kept, 1)


SCALE = (D // MH) ** -0.5


def load_cache(sp, io, cache, cache_in, name, b):
    sp.dma_start(cache[:, b, :, :], io[name][b].rearrange("(t p) h d -> p t (h d)", p=P)).then_inc(cache_in[b], 16)


def attend_prompt(nc, k, io, tmp, kT, v_rows, cache, cache_in):
    tiles = TP // P
    with ExitStack() as ctx:
        def sb(name, shape, dt=F32):
            return ctx.enter_context(nc.sbuf_tensor(name, shape, dt))

        def sem(name):
            return nc.alloc_semaphore("ap_" + name)

        q = sb("ap_q", [P, 2, KT, P])
        probs = sb("ap_probs", [P, 2, MH, M])
        top, bias, total, inv = (sb("ap_" + n, [P, 2, MH]) for n in ("top", "bias", "total", "inv"))
        pT = sb("ap_pT", [P, 2, MH * MT, P])
        o = sb("ap_o", [P, 2, KT, P])
        ps_s = ctx.enter_context(nc.psum_tensor("ap_s", [P, MH, M], F32))
        ps_t = ctx.enter_context(nc.psum_tensor("ap_t", [P, MH * MT, P], F32))
        ps_o = ctx.enter_context(nc.psum_tensor("ap_o_ps", [P, KT, P], F32))
        landed = [sem("landed0"), sem("landed1")]
        stored = [sem("stored0"), sem("stored1")]
        scored, topped, biased, raised, own, normed, turned, kept, summed, out_kept = (
            sem(n) for n in ("scored", "topped", "biased", "raised", "own", "normed", "turned", "kept", "summed", "out_kept"))
        block = ctx.enter_context(nc.Block())

        @block.sync
        def _(sp):
            def load(t, s, first=False):
                if not first:
                    sp.wait_ge(scored, t - 1)
                sp.dma_start(q[:, s, :, :], tmp["mq"][:, :, ds(t * P, P)]).then_inc(landed[s], 16)

            for s in range(2):
                load(s, s, first=True)
            for b in range(NB):
                load_cache(sp, io, cache, cache_in, "cache_mem_k", b)
            with sp.Fori(1, tiles // 2) as i:
                for s in range(2):
                    load(2 * i + s, s)

        @block.gpsimd
        def _(pool):
            with pool.Fori(0, tiles // 2) as i:
                for s in range(2):
                    pool.wait_ge(out_kept, 2 * i + s + 1)
                    pool.dma_start(tmp["ym"][:, :, ds((2 * i + s) * P, P)], o[:, s, :, :]).then_inc(stored[s], 16)
            for s in range(2):
                pool.wait_ge(stored[s], 16 * (tiles // 2))

        @block.tensor
        def _(pe):
            def scores(i, s, first=False):
                t = 2 * i + s
                pe.wait_ge(landed[s], 16 * i + 16)
                if not first:
                    pe.wait_ge(raised, t)
                for h in range(MH):
                    for c in range(2):
                        last = pe.matmul(ps_s[:, h, :], q[:, s, 2 * h + c, :], kT[:, 2 * h + c, :],
                                         start=(c == 0), stop=(c == 1))
                last.then_inc(scored, 1)

            def values(i, s):
                t = 2 * i + s
                pe.wait_ge(normed, t + 1)
                for b in range(MH * MT):
                    last = pe.transpose(ps_t[:, b, :], probs[:, s, b // MT, (b % MT) * P:(b % MT + 1) * P], k["ident"][:, :])
                last.then_inc(turned, 1)
                pe.wait_ge(kept, t + 1)
                for c in range(KT):
                    for m in range(MT):
                        last = pe.matmul(ps_o[:, c, :], v_rows[:, m, c * P:(c + 1) * P], pT[:, s, (c // 2) * MT + m, :],
                                         start=(m == 0), stop=(m == MT - 1))
                last.then_inc(summed, 1)

            scores(0, 0, first=True)
            scores(0, 1)
            values(0, 0)
            with pe.Fori(1, tiles // 2) as i:
                scores(i, 0)
                values(i - 1, 1)
                scores(i, 1)
                values(i, 0)
            values(tiles // 2 - 1, 1)

        @block.scalar
        def _(act):
            def keep(t, s, first=False):
                act.wait_ge(turned, t + 1)
                if not first:
                    act.wait_ge(out_kept, t)
                act.copy(pT[:, s, 0:4, :], ps_t[:, 0:4, :])
                act.copy(pT[:, s, 4:8, :], ps_t[:, 4:8, :]).then_inc(kept, 1)

            def turn(i, first=False):
                for s in range(2):
                    t = 2 * i + s
                    act.wait_ge(topped, t + 1)
                    act.mul(bias[:, s, :], top[:, s, :], -SCALE).then_inc(biased, 1)
                    act.wait_ge(biased, t + 1)
                    for h in range(MH):
                        last = act.activation(probs[:, s, h, :], ps_s[:, h, :], ACT.Exp, bias=bias[:, s, h:h + 1],
                                              scale=SCALE, accum_out=total[:, s, h:h + 1])
                    last.then_inc(raised, 1)
                    if not (first and s == 0):
                        keep(t - 1, 1 - s, first=first)

            turn(0, first=True)
            with act.Fori(1, tiles // 2) as i:
                turn(i)
            keep(tiles - 1, 1)

        @block.vector
        def _(dve):
            def norm(t, s):
                dve.wait_ge(raised, t + 1)
                dve.reciprocal(inv[:, s, :], total[:, s, :]).then_inc(own, 1)
                dve.wait_ge(own, t + 1)
                for h in range(MH):
                    last = dve.tensor_scalar(probs[:, s, h, :], probs[:, s, h, :], inv[:, s, h:h + 1], None, ALU.mult)
                last.then_inc(normed, 1)

            def outputs(i, t, s, first=False):
                dve.wait_ge(summed, t + 1)
                if not first:
                    dve.wait_ge(stored[s], 16 * i)
                dve.tensor_copy(o[:, s, :, :], ps_o[:, :, :]).then_inc(out_kept, 1)

            def turn(i, kind=None):
                for s in range(2):
                    t = 2 * i + s
                    dve.wait_ge(scored, t + 1)
                    dve.reduce_max(top[:, s, :], ps_s[:, :, :], X).then_inc(topped, 1)
                    norm(t, s)
                    if s == 1:
                        outputs(i, t - 1, 0, first=(kind == "first"))
                    elif kind != "first":
                        outputs(i - 1, t - 1, 1, first=(kind == "second"))

            turn(0, "first")
            turn(1, "second")
            with dve.Fori(2, tiles // 2) as i:
                turn(i)
            outputs(tiles // 2 - 1, tiles - 1, 1)


def attend_samples(nc, k, io, tmp, cache, cache_in):
    R = MH * TS
    with ExitStack() as ctx:
        def sb(name, shape, dt=F32):
            return ctx.enter_context(nc.sbuf_tensor(name, shape, dt))

        def sem(name):
            return nc.alloc_semaphore("as_" + name)

        q = sb("as_q", [P, KT, NS])
        qpad = sb("as_qpad", [P, NB, KT, P])
        kT = sb("as_kT", [P, 2, KT, M])
        probs = sb("as_probs", [P, M])
        top, bias, total, inv = (sb("as_" + n, [P, 1]) for n in ("top", "bias", "total", "inv"))
        pT = sb("as_pT", [P, MT, P])
        o = sb("as_o", [P, KT, NS])
        ps_t = ctx.enter_context(nc.psum_tensor("as_t", [P, 4, 4, P], F32))
        ps_s = ctx.enter_context(nc.psum_tensor("as_s", [P, 512], F32))
        ps_o = ctx.enter_context(nc.psum_tensor("as_o_ps", [P, KT, NS], F32))
        q_in, zeroed, padded, turned, kept, kept_act, scored, summed, out_kept, stored = (
            sem(n) for n in ("q_in", "zeroed", "padded", "turned", "kept", "kept_act", "scored", "summed", "out_kept", "stored"))
        soft = sem("soft")
        block = ctx.enter_context(nc.Block())

        @block.sync
        def _(sp):
            sp.dma_start(q[:, :, :], tmp["mq"][:, :, TP:N]).then_inc(q_in, 16)
            for b in range(NB):
                sp.wait_ge(turned, 4 * (b + 1))
                load_cache(sp, io, cache, cache_in, "cache_mem_v", b)
            sp.wait_ge(out_kept, 1)
            sp.dma_start(tmp["ym"][:, :, TP:N], o[:, :, :]).then_inc(stored, 16)
            sp.wait_ge(stored, 16)

        @block.vector
        def _(dve):
            dve.memset(qpad[:, :, :, :], 0.0).then_inc(zeroed, 1)
            dve.wait_ge(zeroed, 1)
            dve.wait_ge(q_in, 16)
            for b in range(NB):
                for h in range(MH):
                    row = b * R + h * TS
                    last = dve.tensor_copy(qpad[:, b, 2 * h:2 * h + 2, row:row + TS], q[:, 2 * h:2 * h + 2, b * TS:(b + 1) * TS])
                last.then_inc(padded, 1)
            for g in range(1, 4 * NB, 2):
                dve.wait_ge(turned, g + 1)
                if g >= 8:
                    dve.wait_ge(scored, g // 4 - 1)
                dve.tensor_copy(kT[:, (g // 4) % 2, 4 * (g % 2):4 * (g % 2) + 4, (g // 2 % 2) * P:(g // 2 % 2 + 1) * P],
                                ps_t[:, g % 4, :, :]).then_inc(kept, 1)
            dve.wait_ge(scored, NB)
            dve.reduce_max(top[:, :], ps_s[:, 0:M], X).then_inc(soft, 1)
            dve.wait_ge(soft, 3)
            dve.reciprocal(inv[:, :], total[:, :]).then_inc(soft, 1)
            dve.wait_ge(soft, 4)
            dve.tensor_scalar(probs[:, :], probs[:, :], inv[:, 0:1], None, ALU.mult).then_inc(soft, 1)
            dve.wait_ge(turned, 4 * NB + 1)
            dve.tensor_copy(pT[:, :, :], ps_t[:, 0, 0:MT, :]).then_inc(soft, 1)
            dve.wait_ge(summed, 1)
            dve.tensor_copy(o[:, :, :], ps_o[:, :, :]).then_inc(out_kept, 1)

        @block.scalar
        def _(act):
            for g in range(0, 4 * NB, 2):
                act.wait_ge(turned, g + 1)
                if g >= 8:
                    act.wait_ge(scored, g // 4 - 1)
                act.copy(kT[:, (g // 4) % 2, 4 * (g % 2):4 * (g % 2) + 4, (g // 2 % 2) * P:(g // 2 % 2 + 1) * P],
                         ps_t[:, g % 4, :, :]).then_inc(kept_act, 1)
            act.wait_ge(soft, 1)
            act.mul(bias[:, :], top[:, :], -SCALE).then_inc(soft, 1)
            act.wait_ge(soft, 2)
            act.activation(probs[:, :], ps_s[:, 0:M], ACT.Exp, bias=bias[:, 0:1], scale=SCALE,
                           accum_out=total[:, 0:1]).then_inc(soft, 1)

        @block.tensor
        def _(pe):
            def turn(b):
                pe.wait_ge(cache_in[b], 16)
                for g in range(4 * b, 4 * b + 4):
                    if g >= 4:
                        pe.wait_ge(kept if g % 2 else kept_act, (g - 4) // 2 + 1)
                    for c in range(4):
                        at = (4 * (g % 2) + c) * P
                        last = pe.transpose(ps_t[:, g % 4, c, :], cache[:, b, g // 2 % 2, at:at + P], k["ident"][:, :])
                    last.then_inc(turned, 1)

            def scores(b):
                pe.wait_ge(padded, b + 1)
                pe.wait_ge(kept, 2 * b + 2)
                pe.wait_ge(kept_act, 2 * b + 2)
                for c in range(KT):
                    last = pe.matmul(ps_s[:, 0:M], qpad[:, b, c, :], kT[:, b % 2, c, :],
                                     start=(b == 0 and c == 0), stop=(b == NB - 1 and c == KT - 1))
                last.then_inc(scored, 1)

            turn(0)
            for b in range(NB):
                if b + 1 < NB:
                    turn(b + 1)
                scores(b)
            pe.wait_ge(soft, 5)
            for m in range(MT):
                last = pe.transpose(ps_t[:, 0, m, :], probs[:, m * P:(m + 1) * P], k["ident"][:, :])
            last.then_inc(turned, 1)
            pe.wait_ge(soft, 6)
            for b in range(NB):
                pe.wait_ge(cache_in[b], 32)
                for c in range(KT):
                    row = b * R + (c // 2) * TS
                    for m in range(MT):
                        last = pe.matmul(ps_o[:, c, b * TS:(b + 1) * TS], cache[:, b, m, c * P:(c + 1) * P],
                                         pT[:, m, row:row + TS], start=(m == 0), stop=(m == MT - 1))
            last.then_inc(summed, 1)


HG = H // 2
LEVELS = (1, 2, 4, 8, 16, 32, 64)


def over_heads(mask, heads=HG):
    return mask.unsqueeze(1).broadcast_to([mask.shape[0], heads, mask.shape[1]])


def over_columns(values, columns=P):
    return values.unsqueeze(2).broadcast_to([values.shape[0], values.shape[1], columns])


def decay_sums(nc, k):
    with ExitStack() as ctx:
        def sem(name):
            return nc.alloc_semaphore("sums_" + name)

        ps = ctx.enter_context(nc.psum_tensor("sums_ps", [P, 3, NT * H], F32))
        summed, masked, done = sem("summed"), sem("masked"), sem("done")
        block = ctx.enter_context(nc.Block())

        @block.tensor
        def _(pe):
            for n, mask in enumerate(("upto", "after", "ones")):
                last = pe.matmul(ps[:, n, :], k[mask][:, :], k["glog"][:, :, :], start=True, stop=True)
            last.then_inc(summed, 1)

        @block.scalar
        def _(act):
            act.wait_ge(summed, 1)
            act.activation(k["decays"][:, :, :, :], ps[:, :, :], ACT.Exp).then_inc(done, 1)

        @block.vector
        def _(dve):
            dve.wait_ge(done, 1)
            dve.tensor_tensor(k["beta_decay"][:, :, :], k["beta"][:, :, :], k["decays"][:, 0, :, :], ALU.mult)

        @block.gpsimd
        def _(pool):
            for n, s in enumerate(LEVELS):
                m = k["level"][:, n, :].rearrange("p (c e j) -> p c e j", e=2, j=s)
                pool.memset(k["level"][:, n, :], 0.0).then_inc(masked, 1)
                pool.wait_ge(masked, 3 * n + 1)
                lower = m[:, :, 0, :]
                pool.affine_select(out=lower, in_=k["ones"][:, 0:P // 2].rearrange("p (c j) -> p c j", j=s),
                                   compare_op=ALU.is_ge, fill=0.0, base=-s, pattern=[[-2 * s, P // (2 * s)], [0, s]],
                                   channel_multiplier=1).then_inc(masked, 1)
                pool.wait_ge(masked, 3 * n + 2)
                pool.affine_select(out=lower, in_=lower, compare_op=ALU.is_ge, fill=0.0, base=2 * s - 1,
                                   pattern=[[2 * s, P // (2 * s)], [0, s]], channel_multiplier=-1).then_inc(masked, 1)


def delta_prompt(nc, k, io, tmp, S_seq, S_seq_in):
    chunks = TP // P
    NL = len(LEVELS)
    with ExitStack() as ctx:
        def sb(name, dt=F32):
            return [ctx.enter_context(nc.sbuf_tensor(f"dp_{name}{g}", [P, HG, P], dt)) for g in range(2)]

        def sem(name):
            return nc.alloc_semaphore("dp_" + name)

        qkv = ctx.enter_context(nc.sbuf_tensor("dp_qkv", [P, 2, 3, H, P], F32))
        z = ctx.enter_context(nc.sbuf_tensor("dp_z", [P, 2, H, P], F32))
        S = ctx.enter_context(nc.sbuf_tensor("dp_S", [P, H, P], F32))
        y = ctx.enter_context(nc.sbuf_tensor("dp_y", [P, 2, HG, P], F32))
        sq_q, sq_k, root_q, root_k = (sb(n) for n in ("sq_q", "sq_k", "root_q", "root_k"))
        g_upto, decay, decayT, weight, weightT = (sb(n) for n in ("g_upto", "decay", "decayT", "weight", "weightT"))
        L, attnT, inv, invT, R = (sb(n) for n in ("L", "attnT", "inv", "invT", "R"))
        Lm = [ctx.enter_context(nc.sbuf_tensor(f"dp_Lm{g}", [P, NL, HG, P], F32)) for g in range(2)]
        k_in, v_in, k_out, wT, v_new, o_state, o, o_sq = (
            sb(n) for n in ("k_in", "v_in", "k_out", "wT", "v_new", "o_state", "o", "o_sq"))
        o_ss, o_root, o_r = ([ctx.enter_context(nc.sbuf_tensor(f"dp_{n}{g}", [P, HG], F32)) for g in range(2)]
                             for n in ("o_ss", "o_root", "o_r"))
        banks = ctx.enter_context(nc.psum_tensor("dp_ps", [P, 2, 4, HG, P], F32))
        landed = [sem("landed0"), sem("landed1")]
        stored = [sem("stored0"), sem("stored1")]
        names = ("squared q_summed k_summed q_rooted k_rooted q_ready k_ready g_ready q_inverted k_inverted diffed raised weighted gram attn_done L_ready "
                 "masked turned1 inv_ready r_done r_kept grown krow_done krow_kept vrow_done vrow_kept "
                 "w_done w_kept v_done v_kept state_done intra_done grow_done S_ready o_part o_ready o_squared "
                 "o_rooted o_inv o_normed o_turned y_ready zeroed S_out S_part").split()
        m = {n: sem(n) for n in names}
        block = ctx.enter_context(nc.Block())

        def q_of(g, s):
            return qkv[:, s, 0, g * HG:(g + 1) * HG, :]

        def k_of(g, s):
            return qkv[:, s, 1, g * HG:(g + 1) * HG, :]

        def v_of(g, s):
            return qkv[:, s, 2, g * HG:(g + 1) * HG, :]

        def S_of(g):
            return S[:, g * HG:(g + 1) * HG, :]

        def blocks_of(x, lv, odd):
            return x[:, :, :].rearrange("p h (c e j) -> p h c e j", e=2, j=LEVELS[lv])[:, :, :, odd, :]

        def packed(bank, lv):
            return bank[:, :, 0:P // 2].rearrange("p h (c j) -> p h c j", j=LEVELS[lv])

        def level_at(t, lv, g, per=NL):
            return (t * per + lv) * 2 + g + 1

        @block.sync
        def _(sp):
            def load(i, s):
                t = 2 * i + s
                sp.dma_start(qkv[:, s, :, :, :], tmp["qkv"][:, :, ds(t * P, P)].rearrange("p (a h) n -> p a h n", h=H)).then_inc(landed[s], 16)
                sp.dma_start(z[:, s, :, :], tmp["z"][:, :, ds(t * P, P)]).then_inc(landed[s], 16)

            def store(i, s):
                t = 2 * i + s
                for g in range(2):
                    sp.wait_ge(m["y_ready"], 2 * t + g + 1)
                    sp.dma_start(tmp["yb"][:, g * HG:(g + 1) * HG, ds(t * P, P)], y[:, g, :, :]).then_inc(stored[g], 16)

            for s in range(2):
                load(0, s)
            for b in range(NB):
                sp.dma_start(S_seq[:, b, :, :], io["state_gdn"][b].rearrange("h d e -> d h e")).then_inc(S_seq_in, 16)
            with sp.Fori(0, chunks // 2 - 1) as i:
                for s in range(2):
                    store(i, s)
                    load(i + 1, s)
            for s in range(2):
                store(chunks // 2 - 1, s)
            for g in range(2):
                sp.wait_ge(stored[g], 16 * chunks)
            sp.wait_ge(m["S_ready"], 2 * chunks)
            sp.dma_start(io["out_gdn_p"].rearrange("h d e -> d h e"), S[:, :, :]).then_inc(m["S_out"], 16)
            sp.wait_ge(m["S_out"], 16)

        @block.tensor
        def _(pe):
            def heads(out, lhsT, rhs, start=True, stop=True, fixed=None):
                for h in range(HG):
                    last = pe.matmul(out[:, h], lhsT[:, h], fixed if fixed is not None else rhs[:, h],
                                     start=start, stop=stop)
                return last

            def turn(out, src):
                for h in range(HG):
                    last = pe.transpose(out[:, h, :], src[:, h, :], k["ident"][:, :])
                return last

            def B(g, b):
                return banks[:, g, b, :, :]

            def sum_q(n, g):
                pe.wait_ge(m["squared"], n + 1)
                pe.matmul(B(g, 2), k["ones"][:, :], sq_q[g][:, :, :], start=True, stop=True).then_inc(m["q_summed"], 1)

            def sum_k(n, g):
                pe.wait_ge(m["q_rooted"], n + 1)
                pe.matmul(B(g, 2), k["ones"][:, :], sq_k[g][:, :, :], start=True, stop=True).then_inc(m["k_summed"], 1)

            def differences(n, g):
                pe.wait_ge(m["g_ready"], n + 1)
                pe.wait_ge(m["k_rooted"], n + 1)
                heads(B(g, 2), g_upto[g], None, fixed=k["after"][:, :])
                pe.matmul(B(g, 0), k["after"][:, :], g_upto[g][:, :, :], start=True, stop=True).then_inc(m["diffed"], 1)

            def turn_output(n, g):
                pe.wait_ge(m["o_normed"], n + 1)
                pe.wait_ge(m["S_ready"], n + 1)
                turn(B(g, 3), o[g]).then_inc(m["o_turned"], 1)

            def chunk_turn(i, s, first=False, last=False):
                t = 2 * i + s
                for g in range(2):
                    n = 2 * t + g
                    pe.wait_ge(m["raised"], n + 1)
                    pe.wait_ge(m["k_ready"], n + 1)
                    heads(B(g, 0), k_of(g, s), k_of(g, s)).then_inc(m["gram"], 1)
                    pe.wait_ge(m["q_ready"], n + 1)
                    if not first:
                        pe.wait_ge(m["o_part"], n - 1)
                    heads(B(g, 1), k_of(g, s), q_of(g, s)).then_inc(m["attn_done"], 1)
                if not first:
                    for g in range(2):
                        turn_output(2 * t + g - 2, g)
                for g in range(2):
                    n = 2 * t + g
                    if not first:
                        pe.wait_ge(m["o_ready"], n - 1)
                    pe.wait_ge(m["masked"], level_at(t, 0, g))
                    turn(B(g, 2), Lm[g][:, 0, :, :]).then_inc(m["turned1"], 1)
                for lv in range(1, NL):
                    for g in range(2):
                        n = 2 * t + g
                        pe.wait_ge(m["masked"], level_at(t, lv, g))
                        pe.wait_ge(m["inv_ready"], level_at(t, lv - 1, g))
                        if lv == 1 and not first:
                            pe.wait_ge(m["y_ready"], n - 1)
                        heads(B(g, 3), Lm[g][:, lv, :, :], invT[g]).then_inc(m["r_done"], 1)
                        if lv == 1:
                            turn(B(g, 2), k_of(g, s)).then_inc(m["krow_done"], 1)
                        if lv == 3:
                            pe.wait_ge(m["krow_kept"], n + 1)
                            turn(B(g, 2), v_of(g, s)).then_inc(m["vrow_done"], 1)
                        if lv == 4:
                            pe.wait_ge(m["vrow_kept"], n + 1)
                        if not last:
                            if lv == 4:
                                sum_q(n + 2, g)
                            if lv == 5:
                                sum_k(n + 2, g)
                            if lv == 6:
                                differences(n + 2, g)
                    for g in range(2):
                        pe.wait_ge(m["r_kept"], level_at(t, lv - 1, g, NL - 1))
                        if lv < NL - 1:
                            heads(packed(B(g, 0), lv), R[g], blocks_of(inv[g], lv, 0))
                        heads(packed(B(g, 1), lv), inv[g], blocks_of(R[g], lv, 1)).then_inc(m["grown"], 1)
                for g in range(2):
                    pe.wait_ge(m["inv_ready"], level_at(t, NL - 1, g))
                    heads(B(g, 3), k_in[g], invT[g]).then_inc(m["w_done"], 1)
                for g in range(2):
                    n = 2 * t + g
                    pe.wait_ge(m["w_kept"], n + 1)
                    if not last:
                        pe.wait_ge(m["raised"], n + 3)
                    for h in range(HG):
                        pe.matmul(B(g, 0)[:, h, :], invT[g][:, h, :], v_in[g][:, h, :], start=True, stop=False)
                        done = pe.matmul(B(g, 0)[:, h, :], wT[g][:, h, :], S_of(g)[:, h, :], start=False, stop=True)
                    done.then_inc(m["v_done"], 1)
                    heads(B(g, 1), q_of(g, s), S_of(g)).then_inc(m["state_done"], 1)
                for g in range(2):
                    n = 2 * t + g
                    pe.wait_ge(m["v_kept"], n + 1)
                    heads(B(g, 3), k_out[g], v_new[g]).then_inc(m["grow_done"], 1)
                    heads(B(g, 2), attnT[g], v_new[g]).then_inc(m["intra_done"], 1)

            for step in (sum_q, sum_k, differences):
                for g in range(2):
                    step(g, g)
            pe.wait_ge(m["zeroed"], 1)
            chunk_turn(0, 0, first=True)
            chunk_turn(0, 1)
            with pe.Fori(1, chunks // 2 - 1) as i:
                for s in range(2):
                    chunk_turn(i, s)
            chunk_turn(chunks // 2 - 1, 0)
            chunk_turn(chunks // 2 - 1, 1, last=True)
            for g in range(2):
                turn_output(2 * chunks - 2 + g, g)

        @block.scalar
        def _(act):
            def B(g, b):
                return banks[:, g, b, :, :]

            def square(i, s):
                act.wait_ge(landed[s], 32 * i + 32)
                for g in range(2):
                    act.activation(sq_q[g][:, :, :], q_of(g, s), ACT.Square)
                    act.activation(sq_k[g][:, :, :], k_of(g, s), ACT.Square).then_inc(m["squared"], 1)

            def root(n, g, summed, rooted, out):
                act.wait_ge(m[summed], n + 1)
                act.activation(out[g][:, :, :], B(g, 2), ACT.Sqrt, bias=k["eps"][:, 0:1]).then_inc(m[rooted], 1)

            def raise_decays(n, g):
                act.wait_ge(m["diffed"], n + 1)
                act.activation(decay[g][:, :, :], B(g, 2), ACT.Exp)
                act.activation(decayT[g][:, :, :], B(g, 0), ACT.Exp).then_inc(m["raised"], 1)

            def chunk_turn(i, s, last=False):
                t = 2 * i + s
                for lv in range(1, NL):
                    for g in range(2):
                        act.wait_ge(m["r_done"], level_at(t, lv - 1, g, NL - 1))
                        act.copy(R[g][:, :, :], B(g, 3)).then_inc(m["r_kept"], 1)
                    if not last:
                        if lv == 3:
                            square(i + s, 1 - s)
                        for g in range(2):
                            n = 2 * t + 2 + g
                            if lv == 4:
                                root(n, g, "q_summed", "q_rooted", root_q)
                            if lv == 5:
                                root(n, g, "k_summed", "k_rooted", root_k)
                            if lv == 6:
                                raise_decays(n, g)
                for g in range(2):
                    n = 2 * t + g
                    act.wait_ge(m["w_done"], n + 1)
                    act.mul(wT[g][:, :, :], B(g, 3), -1.0).then_inc(m["w_kept"], 1)
                for g in range(2):
                    n = 2 * t + g
                    act.wait_ge(m["v_done"], n + 1)
                    act.copy(v_new[g][:, :, :], B(g, 0)).then_inc(m["v_kept"], 1)
                for g in range(2):
                    n = 2 * t + g
                    act.wait_ge(m["o_ready"], n + 1)
                    for h in range(HG):
                        done = act.activation(o_sq[g][:, h, :], o[g][:, h, :], ACT.Square, accum_out=o_ss[g][:, h:h + 1])
                    done.then_inc(m["o_squared"], 1)
                for g in range(2):
                    n = 2 * t + g
                    act.wait_ge(m["o_squared"], n + 1)
                    act.activation(o_root[g][:, :], o_ss[g][:, :], ACT.Sqrt, bias=k["eps"][:, 0:1], scale=1.0 / P).then_inc(m["o_rooted"], 1)

            square(0, 0)
            for g in range(2):
                root(g, g, "q_summed", "q_rooted", root_q)
            for g in range(2):
                root(g, g, "k_summed", "k_rooted", root_k)
            for g in range(2):
                raise_decays(g, g)
            with act.Fori(0, chunks // 2 - 1) as i:
                for s in range(2):
                    chunk_turn(i, s)
            chunk_turn(chunks // 2 - 1, 0)
            chunk_turn(chunks // 2 - 1, 1, last=True)

        @block.gpsimd
        def _(pool):
            def weights(t, first=False):
                for g in range(2):
                    n = 2 * t + g
                    beta = k["beta"][:, ds(t, 1), g * HG:(g + 1) * HG].rearrange("p o h -> p (o h)")
                    own = Steps(pool, m["weighted"], 3 * n)
                    if not first:
                        pool.wait_ge(m["inv_ready"], level_at(t - 1, 0, g))
                    own.did(pool.tensor_tensor(weight[g][:, :, :], over_heads(k["after"][:, :]), over_columns(beta), ALU.mult))
                    pool.wait_ge(m["raised"], n + 1)
                    own.wait()
                    own.did(pool.tensor_tensor(weight[g][:, :, :], weight[g][:, :, :], decay[g][:, :, :], ALU.mult))
                    own.did(pool.tensor_tensor(weightT[g][:, :, :], over_heads(k["upto"][:, :]), decayT[g][:, :, :], ALU.mult))

            def chunk_turn(i, s, last=False):
                t = 2 * i + s
                for lv in range(NL):
                    for g in range(2):
                        if lv == 0:
                            pool.wait_ge(m["L_ready"], 2 * t + g + 1)
                        pool.tensor_tensor(Lm[g][:, lv, :, :], L[g][:, :, :], over_heads(k["level"][:, lv, :]), ALU.mult).then_inc(m["masked"], 1)
                if not last:
                    weights(t + 1)

            weights(0, first=True)
            with pool.Fori(0, chunks // 2 - 1) as i:
                for s in range(2):
                    chunk_turn(i, s)
            chunk_turn(chunks // 2 - 1, 0)
            chunk_turn(chunks // 2 - 1, 1, last=True)

        @block.vector
        def _(dve):
            def B(g, b):
                return banks[:, g, b, :, :]

            def of(name, t, g):
                return k[name][:, ds(t, 1), g * HG:(g + 1) * HG].rearrange("p o h -> p (o h)")

            def decays(n, t, g):
                return k["decays"][:, n:n + 1, ds(t, 1), g * HG:(g + 1) * HG].rearrange("p a o h -> p (a o h)")

            def gates(t):
                for g in range(2):
                    dve.tensor_tensor(g_upto[g][:, :, :], over_heads(k["upto"][:, :]), over_columns(of("glog", t, g)), ALU.mult).then_inc(m["g_ready"], 1)

            def norm_q(n, g, s):
                dve.wait_ge(m["q_rooted"], n + 1)
                dve.reciprocal(root_q[g][:, :, :], root_q[g][:, :, :]).then_inc(m["q_inverted"], 1)
                dve.wait_ge(m["q_inverted"], n + 1)
                dve.scalar_tensor_tensor(out=q_of(g, s), in0=q_of(g, s), scalar=float(P) ** -0.5, in1=root_q[g][:, :, :],
                                         op0=ALU.mult, op1=ALU.mult).then_inc(m["q_ready"], 1)

            def norm_k(n, g, s):
                dve.wait_ge(m["k_rooted"], n + 1)
                dve.reciprocal(root_k[g][:, :, :], root_k[g][:, :, :]).then_inc(m["k_inverted"], 1)
                dve.wait_ge(m["k_inverted"], n + 1)
                dve.tensor_tensor(k_of(g, s), k_of(g, s), root_k[g][:, :, :], ALU.mult).then_inc(m["k_ready"], 1)

            def norm_output(n, g):
                dve.wait_ge(m["o_rooted"], n + 1)
                dve.reciprocal(o_r[g][:, :], o_root[g][:, :]).then_inc(m["o_inv"], 1)
                dve.wait_ge(m["o_inv"], n + 1)
                dve.tensor_tensor(o[g][:, :, :], o[g][:, :, :], over_columns(o_r[g][:, :]), ALU.mult).then_inc(m["o_normed"], 1)

            def finish_output(t, g, s, first=False):
                dve.wait_ge(m["o_turned"], 2 * t + g + 1)
                if not first:
                    dve.wait_ge(stored[g], 16 * t)
                dve.scalar_tensor_tensor(out=y[:, g, :, :], in0=B(g, 3), scalar=k["gdn_gain"][:, 0:1],
                                         in1=z[:, s, g * HG:(g + 1) * HG, :], op0=ALU.mult, op1=ALU.mult).then_inc(m["y_ready"], 1)

            def chunk_turn(i, s, kind=None):
                t = 2 * i + s
                first, last = kind == "first", kind == "last"
                for g in range(2):
                    n = 2 * t + g
                    dve.wait_ge(m["gram"], n + 1)
                    dve.wait_ge(m["weighted"], 3 * n + 3)
                    dve.tensor_tensor(L[g][:, :, :], B(g, 0), weight[g][:, :, :], ALU.mult).then_inc(m["L_ready"], 1)
                if not first:
                    for g in range(2):
                        norm_output(2 * t + g - 2, g)
                for g in range(2):
                    n = 2 * t + g
                    dve.wait_ge(m["attn_done"], n + 1)
                    dve.tensor_tensor(attnT[g][:, :, :], B(g, 1), weightT[g][:, :, :], ALU.mult)
                    dve.wait_ge(m["masked"], level_at(t, 0, g))
                    dve.tensor_tensor(inv[g][:, :, :], over_heads(k["ident"][:, :]), Lm[g][:, 0, :, :], ALU.subtract)
                    dve.wait_ge(m["turned1"], n + 1)
                    dve.tensor_tensor(invT[g][:, :, :], over_heads(k["ident"][:, :]), B(g, 2), ALU.subtract).then_inc(m["inv_ready"], 1)
                if not first:
                    for g in range(2):
                        finish_output(t - 1, g, 1 - s, first=(kind == "second"))
                for lv in range(1, NL):
                    for g in range(2):
                        n = 2 * t + g
                        dve.wait_ge(m["grown"], level_at(t, lv - 1, g, NL - 1))
                        if lv < NL - 1:
                            at = blocks_of(inv[g], lv, 0)
                            dve.tensor_tensor(at, at, packed(B(g, 0), lv), ALU.subtract)
                        at = blocks_of(invT[g], lv, 1)
                        dve.tensor_tensor(at, at, packed(B(g, 1), lv), ALU.subtract).then_inc(m["inv_ready"], 1)
                        if lv == 1:
                            dve.wait_ge(m["krow_done"], n + 1)
                            dve.tensor_tensor(k_in[g][:, :, :], B(g, 2), over_columns(of("beta_decay", t, g)), ALU.mult)
                            dve.tensor_tensor(k_out[g][:, :, :], B(g, 2), over_columns(decays(1, t, g)), ALU.mult).then_inc(m["krow_kept"], 1)
                        if lv == 3:
                            dve.wait_ge(m["vrow_done"], n + 1)
                            dve.tensor_tensor(v_in[g][:, :, :], B(g, 2), over_columns(of("beta", t, g)), ALU.mult).then_inc(m["vrow_kept"], 1)
                    if not last:
                        if lv == 2:
                            gates(t + 1)
                        for g in range(2):
                            if lv == 5:
                                norm_q(2 * t + 2 + g, g, 1 - s)
                            if lv == 6:
                                norm_k(2 * t + 2 + g, g, 1 - s)
                for g in range(2):
                    n = 2 * t + g
                    dve.wait_ge(m["state_done"], n + 1)
                    dve.tensor_tensor(o_state[g][:, :, :], B(g, 1), over_columns(decays(0, t, g)), ALU.mult).then_inc(m["o_part"], 1)
                for g in range(2):
                    n = 2 * t + g
                    dve.tensor_tensor(S_of(g), S_of(g), over_columns(decays(2, t, g)), ALU.mult).then_inc(m["S_part"], 1)
                    dve.wait_ge(m["S_part"], n + 1)
                    dve.wait_ge(m["grow_done"], n + 1)
                    dve.tensor_tensor(S_of(g), S_of(g), B(g, 3), ALU.add).then_inc(m["S_ready"], 1)
                    dve.wait_ge(m["o_part"], n + 1)
                    dve.wait_ge(m["intra_done"], n + 1)
                    dve.tensor_tensor(o[g][:, :, :], o_state[g][:, :, :], B(g, 2), ALU.add).then_inc(m["o_ready"], 1)

            dve.memset(S[:, :, :], 0.0).then_inc(m["zeroed"], 1)
            gates(0)
            for step in (norm_q, norm_k):
                for g in range(2):
                    step(g, g, 0)
            chunk_turn(0, 0, "first")
            chunk_turn(0, 1, "second")
            with dve.Fori(1, chunks // 2 - 1) as i:
                for s in range(2):
                    chunk_turn(i, s)
            chunk_turn(chunks // 2 - 1, 0)
            chunk_turn(chunks // 2 - 1, 1, "last")
            for g in range(2):
                norm_output(2 * chunks - 2 + g, g)
            for g in range(2):
                finish_output(chunks - 1, g, 1)


def delta_samples(nc, k, io, tmp, S, S_in):
    levels = [s for s in LEVELS if s < TS]
    last_tile = NT - 1
    with ExitStack() as ctx:
        def sb(name, shape, dt=F32):
            return ctx.enter_context(nc.sbuf_tensor("ds_" + name, shape, dt))

        def sem(name):
            return nc.alloc_semaphore("ds_" + name)

        qkv = sb("qkv", [P, 3, H, NS])
        z = sb("z", [P, H, NS])
        upto, after = sb("upto", [NS, NS]), sb("after", [NS, NS])
        sq, root, rinv = sb("sq", [P, 2, H, NS]), sb("root", [P, 2, H, NS]), sb("rinv", [P, 2, H, NS])
        glog, beta = k["glog"][0:NS, last_tile, :], k["beta"][0:NS, last_tile, :]
        g_upto, g_seq = sb("g_upto", [NS, H, NS]), sb("g_seq", [NS, NB, H])
        decay, decayT = sb("decay", [NS, H, NS]), sb("decayT", [NS, H, NS])
        weight, weightT = sb("weight", [NS, H, NS]), sb("weightT", [NS, H, NS])
        sums, beta_decay = sb("sums", [NS, 2, H]), sb("beta_decay", [NS, H])
        keep = sb("keep", [P, NB, H])
        L, Lm, attnT = sb("L", [NS, H, NS]), sb("Lm", [NS, len(levels), H, NS]), sb("attnT", [NS, H, NS])
        inv, invT, R = sb("inv", [NS, H, NS]), sb("invT", [NS, H, NS]), sb("R", [NS, H, NS])
        k_in, k_out, v_in, v_new = (sb(n, [NS, H, P]) for n in ("k_in", "k_out", "v_in", "v_new"))
        seq_mask = sb("seq_mask", [P, NB, NS])
        wq = sb("wq", [P, H, NB, 2, NS])
        o_raw = sb("o_raw", [NS, H, P])
        v_seq = sb("v_seq", [NS, 2, NB, P])
        o_state, o, o_sq = (sb(n, [NS, H, P]) for n in ("o_state", "o", "o_sq"))
        o_ss, o_root, o_r = (sb(n, [NS, H]) for n in ("o_ss", "o_root", "o_r"))
        y = sb("y", [P, H, NS])
        ps = ctx.enter_context(nc.psum_tensor("ds_ps", [P, 8, 512], F32))
        landed, made, did_pe, did_act, stored, S_step = (
            sem(n) for n in ("landed", "dve_step", "pe_step", "act_step", "stored", "S_step"))
        v_masked, grow_done = sem("v_masked"), sem("grow_done")
        mask_zeroed, mask_made, q_padded, o_copied, S_scaled = (
            sem(n) for n in ("mask_zeroed", "mask_made", "q_padded", "o_copied", "S_scaled"))
        block = ctx.enter_context(nc.Block())

        def cols(b, rows=P, n=NS):
            return ps[0:rows, b, 0:H * n].rearrange("p (h n) -> p h n", n=n)

        def wide(b, rows=NS):
            return ps[0:rows, b:b + 2, :].rearrange("p b (h n) -> p (b h) n", n=P)

        mask4 = k["same_seq"][:, :].rearrange("p (b t) -> p b t", t=TS)[:, :, 0]

        @block.sync
        def _(sp):
            sp.dma_start(qkv[:, :, :, :], tmp["qkv"][:, :, TP:N].rearrange("p (a h) n -> p a h n", h=H)).then_inc(landed, 16)
            sp.dma_start(z[:, :, :], tmp["z"][:, :, TP:N]).then_inc(landed, 16)
            sp.wait_ge(made, 21)
            sp.dma_start(tmp["yb"][:, :, TP:N], y[:, :, :]).then_inc(stored, 16)
            for h in range(H):
                sp.wait_ge(S_step, 2 * h + 2)
                sp.dma_start(io["out_gdn_s"][:, h].rearrange("b d e -> d b e"), S[:, :, h, :]).then_inc(stored, 16)
            sp.wait_ge(stored, 16 * (H + 1))

        @block.gpsimd
        def _(pool):
            pool.memset(seq_mask[:, :, :], 0.0).then_inc(mask_zeroed, 1)
            pool.wait_ge(mask_zeroed, 1)
            for b in range(NB):
                pool.memset(seq_mask[:, b, b * TS:(b + 1) * TS], 1.0).then_inc(mask_made, 1)
            pool.wait_ge(mask_made, NB)
            pool.wait_ge(made, 6)
            pool.tensor_tensor(wq[:, :, :, 1, :], qkv[:, 0, :, :].unsqueeze(2).broadcast_to([P, H, NB, NS]),
                               seq_mask[:, :, :].unsqueeze(1).broadcast_to([P, H, NB, NS]), ALU.mult).then_inc(q_padded, 1)
            pool.wait_ge(did_act, 3)
            pool.wait_ge(did_pe, 9)
            for h in range(H):
                pool.tensor_tensor(S[:, :, h, :], S[:, :, h, :], over_columns(keep[:, :, h]), ALU.mult).then_inc(S_scaled, 1)

        @block.vector
        def _(dve):
            own = Steps(dve, made)
            own.did(dve.tensor_tensor(upto[:, :], k["upto"][0:NS, 0:NS], k["same_seq"][:, :], ALU.mult))
            own.did(dve.tensor_tensor(after[:, :], k["after"][0:NS, 0:NS], k["same_seq"][:, :], ALU.mult))
            own.wait()
            own.did(dve.tensor_tensor(g_upto[:, :, :], over_heads(upto[:, :], H), over_columns(glog, NS), ALU.mult))
            own.did(dve.tensor_tensor(g_seq[:, :, :], over_heads(glog, NB), over_columns(mask4, H), ALU.mult))
            dve.tensor_tensor(weight[:, :, :], over_heads(after[:, :], H), over_columns(beta, NS), ALU.mult)
            dve.wait_ge(did_act, 2)
            own.did(dve.reciprocal(rinv[:, :, :, :], root[:, :, :, :]))
            own.wait()
            dve.scalar_tensor_tensor(out=qkv[:, 0, :, :], in0=qkv[:, 0, :, :], scalar=float(P) ** -0.5,
                                     in1=rinv[:, 0, :, :], op0=ALU.mult, op1=ALU.mult)
            own.did(dve.tensor_tensor(qkv[:, 1, :, :], qkv[:, 1, :, :], rinv[:, 1, :, :], ALU.mult))
            dve.wait_ge(did_act, 3)
            dve.tensor_tensor(weight[:, :, :], weight[:, :, :], decay[:, :, :], ALU.mult)
            dve.tensor_tensor(weightT[:, :, :], over_heads(upto[:, :], H), decayT[:, :, :], ALU.mult)
            own.did(dve.tensor_tensor(beta_decay[:, :], beta, sums[:, 0, :], ALU.mult))
            own.wait()
            dve.wait_ge(did_pe, 3)
            dve.tensor_tensor(attnT[:, :, :], cols(5, NS), weightT[:, :, :], ALU.mult)
            own.did(dve.tensor_tensor(L[:, :, :], cols(4, NS), weight[:, :, :], ALU.mult))
            own.wait()
            for n in range(len(levels)):
                last = dve.tensor_tensor(Lm[:, n, :, :], L[:, :, :], over_heads(k["level"][0:NS, n, 0:NS], H), ALU.mult)
            own.did(last)
            own.wait()
            dve.tensor_tensor(inv[:, :, :], over_heads(k["ident"][0:NS, 0:NS], H), Lm[:, 0, :, :], ALU.subtract)
            dve.wait_ge(did_pe, 4)
            own.did(dve.tensor_tensor(invT[:, :, :], over_heads(k["ident"][0:NS, 0:NS], H), cols(6, NS), ALU.subtract))
            own.wait()
            dve.wait_ge(did_pe, 5)
            own.did(dve.tensor_copy(R[:, :, :], cols(7, NS)))
            dve.wait_ge(did_pe, 6)
            own.did(dve.tensor_tensor(invT[:, :, :], invT[:, :, :], cols(6, NS), ALU.subtract))
            dve.wait_ge(did_pe, 7)
            dve.tensor_tensor(k_in[:, :, :], wide(0), over_columns(beta_decay[:, :]), ALU.mult)
            dve.tensor_tensor(k_out[:, :, :], wide(0), over_columns(sums[:, 1, :]), ALU.mult)
            own.did(dve.tensor_tensor(v_in[:, :, :], wide(2), over_columns(beta), ALU.mult))
            dve.wait_ge(did_pe, 8)
            dve.wait_ge(mask_made, NB)
            own.did(dve.tensor_tensor(wq[:, :, :, 0, :], cols(4).unsqueeze(2).broadcast_to([P, H, NB, NS]),
                                      seq_mask[:, :, :].unsqueeze(1).broadcast_to([P, H, NB, NS]), ALU.mult))
            dve.wait_ge(did_pe, 9)
            own.did(dve.tensor_copy(v_new[:, :, :], wide(0)))
            own.wait()
            own.did(dve.tensor_tensor(v_new[:, :, :], v_new[:, :, :], wide(4), ALU.subtract))
            dve.wait_ge(o_copied, 1)
            own.did(dve.tensor_tensor(o_state[:, :, :], o_raw[:, :, :], over_columns(sums[:, 0, :]), ALU.mult))
            own.wait()
            dve.wait_ge(did_pe, 10)
            own.did(dve.tensor_tensor(o[:, :, :], wide(2), o_state[:, :, :], ALU.add))
            dve.wait_ge(did_act, 5)
            own.did(dve.reciprocal(o_r[:, :], o_root[:, :]))
            own.wait()
            own.did(dve.tensor_tensor(o[:, :, :], o[:, :, :], over_columns(o_r[:, :]), ALU.mult))
            dve.wait_ge(did_pe, 11)
            own.did(dve.scalar_tensor_tensor(out=y[:, :, :], in0=cols(6), scalar=k["gdn_gain"][:, 0:1], in1=z[:, :, :],
                                             op0=ALU.mult, op1=ALU.mult))
            for h in range(H):
                if h >= 2:
                    dve.wait_ge(grow_done, h - 1)
                dve.tensor_tensor(v_seq[:, h % 2, :, :], over_heads(v_new[:, h, :], NB), over_columns(mask4), ALU.mult).then_inc(v_masked, 1)
                dve.wait_ge(S_scaled, h + 1)
                dve.wait_ge(grow_done, h + 1)
                for half in range(2):
                    bs = slice(half * NB // 2, (half + 1) * NB // 2)
                    src = ps[:, 2 * (h % 2) + half, :].rearrange("p (b e) -> p b e", e=P)
                    dve.tensor_tensor(S[:, bs, h, :], S[:, bs, h, :], src, ALU.add).then_inc(S_step, 1)

        @block.scalar
        def _(act):
            act.wait_ge(landed, 32)
            act.activation(sq[:, :, :, :], qkv[:, 0:2, :, :], ACT.Square).then_inc(did_act, 1)
            act.wait_ge(did_pe, 1)
            act.activation(root[:, :, :, :], ps[:, 0, :].rearrange("p (a h n) -> p a h n", a=2, h=H), ACT.Sqrt, bias=k["eps"][:, 0:1]).then_inc(did_act, 1)
            act.wait_ge(did_pe, 2)
            act.activation(decay[:, :, :], cols(1, NS), ACT.Exp)
            act.activation(decayT[:, :, :], cols(2, NS), ACT.Exp)
            act.activation(sums[:, :, :], ps[0:NS, 3, 0:2 * H].rearrange("p (a h) -> p a h", h=H), ACT.Exp)
            act.activation(keep[:, :, :], ps[:, 6, 0:NB * H].rearrange("p (b h) -> p b h", h=H), ACT.Exp).then_inc(did_act, 1)
            act.wait_ge(did_pe, 9)
            act.copy(o_raw[:, :, :], ps[NS:2 * NS, 4:6, :].rearrange("p b (h n) -> p (b h) n", n=P)).then_inc(o_copied, 1)
            act.wait_ge(made, 18)
            for h in range(H):
                last = act.activation(o_sq[:, h, :], o[:, h, :], ACT.Square, accum_out=o_ss[:, h:h + 1])
            last.then_inc(did_act, 1)
            act.wait_ge(did_act, 4)
            act.activation(o_root[:, :], o_ss[:, :], ACT.Sqrt, bias=k["eps"][0:NS, 0:1], scale=1.0 / P).then_inc(did_act, 1)

        @block.tensor
        def _(pe):
            own = Steps(pe, did_pe)

            def heads(out, lhsT, rhs):
                for h in range(H):
                    last = pe.matmul(out[:, h, :], lhsT[:, h, :], rhs[:, h, :], start=True, stop=True)
                return last

            def turn(out, src, n):
                for h in range(H):
                    last = pe.transpose(out[:, h, :], src[:, h, :], k["ident"][0:n, 0:n])
                return last

            pe.wait_ge(did_act, 1)
            own.did(pe.matmul(ps[:, 0, :], k["ones"][:, :], sq[:, :, :, :], start=True, stop=True))
            pe.wait_ge(made, 4)
            for h in range(H):
                pe.matmul(cols(1, NS)[:, h, :], g_upto[:, h, :], after[:, :], start=True, stop=True)
            pe.matmul(ps[0:NS, 2, 0:H * NS], after[:, :], g_upto[:, :, :], start=True, stop=True)
            pe.matmul(ps[0:NS, 3, 0:H], upto[:, :], glog, start=True, stop=True)
            pe.matmul(ps[0:NS, 3, H:2 * H], after[:, :], glog, start=True, stop=True)
            own.did(pe.matmul(ps[:, 6, 0:NB * H], k["ones"][0:NS, :], g_seq[:, :, :], start=True, stop=True))
            pe.wait_ge(made, 6)
            heads(cols(4, NS), qkv[:, 1, :, :], qkv[:, 1, :, :])
            own.did(heads(cols(5, NS), qkv[:, 1, :, :], qkv[:, 0, :, :]))
            pe.wait_ge(made, 9)
            pe.wait_ge(did_act, 3)
            own.did(turn(cols(6, NS), Lm[:, 0, :, :], NS))
            pe.wait_ge(made, 10)
            own.did(heads(cols(7, NS), Lm[:, 1, :, :], invT))
            pe.wait_ge(made, 11)
            own.did(heads(cols(6, NS), inv, R))
            turn(wide(0), qkv[:, 1, :, :], P)
            own.did(turn(wide(2), qkv[:, 2, :, :], P))
            pe.wait_ge(made, 13)
            own.did(heads(cols(4), k_in, invT))
            pe.wait_ge(made, 14)
            pe.wait_ge(S_in, 16 * NB)
            pe.wait_ge(q_padded, 1)
            heads(wide(0), invT, v_in)
            for h in range(H):
                for b in range(NB):
                    last = pe.matmul(ps[0:2 * NS, 4 + h // 4, (h % 4) * P:(h % 4 + 1) * P],
                                     wq[:, h, b, :, :].rearrange("p a n -> p (a n)"), S[:, b, h, :],
                                     start=(b == 0), stop=(b == NB - 1))
            own.did(last)
            pe.wait_ge(made, 16)
            own.did(heads(wide(2), attnT, v_new))
            pe.wait_ge(made, 20)
            own.did(turn(cols(6), o, NS))
            for h in range(H):
                pe.wait_ge(v_masked, h + 1)
                if h >= 2:
                    pe.wait_ge(S_step, 2 * (h - 2) + 2)
                for half in range(2):
                    bs = slice(half * NB // 2, (half + 1) * NB // 2)
                    last = pe.matmul(ps[:, 2 * (h % 2) + half, :], k_out[:, h, :], v_seq[:, h % 2, bs, :], start=True, stop=True)
                last.then_inc(grow_done, 1)


def merge_branches(nc, k, io, tmp, x2T, high, low, wt):
    stages = (("ya", "w_br_conv"), ("yb", "w_br_gdn"), ("ym", "w_br_mem"), (None, "w_out"))
    with ExitStack() as ctx:
        def sb(name, shape, dt=F32):
            return ctx.enter_context(nc.sbuf_tensor("mb_" + name, shape, dt))

        def sem(name):
            return nc.alloc_semaphore("mb_" + name)

        ps = ctx.enter_context(nc.psum_tensor("mb_ps", [P, 2, 4, 512], F32))
        raw = sb("raw", [P, KT, N])
        gate = sb("gate", [P, 2, N])
        part = sb("part", [P, 2, N])
        merged = x2T
        raw_in = sem("raw_in")
        gate_in = [sem("gate_in0"), sem("gate_in1")]
        high_made, low_made, gated, merged_done = sem("high_made"), sem("low_made"), sem("gated"), sem("merged_done")
        x2_out = sem("x2_out")
        block = ctx.enter_context(nc.Block())

        @block.sync
        def _(sp):
            sp.dma_start(raw[:, :, :], tmp["ya"]).then_inc(raw_in, 16)
            for st, (_, name) in enumerate(stages):
                if st == 0:
                    for u in range(2):
                        load_weights(sp, wt, io[name], u * P, u, u, first=True)
                with sp.Fori(1 if st == 0 else 0, KT // 2) as i:
                    for u in range(2):
                        load_weights(sp, wt, io[name], (2 * i + u) * P, st * KT + 2 * i + u, u)
                if st < 3:
                    sp.wait_ge(low_made, KT * (st + 1))
                    sp.dma_start(raw[:, :, :], tmp[stages[st + 1][0]] if st < 2 else tmp["xT"]).then_inc(raw_in, 16)
            sp.wait_ge(gated, 4 * KT)
            sp.dma_start(tmp["x2T"], x2T[:, :, :]).then_inc(x2_out, 16)
            sp.wait_ge(x2_out, 16)

        @block.gpsimd
        def _(pool):
            for u in range(2):
                cut_weights(pool, wt, u, 0, u, first=True)
            with pool.Fori(1, 4 * KT // 2) as i:
                for u in range(2):
                    cut_weights(pool, wt, u, i, 2 * i + u)

        @block.tensor
        def _(pe):
            for st in range(4):
                for s in range(2):
                    w = st * KT + s
                    pe.wait_ge(wt.low_made, w + 1)
                    if st:
                        pe.wait_ge(gated, w - 1)
                    multiply(pe, wt, high, low, ps[:, s, :, :], s, cut=(low_made, KT * st) if s == 0 else None)
                with pe.Fori(1, KT // 2) as i:
                    for s in range(2):
                        w = st * KT + 2 * i + s
                        pe.wait_ge(wt.low_made, w + 1)
                        pe.wait_ge(gated, w - 1)
                        multiply(pe, wt, high, low, ps[:, s, :, :], s)

        @block.scalar
        def _(act):
            for st in range(4):
                for c in range(KT):
                    if c == 0:
                        if st < 3:
                            act.wait_ge(raw_in, 16 * (st + 1))
                        else:
                            act.wait_ge(merged_done, 2 * KT)
                        if st:
                            act.wait_ge(wt.product_done, st * KT)
                    act.copy(high[:, c, :], raw[:, c, :] if st < 3 else merged[:, c, :]).then_inc(high_made, 1)
                if st == 3:
                    break
                if st == 0:
                    for s in range(2):
                        act.dma_start(gate[:, s, :], tmp["gate"][:, s, :]).then_inc(gate_in[s], 16)
                with act.Fori(1 if st == 0 else 0, KT // 2) as i:
                    for s in range(2):
                        w = st * KT + 2 * i + s
                        act.wait_ge(gated, w - 1)
                        act.dma_start(gate[:, s:s + 1, :], tmp["gate"][:, ds(w, 1), :]).then_inc(gate_in[s], 16)

        @block.vector
        def _(dve):
            for st in range(4):
                for c in range(KT):
                    dve.wait_ge(high_made, st * KT + c + 1)
                    src = raw[:, c, :] if st < 3 else merged[:, c, :]
                    dve.tensor_tensor(low[:, c, :], src, high[:, c, :].bitcast(F32), ALU.subtract).then_inc(low_made, 1)
                if st == 3:
                    dve.wait_ge(raw_in, 64)
                    dve.wait_ge(low_made, 4 * KT)
                with dve.Fori(0, KT // 2) as i:
                    for s in range(2):
                        c = 2 * i + s
                        w = st * KT + c
                        dve.wait_ge(wt.product_done, w + 1)
                        if st < 3:
                            dve.wait_ge(gate_in[s], 16 * (st * (KT // 2)) + 16 * i + 16)
                        for n in range(NCH):
                            at = merged[:, ds(c, 1), chunk(n)].rearrange("p o n -> p (o n)")
                            if st == 0:
                                last = dve.tensor_tensor(at, ps[:, s, n, 0:CH], gate[:, s, chunk(n)], ALU.mult)
                            elif st < 3:
                                last = dve.tensor_tensor(part[:, s, chunk(n)], ps[:, s, n, 0:CH], gate[:, s, chunk(n)], ALU.mult)
                            else:
                                x_at = raw[:, ds(c, 1), chunk(n)].rearrange("p o n -> p (o n)")
                                last = dve.tensor_tensor(at, ps[:, s, n, 0:CH], x_at, ALU.add)
                        last.then_inc(gated, 1)
                        if st in (1, 2):
                            dve.wait_ge(gated, w + 1)
                            dve.tensor_tensor(merged[:, ds(c, 1), :], merged[:, ds(c, 1), :], part[:, s:s + 1, :], ALU.add).then_inc(merged_done, 1)


LOWEST = -3.4028234663852886e38
TOP_A, TOP_B = 4, 4
assert (TOP_A + 1) * (TOP_B + 1) > TOPK
WIDE = TOP_A * TOPK
PAIRS = WIDE + (TOPK - TOP_A) * TOP_B


def top_experts(nc, k, io, high, low, chosen, wt):
    HK = H * TOPK
    TK = NT * TOPK
    tiles = 2 * KT
    with ExitStack() as ctx:
        def sb(name, shape, dt=F32):
            return ctx.enter_context(nc.sbuf_tensor("tk_" + name, shape, dt))

        def sem(name):
            return nc.alloc_semaphore("tk_" + name)

        ps = ctx.enter_context(nc.psum_tensor("tk_ps", [P, 8, 512], F32))
        keys = sb("keys", [P, 2, P])
        keysT = sb("keysT", [P, tiles, P])
        qT = [sb(f"qT{s}", [P, NT * P]) for s in range(2)]
        score = [sb(f"score{s}", [P, NT, P]) for s in range(2)]
        rest = sb("rest", [P, NT, P])
        top = [sb(f"top{s}", [P, NT, TOPK]) for s in range(2)]
        at = [sb(f"at{s}", [P, NT, TOPK], U32) for s in range(2)]
        keys_in = [sem("keys_in0"), sem("keys_in1")]
        turned, keysT_kept, padded = sem("turned"), sem("keysT_kept"), sem("padded")
        evacuated, scored, score_kept, found = (sem(n) for n in ("evacuated", "scored", "score_kept", "found"))
        where = [sb(f"where{s}", [P, NT, TOPK]) for s in range(2)]
        cand, cand_rest = sb("cand", [P, NT, PAIRS]), sb("cand_rest", [P, NT, PAIRS])
        sums = sb("sums", [P, NT, TOPK])
        sums_at = sb("sums_at", [P, NT, TOPK], U32)
        rank_i = sb("rank_i", [P, 2, TK], U32)
        rank_f = sb("rank_f", [P, 4, TK])
        rank = sb("rank", [P, 2, TK])
        is_rank = [sb(f"is_rank{p}", [P, TK, TOPK]) for p in range(2)]
        shifted, total, inv = sb("shifted", [P, NT, TOPK]), sb("total", [P, NT]), sb("inv", [P, NT])
        rows = sb("rows", [P, NT, 3, HK])
        step, passed, ranked, picked0, picked1, shifted_done, raised, rows_turned, rows_kept = (
            sem(n) for n in ("step", "passed", "ranked", "picked0", "picked1", "shifted_done", "raised", "rows_turned", "rows_kept"))
        steps = 2 * 4 + 11 + 4
        block = ctx.enter_context(nc.Block())

        @block.sync
        def _(sp):
            for w in range(tiles):
                if w >= 2:
                    sp.wait_ge(turned, w - 1)
                sp.dma_start(keys[:, w % 2, :], io["peer_sub_keys"][w % 2, w // 2]).then_inc(keys_in[w % 2], 16)
            with sp.Fori(1, tiles // 2) as i:
                for u in range(2):
                    load_weights(sp, wt, io["peer_w_q"], (2 * i + u) * P, 2 * i + u, u)

        def pick_keys(pool, h):
            for p, picked in enumerate((picked0, picked1)):
                v = is_rank[p][:, :, :].rearrange("p (t k) a -> p t k a", t=NT)
                keys_of = where[p][:, :, :].unsqueeze(2).broadcast_to([P, NT, TOPK, TOPK])
                pool.wait_ge(ranked, 2 * h + p + 1)
                pool.tensor_tensor(v, v, keys_of, ALU.mult).then_inc(picked, 1)

        @block.gpsimd
        def _(pool):
            for s in range(2):
                pool.memset(qT[s][:, N:NT * P], 0.0).then_inc(padded, 1)
            cut_weights(pool, wt, 0, 1, 2)
            with pool.Fori(1, H - 1) as i:
                cut_weights(pool, wt, 1, i, 2 * i + 1)
                cut_weights(pool, wt, 0, i + 1, 2 * i + 2)
                pick_keys(pool, i - 1)
            cut_weights(pool, wt, 1, H - 1, tiles - 1)
            pick_keys(pool, H - 2)
            pick_keys(pool, H - 1)

        def product_banks(s):
            return ps[:, 3 * s:3 * s + NCH, :]

        def score_bank(s, t):
            return ps[:, 6 + t // 4, (t % 4) * P:(t % 4 + 1) * P] if t < NT - 1 else ps[:, 3 * s, CH:CH + P]

        @block.tensor
        def _(pe):
            for w in range(tiles):
                pe.wait_ge(keys_in[w % 2], 16 * (w // 2 + 1))
                if w >= 2:
                    pe.wait_ge(keysT_kept, w - 1)
                pe.transpose(ps[:, w % 2, 0:P], keys[:, w % 2, :], k["ident"][:, :]).then_inc(turned, 1)
            pe.wait_ge(keysT_kept, tiles)
            pe.wait_ge(padded, 2)

            def product(w, s, first=False):
                pe.wait_ge(wt.low_made, w + 1)
                if not first:
                    pe.wait_ge(evacuated, w - 1)
                    pe.wait_ge(score_kept, w - 1)
                multiply(pe, wt, high, low, product_banks(s), s)

            def scores(w, s, first=False):
                pe.wait_ge(evacuated, w + 1)
                if not first:
                    pe.wait_ge(score_kept, w)
                for t in range(NT):
                    last = pe.matmul(score_bank(s, t), qT[s][:, t * P:(t + 1) * P],
                                     keysT[:, ds(w, 1), :].rearrange("p o k -> p (o k)"), start=True, stop=True)
                last.then_inc(scored, 1)

            product(0, 0, first=True)
            product(1, 1, first=True)
            scores(0, 0, first=True)
            with pe.Fori(1, tiles // 2) as i:
                product(2 * i, 0)
                scores(2 * i - 1, 1)
                product(2 * i + 1, 1)
                scores(2 * i, 0)
            scores(tiles - 1, 1)
            pe.wait_ge(score_kept, tiles)
            pe.wait_ge(step, H * steps)
            for t in range(NT):
                if t >= 2:
                    pe.wait_ge(rows_kept, t - 1)
                for n in range(3):
                    last = pe.transpose(ps[:, t % 2, n * P:(n + 1) * P], rows[:, t, n, :], k["ident"][:, :])
                last.then_inc(rows_turned, 1)

        @block.scalar
        def _(act):
            def keep_scores(w, s, first=False):
                act.wait_ge(scored, w + 1)
                if not first:
                    act.wait_ge(found, w - 1)
                for b in range(2):
                    act.copy(score[s][:, 4 * b:4 * b + 4, :], ps[:, 6 + b, :].rearrange("p (t k) -> p t k", k=P))
                act.copy(score[s][:, NT - 1, :], score_bank(s, NT - 1)).then_inc(score_kept, 1)

            def keep_q(w, s):
                act.wait_ge(wt.product_done, w + 1)
                for n in range(NCH):
                    last = act.copy(qT[s][:, chunk(n)], product_banks(s)[:, n, 0:CH])
                last.then_inc(evacuated, 1)

            def raise_sums(h):
                act.wait_ge(shifted_done, h + 1)
                act.activation(shifted[:, :, :], shifted[:, :, :], ACT.Exp).then_inc(raised, 1)

            keep_q(0, 0)
            keep_q(1, 1)
            keep_scores(0, 0, first=True)
            keep_q(2, 0)
            keep_scores(1, 1, first=True)
            keep_q(3, 1)
            keep_scores(2, 0)
            raise_sums(0)
            with act.Fori(2, tiles // 2) as i:
                keep_q(2 * i, 0)
                keep_scores(2 * i - 1, 1)
                keep_q(2 * i + 1, 1)
                keep_scores(2 * i, 0)
                raise_sums(i - 1)
            keep_scores(tiles - 1, 1)
            raise_sums(H - 1)
            for t in range(NT):
                act.wait_ge(rows_turned, t + 1)
                act.copy(chosen[:, :, t * P:(t + 1) * P], ps[:, t % 2, 0:3 * P].rearrange("p (n c) -> p n c", n=3)).then_inc(rows_kept, 1)

        @block.vector
        def _(dve):
            for w in range(tiles):
                dve.wait_ge(turned, w + 1)
                dve.tensor_copy(keysT[:, w, :], ps[:, w % 2, 0:P]).then_inc(keysT_kept, 1)

            def search(h, s, own, first=False):
                w = 2 * h + s
                dve.wait_ge(score_kept, w + 1)
                pass_waits(dve, passed)
                for t in range(NT):
                    last = dve.max(out=top[s][:, t, 0:8], in_=score[s][:, t, :])
                own.did(last)
                own.wait()
                pass_waits(dve, passed)
                for t in range(NT):
                    dve.max_index(out=at[s][:, t, 0:8], in_max=top[s][:, t, 0:8], in_values=score[s][:, t, :])
                    last = dve.match_replace(out=rest[:, t, :], in_to_replace=top[s][:, t, 0:8],
                                             in_values=score[s][:, t, :], imm_value=LOWEST)
                own.did(last)
                own.wait()
                pass_waits(dve, passed)
                for t in range(NT):
                    last = dve.max(out=top[s][:, t, 8:16], in_=rest[:, t, :])
                own.did(last)
                own.wait()
                pass_waits(dve, passed)
                for t in range(NT):
                    last = dve.max_index(out=at[s][:, t, 8:16], in_max=top[s][:, t, 8:16], in_values=rest[:, t, :])
                last.then_inc(found, 1)
                if not first:
                    dve.wait_ge((picked0, picked1)[s], h)
                dve.wait_ge(found, w + 1)
                own.did(dve.tensor_copy(where[s][:, :, :], at[s][:, :, :]))

            def select(h, own):
                for a0, a1, nb, at0 in ((0, TOP_A, TOPK, 0), (TOP_A, TOPK, TOP_B, WIDE)):
                    one = top[0][:, :, a0:a1].unsqueeze(3).broadcast_to([P, NT, a1 - a0, nb])
                    two = top[1][:, :, 0:nb].unsqueeze(2).broadcast_to([P, NT, a1 - a0, nb])
                    pairs = cand[:, :, at0:at0 + (a1 - a0) * nb].rearrange("p t (a b) -> p t a b", b=nb)
                    last = dve.tensor_tensor(pairs, one, two, ALU.add)
                own.did(last)
                own.wait()
                pass_waits(dve, passed)
                for t in range(NT):
                    last = dve.max(out=sums[:, t, 0:8], in_=cand[:, t, :])
                own.did(last)
                own.wait()
                pass_waits(dve, passed)
                for t in range(NT):
                    dve.max_index(out=sums_at[:, t, 0:8], in_max=sums[:, t, 0:8], in_values=cand[:, t, :])
                    last = dve.match_replace(out=cand_rest[:, t, :], in_to_replace=sums[:, t, 0:8], in_values=cand[:, t, :],
                                             imm_value=LOWEST)
                own.did(last)
                own.wait()
                pass_waits(dve, passed)
                for t in range(NT):
                    last = dve.max(out=sums[:, t, 8:16], in_=cand_rest[:, t, :])
                own.did(last)
                own.wait()
                dve.tensor_tensor(shifted[:, :, :], sums[:, :, :], over_columns(sums[:, :, 0], TOPK), ALU.subtract).then_inc(shifted_done, 1)
                for t in range(NT):
                    last = dve.max_index(out=sums_at[:, t, 8:16], in_max=sums[:, t, 8:16], in_values=cand_rest[:, t, :])
                own.did(last)
                own.wait()
                flat_at = sums_at[:, :, :].rearrange("p t k -> p (t k)")
                dve.tensor_scalar(rank_i[:, 0, :], flat_at, 4, None, ALU.logical_shift_right)
                own.did(dve.tensor_scalar(rank_i[:, 1, :], flat_at, 2, None, ALU.logical_shift_right))
                own.wait()
                dve.tensor_copy(rank_f[:, 2, :], flat_at)
                own.did(dve.tensor_copy(rank_f[:, 0:2, :], rank_i[:, :, :]))
                own.wait()
                own.did(dve.scalar_tensor_tensor(out=rank[:, 0, :], in0=rank_f[:, 1, :], scalar=float(TOP_A - WIDE // TOP_B),
                                                 in1=rank_f[:, 0, :], op0=ALU.add, op1=ALU.max))
                own.wait()
                own.did(dve.tensor_scalar(rank_f[:, 3, :], rank[:, 0, :], float(TOP_B), float(WIDE - TOP_A * TOP_B), ALU.mult, ALU.add))
                own.wait()
                own.did(dve.scalar_tensor_tensor(out=rank_f[:, 3, :], in0=rank[:, 0, :], scalar=float(TOPK), in1=rank_f[:, 3, :],
                                                 op0=ALU.mult, op1=ALU.min))
                own.wait()
                own.did(dve.tensor_tensor(rank[:, 1, :], rank_f[:, 2, :], rank_f[:, 3, :], ALU.subtract))
                own.wait()
                ranks = k["iota"][:, 0:TOPK]
                for p in range(2):
                    dve.tensor_tensor(is_rank[p][:, :, :], over_heads(ranks, TK), over_columns(rank[:, p, :], TOPK), ALU.is_equal).then_inc(ranked, 1)

            def finish(h, own):
                def row(n):
                    return rows[:, :, n:n + 1, ds(h * TOPK, TOPK)].rearrange("p t o k -> p t (o k)")

                def keys_of(p):
                    return is_rank[p][:, :, :].rearrange("p (t k) a -> p t k a", t=NT)

                dve.wait_ge(raised, h + 1)
                own.did(dve.tensor_reduce(total[:, :], shifted[:, :, :], X, ALU.add))
                own.wait()
                own.did(dve.reciprocal(inv[:, :], total[:, :]))
                dve.wait_ge(picked0, h + 1)
                own.did(dve.tensor_reduce(row(0), keys_of(0), X, ALU.add))
                own.wait()
                dve.tensor_tensor(row(2), shifted[:, :, :], over_columns(inv[:, :], TOPK), ALU.mult)
                dve.wait_ge(picked1, h + 1)
                own.did(dve.tensor_reduce(row(1), keys_of(1), X, ALU.add))

            def head(h, first=False):
                own = Steps(dve, step, h * steps - 4)
                if first:
                    own = Steps(dve, step)
                for s in range(2):
                    search(h, s, own, first)
                if not first:
                    finish(h - 1, own)
                select(h, own)
                assert own.n == steps - (4 if first else 0), own.n

            head(0, first=True)
            with dve.Fori(1, H) as h:
                head(h)
            own = Steps(dve, step, H * steps - 4)
            finish(H - 1, own)


GATE_BLOCK = 88


def spread_gates(nc, k, tmp, chosen):
    UN = 8
    BT = GATE_BLOCK
    per = BT // UN
    blocks = N // BT
    with ExitStack() as ctx:
        def sb(name, shape, dt=F32):
            return ctx.enter_context(nc.sbuf_tensor("sg_" + name, shape, dt))

        def sem(name):
            return nc.alloc_semaphore("sg_" + name)

        first_key = [sb(f"first{s}", [P, UN, P]) for s in range(2)]
        weighted = [sb(f"weighted{s}", [P, UN, P]) for s in range(2)]
        second_key = [sb(f"second{s}", [P, UN, P]) for s in range(2)]
        out = [sb(f"out{s}", [P, P, BT]) for s in range(2)]
        ps = ctx.enter_context(nc.psum_tensor("sg_ps", [P, 8, 4, P], F32))
        first_made, second_made, weights_on, spread, kept = (
            sem(n) for n in ("first_made", "second_made", "weights_on", "spread", "kept"))
        stored = [sem("stored0"), sem("stored1")]
        block = ctx.enter_context(nc.Block())

        def all_turns(turn, eng):
            def two_blocks(i, first=False):
                for bs in range(2):
                    for r in range(per):
                        q = 2 * i * per + bs * per + r
                        turn(q, (bs * per + r) % 2, first and bs * per + r < 2)

            two_blocks(0, first=True)
            with eng.Fori(1, blocks // 2) as i:
                two_blocks(i)

        @block.vector
        def _(dve):
            def turn(q, s, first):
                for made, n, used, hot in ((first_made, 0, weights_on, first_key), (second_made, 1, spread, second_key)):
                    if not first:
                        dve.wait_ge(used, q - 1)
                    dve.tensor_tensor(hot[s][:, :, :], over_heads(k["iota"][:, :], UN),
                                      over_columns(chosen[:, n, ds(q * UN, UN)]), ALU.is_equal).then_inc(made, 1)

            all_turns(turn, dve)

        @block.gpsimd
        def _(pool):
            def turn(q, s, first):
                pool.wait_ge(first_made, q + 1)
                if not first:
                    pool.wait_ge(spread, q - 1)
                pool.tensor_tensor(weighted[s][:, :, :], first_key[s][:, :, :],
                                   over_columns(chosen[:, 2, ds(q * UN, UN)]), ALU.mult).then_inc(weights_on, 1)

            all_turns(turn, pool)

        @block.tensor
        def _(pe):
            def turn(q, s, first):
                pe.wait_ge(weights_on, q + 1)
                pe.wait_ge(second_made, q + 1)
                if not first:
                    pe.wait_ge(kept, q - 1)
                for u in range(UN):
                    last = pe.matmul(ps[:, 4 * s + u // 4, u % 4, :], second_key[s][:, u, :], weighted[s][:, u, :],
                                     start=True, stop=True)
                last.then_inc(spread, 1)

            all_turns(turn, pe)

        @block.scalar
        def _(act):
            def keep(q, bs, r):
                act.wait_ge(spread, q + 1)
                for b in range(UN // 4):
                    at = r * UN + 4 * b
                    last = act.copy(out[bs][:, :, at:at + 4], ps[:, 4 * ((bs * per + r) % 2) + b, :, :].rearrange("p n i -> p i n"))
                last.then_inc(kept, 1)

            def two_blocks(i, first=False):
                for bs in range(2):
                    if not first:
                        act.wait_ge(stored[bs], 16 * i)
                    for r in range(per):
                        keep((2 * i + bs) * per + r, bs, r)

            two_blocks(0, first=True)
            with act.Fori(1, blocks // 2) as i:
                two_blocks(i)

        @block.sync
        def _(sp):
            with sp.Fori(0, blocks // 2) as i:
                for bs in range(2):
                    sp.wait_ge(kept, (2 * i + bs) * per + per)
                    sp.dma_start(tmp["gates"][ds(2 * i + bs, 1), :, :, :].rearrange("o j i n -> j (o i) n"), out[bs][:, :, :]).then_inc(stored[bs], 16)
            for bs in range(2):
                sp.wait_ge(stored[bs], 16 * (blocks // 2))


def experts(nc, k, io, tmp, h_high, h_low, yT):
    tiles = NE // P
    groups = tiles // 2
    with ExitStack() as ctx:
        def sb(name, shape, dt=F32):
            return ctx.enter_context(nc.sbuf_tensor("ex_" + name, shape, dt))

        def sem(name):
            return nc.alloc_semaphore("ex_" + name)

        u_raw, v_raw = sb("u_raw", [P, 2, D]), sb("v_raw", [P, 2, D])
        uT_high = [sb(f"uT_high{s}", [P, KT, P], F32R) for s in range(2)]
        uT_low = [sb(f"uT_low{s}", [P, KT, P], F32R) for s in range(2)]
        v_high = [sb(f"v_high{s}", [P, D], F32R) for s in range(2)]
        v_low = [sb(f"v_low{s}", [P, D], F32R) for s in range(2)]
        gate = sb("gate", [P, 2, N])
        coef = sb("coef", [P, N])
        c_high = [[sb(f"c_high{a}{s}", [P, N], F32R) for s in range(2)] for a in range(2)]
        c_low = [[sb(f"c_low{a}{s}", [P, N], F32R) for s in range(2)] for a in range(2)]
        ps_t = ctx.enter_context(nc.psum_tensor("ex_t", [P, 2, 4, P], F32))
        ps_a = ctx.enter_context(nc.psum_tensor("ex_a", [P, NCH, 512], F32))
        ps_y = ctx.enter_context(nc.psum_tensor("ex_y", [P, 3, 512], F32))
        names = "x2_in u_turned uT_high_made uT_low_made acted gelu_done weighted coef_high coef_low v_high_made v_low_made multiplied summed".split()
        m = {n: sem(n) for n in names}
        u_in, v_in, g_in = ([sem(f"{n}{s}") for s in range(2)] for n in ("u_in", "v_in", "g_in"))
        units = KT * NCH
        block = ctx.enter_context(nc.Block())

        @block.sync
        def _(sp):
            def load(g, first=False):
                for s in range(2):
                    e = 2 * g + s
                    if not first:
                        sp.wait_ge(m["weighted"], e - 1)
                    sp.dma_start(gate[:, s, :].rearrange("p (b n) -> p b n", n=GATE_BLOCK),
                                 tmp["gates"][:, :, ds(e, 1), :].rearrange("b j o n -> j b (o n)")).then_inc(g_in[s], 16)
                    if not first:
                        sp.wait_ge(m["v_low_made"], e - 1)
                    sp.dma_start(v_raw[:, s, :], io["peer_v"][ds(e * P, P), :]).then_inc(v_in[s], 16)

            for s in range(2):
                sp.dma_start(u_raw[:, s, :], io["peer_u"][s * P:(s + 1) * P, :]).then_inc(u_in[s], 16)
            load(0, first=True)
            sp.dma_start(yT[:, :, :], tmp["x2T"]).then_inc(m["x2_in"], 16)
            with sp.Fori(1, groups) as g:
                load(g)

        @block.tensor
        def _(pe):
            def turn(g, s, first=False):
                e = 2 * g + s
                pe.wait_ge(u_in[s], 16 * g + 16)
                if not first:
                    pe.wait_ge(m["uT_low_made"], e)
                for c in range(KT):
                    last = pe.transpose(ps_t[:, c // 4, c % 4, :], u_raw[:, s, c * P:(c + 1) * P], k["ident"][:, :])
                last.then_inc(m["u_turned"], 1)

            def products(g, s, first=False):
                e = 2 * g + s
                pe.wait_ge(m["uT_low_made"], e + 1)
                if not first:
                    pe.wait_ge(m["gelu_done"], e)
                for n in range(NCH):
                    for c in range(KT):
                        for a, b in ((uT_high[s], h_high), (uT_high[s], h_low), (uT_low[s], h_high)):
                            last = pe.matmul(ps_a[:, n, 0:CH], a[:, c, :], b[:, c, chunk(n)],
                                             start=(c == 0 and a is uT_high[s] and b is h_high),
                                             stop=(c == KT - 1 and a is uT_low[s]))
                last.then_inc(m["acted"], 1)

            def values(g, a, first=False):
                pe.wait_ge(m["coef_low"], 2 * g + 2)
                pe.wait_ge(m["v_low_made"], 2 * g + 2)
                for c in range(KT):
                    for n in range(NCH):
                        q = c * NCH + n
                        if not first:
                            pe.wait_ge(m["summed"], g * units + q - 2)
                        elif q >= 3:
                            pe.wait_ge(m["summed"], q - 2)
                        for s in range(2):
                            for x, y in ((v_high[s], c_high[a][s]), (v_high[s], c_low[a][s]), (v_low[s], c_high[a][s])):
                                last = pe.matmul(ps_y[:, n, 0:CH], x[:, c * P:(c + 1) * P], y[:, chunk(n)],
                                                 start=(s == 0 and x is v_high[0] and y is c_high[a][0]),
                                                 stop=(s == 1 and x is v_low[1]))
                        last.then_inc(m["multiplied"], 1)

            turn(0, 0, first=True)
            turn(0, 1)
            products(0, 0, first=True)
            turn(1, 0)
            products(0, 1)
            turn(1, 1)
            products(1, 0)
            turn(2, 0)
            products(1, 1)
            values(0, 0, first=True)

            def pair(i, last=False):
                for a in range(2):
                    g = 2 * i + a
                    turn(g, 1)
                    products(g, 0)
                    if not (last and a == 1):
                        turn(g + 1, 0)
                    products(g, 1)
                    values(g - 1, 1 - a)

            with pe.Fori(1, groups // 2 - 1) as i:
                pair(i)
            pair(groups // 2 - 1, last=True)
            values(groups - 1, 1)

        @block.scalar
        def _(act):
            def turned(g, s, first=False, last=False):
                e = 2 * g + s
                act.wait_ge(m["u_turned"], e + 1)
                if not last:
                    act.dma_start(u_raw[:, s, :], io["peer_u"][ds((e + 2) * P, P), :]).then_inc(u_in[s], 16)
                if not first:
                    act.wait_ge(m["acted"], e - 1)
                for b in range(2):
                    last = act.copy(uT_high[s][:, 4 * b:4 * b + 4, :], ps_t[:, b, :, :])
                last.then_inc(m["uT_high_made"], 1)

            def gelu(g, s, first=False):
                e = 2 * g + s
                act.wait_ge(m["acted"], e + 1)
                if not first:
                    act.wait_ge(m["coef_low"], e)
                for n in range(NCH):
                    last = act.activation(coef[:, chunk(n)], ps_a[:, n, 0:CH], ACT.Gelu)
                last.then_inc(m["gelu_done"], 1)

            def cut_v(g, first=False):
                for s in range(2):
                    act.wait_ge(v_in[s], 16 * g + 16)
                    if not first:
                        act.wait_ge(m["multiplied"], g * units)
                    act.copy(v_high[s][:, :], v_raw[:, s, :]).then_inc(m["v_high_made"], 1)

            def group(g, kind=None):
                turned(g, 1, first=(kind == "first"), last=(kind == "last"))
                if kind != "first":
                    cut_v(g - 1, first=(kind == "second"))
                gelu(g, 0, first=(kind == "first"))
                if kind != "last":
                    turned(g + 1, 0, last=(kind == "last but one"))
                gelu(g, 1)

            turned(0, 0, first=True)
            group(0, "first")
            group(1, "second")
            with act.Fori(1, groups // 2 - 1) as i:
                for a in range(2):
                    group(2 * i + a)
            group(groups - 2, "last but one")
            group(groups - 1, "last")
            cut_v(groups - 1)

        @block.vector
        def _(dve):
            def turned(g, s):
                e = 2 * g + s
                dve.wait_ge(m["uT_high_made"], e + 1)
                for b in range(2):
                    last = dve.tensor_tensor(uT_low[s][:, 4 * b:4 * b + 4, :], ps_t[:, b, :, :],
                                             uT_high[s][:, 4 * b:4 * b + 4, :].bitcast(F32), ALU.subtract)
                last.then_inc(m["uT_low_made"], 1)

            def weigh(g, a, s):
                e = 2 * g + s
                dve.wait_ge(m["gelu_done"], e + 1)
                dve.wait_ge(g_in[s], 16 * g + 16)
                dve.tensor_tensor(coef[:, :], coef[:, :], gate[:, s, :], ALU.mult).then_inc(m["weighted"], 1)
                dve.wait_ge(m["weighted"], e + 1)
                dve.tensor_copy(c_high[a][s][:, :], coef[:, :]).then_inc(m["coef_high"], 1)
                dve.wait_ge(m["coef_high"], e + 1)
                dve.tensor_tensor(c_low[a][s][:, :], coef[:, :], c_high[a][s][:, :].bitcast(F32), ALU.subtract).then_inc(m["coef_low"], 1)

            def cut_v(g):
                for s in range(2):
                    dve.wait_ge(m["v_high_made"], 2 * g + s + 1)
                    dve.tensor_tensor(v_low[s][:, :], v_raw[:, s, :], v_high[s][:, :].bitcast(F32), ALU.subtract).then_inc(m["v_low_made"], 1)

            def sum_up(g):
                for c in range(KT):
                    for n in range(NCH):
                        dve.wait_ge(m["multiplied"], g * units + c * NCH + n + 1)
                        at = yT[:, c, chunk(n)]
                        dve.tensor_tensor(at, at, ps_y[:, n, 0:CH], ALU.add).then_inc(m["summed"], 1)

            def group(g, a, kind=None):
                turned(g, 1)
                if kind != "first":
                    cut_v(g - 1)
                    weigh(g - 1, 1 - a, 1)
                weigh(g, a, 0)
                if kind != "last":
                    turned(g + 1, 0)
                if kind != "first":
                    sum_up(g - 1)

            turned(0, 0)
            group(0, 0, "first")
            dve.wait_ge(m["x2_in"], 16)
            group(1, 1)
            with dve.Fori(1, groups // 2 - 1) as i:
                for a in range(2):
                    group(2 * i + a, a)
            group(groups - 2, 0)
            group(groups - 1, 1, "last")
            cut_v(groups - 1)
            weigh(groups - 1, 1, 1)
            sum_up(groups - 1)


def norm_rows_out(nc, k, yT, gain_dram, dram):
    with ExitStack() as ctx:
        def sb(name, shape):
            return ctx.enter_context(nc.sbuf_tensor("ro_" + name, shape, F32))

        def sem(name):
            return nc.alloc_semaphore("ro_" + name)

        SLOTS = 3
        gain = sb("gain", [P, D])
        sq = sb("sq", [P, 3, N])
        total = sb("total", [1, NT * P])
        root, rinv = sb("root", [P, NT]), sb("rinv", [P, NT])
        rows = sb("rows", [P, SLOTS, D])
        ps = ctx.enter_context(nc.psum_tensor("ro_ps", [P, 2, 2, 512], F32))
        row_sums = ctx.enter_context(nc.psum_tensor("ro_row_sums", [1, NCH, 512], F32))
        sums = ctx.enter_context(nc.psum_tensor("ro_sums", [P, NT], F32))
        gain_in, squared, summed, row_kept, in_columns, rooted, inverted, turned, scaled = (
            sem(n) for n in ("gain_in", "squared", "summed", "row_kept", "in_columns", "rooted", "inverted", "turned", "scaled"))
        stored = [sem(f"stored{s}") for s in range(SLOTS)]
        size = [min(P, N - t * P) for t in range(NT)]
        block = ctx.enter_context(nc.Block())

        @block.tensor
        def _(pe):
            def turn(t):
                if t >= 2:
                    pe.wait_ge(scaled, t - 1)
                for c in range(KT):
                    last = pe.transpose(ps[0:size[t], t % 2, c // 4, (c % 4) * P:(c % 4 + 1) * P],
                                        yT[:, c, t * P:t * P + size[t]], k["ident"][:, :])
                last.then_inc(turned, 1)

            for c in range(KT):
                pe.wait_ge(squared, c + 1)
                for n in range(NCH):
                    last = pe.matmul(row_sums[0:1, n, 0:CH], k["ones"][:, 0:1], sq[:, c % 3, chunk(n)],
                                     start=(c == 0), stop=(c == KT - 1))
                last.then_inc(summed, 1)
            turn(0)
            pe.wait_ge(row_kept, 1 + NCH)
            for t in range(NT):
                last = pe.matmul(sums[:, t:t + 1], total[0:1, t * P:(t + 1) * P], k["ones"][0:1, 0:1], start=True, stop=True)
            last.then_inc(in_columns, 1)
            for t in range(1, NT):
                turn(t)

        @block.scalar
        def _(act):
            for c in range(KT):
                if c >= 3:
                    act.wait_ge(summed, c - 2)
                act.activation(sq[:, c % 3, :], yT[:, c, :], ACT.Square).then_inc(squared, 1)
            act.wait_ge(in_columns, 1)
            act.activation(root[:, :], sums[:, :], ACT.Sqrt, bias=k["eps"][:, 0:1], scale=1.0 / D).then_inc(rooted, 1)

        @block.vector
        def _(dve):
            dve.memset(total[:, N:NT * P], 0.0).then_inc(row_kept, 1)
            dve.wait_ge(summed, KT)
            for n in range(NCH):
                dve.tensor_copy(total[:, chunk(n)], row_sums[0:1, n, 0:CH]).then_inc(row_kept, 1)
            dve.wait_ge(rooted, 1)
            dve.reciprocal(rinv[:, :], root[:, :]).then_inc(inverted, 1)
            dve.wait_ge(inverted, 1)
            dve.wait_ge(gain_in, 16)
            for t in range(NT):
                dve.wait_ge(turned, t + 1)
                if t >= SLOTS:
                    dve.wait_ge(stored[t % SLOTS], 16 * (t // SLOTS))
                dve.scalar_tensor_tensor(out=rows[0:size[t], t % SLOTS, :],
                                         in0=ps[0:size[t], t % 2, :, :].rearrange("p b n -> p (b n)"),
                                         scalar=rinv[0:size[t], t:t + 1], in1=gain[0:size[t], :],
                                         op0=ALU.mult, op1=ALU.mult).then_inc(scaled, 1)

        @block.sync
        def _(sp):
            sp.dma_start(gain[:, :], gain_dram.rearrange("o d -> (o d)").partition_broadcast(P)).then_inc(gain_in, 16)
            for t in range(NT):
                sp.wait_ge(scaled, t + 1)
                sp.dma_start(dram[t * P:t * P + size[t], :], rows[0:size[t], t % SLOTS, :]).then_inc(stored[t % SLOTS], 16)
            for s in range(SLOTS):
                sp.wait_ge(stored[s], 16 * len(range(s, NT, SLOTS)))


SHAPES = dict(
    x=(N, D), mem=(M, D), cache_mem_k=(NB, M, MH, D // MH), cache_mem_v=(NB, M, MH, D // MH),
    state_conv=(NB, CK - 1, D), state_gdn_conv=(NB, GK - 1, 3 * D), state_gdn=(NB, H, P, P),
    norm_mix_g=(1, D), w_in=(D, COL_GATE + 3 * D), conv_w=(CK, D), gdn_conv_w=(GK, 3 * D),
    gdn_a_log=(H,), gdn_dt_bias=(H,), gdn_norm_g=(P,), mem_norm_g=(1, D), w_mem_kv=(D, 2 * D),
    w_br_conv=(D, D), w_br_gdn=(D, D), w_br_mem=(D, D), w_out=(D, D), norm_ffn_g=(1, D),
    peer_w_q=(D, 2 * D), peer_sub_keys=(2, H, P, P), peer_u=(NE, D), peer_v=(NE, D), final_norm_g=(1, D))
OUTS = dict(
    out_y=(N, D), out_mem_k=(M, D), out_mem_v=(M, D), out_conv_p=(CK - 1, D), out_gconv_p=(GK - 1, 3 * D),
    out_gdn_p=(H, P, P), out_conv_s=(NB * (CK - 1), D), out_gconv_s=(NB * (GK - 1), 3 * D),
    out_gdn_s=(NB, H, P, P))


def build(nc, io):
    tmp = {name: nc.dram_tensor("tmp_" + name, shape, F32, kind="Internal").ap()
           for name, shape in dict(
               xT=(P, KT, N), ya=(P, KT, N), qkv=(P, 3 * KT, N), z=(P, KT, N), mq=(P, KT, N), gate=(P, 3 * KT, N),
               ym=(P, KT, N), yb=(P, KT, N), x2T=(P, KT, N), gates=(N // GATE_BLOCK, P, P, GATE_BLOCK)).items()}
    with ExitStack() as ctx:
        def sb(name, shape, dt=F32):
            return ctx.enter_context(nc.sbuf_tensor(name, shape, dt))

        k = dict(ones=sb("ones", [P, P]), eps=sb("eps", [P, 1]), ident=sb("ident", [P, P]),
                 iota_i=sb("iota_i", [P, P], I32), iota=sb("iota", [P, P]), upto=sb("upto", [P, P]),
                 after=sb("after", [P, P]), same_seq=sb("same_seq", [NS, NS]), chan_a=sb("chan_a", [P, KT, 32]),
                 chan_g=sb("chan_g", [P, 3 * KT, 32]), gdn_gain=sb("gdn_gain", [P, 1]), dt_bias=sb("dt_bias", [P, H]),
                 a_log=sb("a_log", [P, H]), decays=sb("decays", [P, 3, NT, H]), beta_decay=sb("beta_decay", [P, NT, H]),
                 level=sb("level", [P, len(LEVELS), P]), glog=sb("glog", [P, NT, H]), beta=sb("beta", [P, NT, H]))

        def gain(n):
            return k["chan_a"][:, :, A_GAIN + n:A_GAIN + n + 1]

        with nc.cleanup_on_exit(), ExitStack() as part:
            make_constants(nc, k, io)
            high = part.enter_context(nc.sbuf_tensor("h_high", [P, KT, N], F32R))
            low = part.enter_context(nc.sbuf_tensor("h_low", [P, KT, N], F32R))
            wt = Weights(nc, part, "w_in")
            with nc.sbuf_tensor("xT", [P, KT, N], F32) as xT:
                turn_rows(nc, k, io["x"], xT, NT, "x", save=tmp["xT"])
                norm_channels(nc, k, xT, gain(MIX), N, "mix", high=high, low=low, wt=wt,
                              first_tiles=[(io["w_in"], run_column("conv", 0, u)) for u in range(2)])
            project_in(nc, k, io, tmp, high, low, wt)
        with nc.cleanup_on_exit(), ExitStack() as part:
            memT, memn, kT = (part.enter_context(nc.sbuf_tensor(n, [P, KT, M], F32)) for n in ("memT", "memn", "kT"))
            v_rows = part.enter_context(nc.sbuf_tensor("v_rows", [P, MT, D], F32))
            turn_rows(nc, k, io["mem"], memT, MT, "mem")
            norm_channels(nc, k, memT, gain(MEM), M, "memn", out=memn)
            memory_kv(nc, k, io, memn, kT, v_rows)
            cache = part.enter_context(nc.sbuf_tensor("cache", [P, NB, MT, D], F32))
            cache_in = [nc.alloc_semaphore(f"cache_in{b}") for b in range(NB)]
            attend_prompt(nc, k, io, tmp, kT, v_rows, cache, cache_in)
            attend_samples(nc, k, io, tmp, cache, cache_in)
        with nc.cleanup_on_exit(), nc.sbuf_tensor("S_seq", [P, NB, H, P], F32) as S_seq:
            decay_sums(nc, k)
            S_seq_in = nc.alloc_semaphore("S_seq_in")
            delta_prompt(nc, k, io, tmp, S_seq, S_seq_in)
            delta_samples(nc, k, io, tmp, S_seq, S_seq_in)
        with ExitStack() as part:
            high = part.enter_context(nc.sbuf_tensor("h2_high", [P, KT, N], F32R))
            low = part.enter_context(nc.sbuf_tensor("h2_low", [P, KT, N], F32R))
            with nc.sbuf_tensor("chosen", [P, 3, NT * P], F32) as chosen:
                with nc.cleanup_on_exit(), ExitStack() as streams:
                    wt_merge = Weights(nc, streams, "w_mb")
                    wt_keys = Weights(nc, streams, "w_tk", slots_of=wt_merge)
                    with nc.sbuf_tensor("x2T", [P, KT, N], F32) as x2T:
                        merge_branches(nc, k, io, tmp, x2T, high, low, wt_merge)
                        norm_channels(nc, k, x2T, gain(FFN), N, "ffn", high=high, low=low, wt=wt_keys,
                                      first_tiles=[(io["peer_w_q"], u * P) for u in range(2)])
                    top_experts(nc, k, io, high, low, chosen, wt_keys)
                with nc.cleanup_on_exit():
                    spread_gates(nc, k, tmp, chosen)
            with nc.cleanup_on_exit(), nc.sbuf_tensor("yT", [P, KT, N], F32) as yT:
                experts(nc, k, io, tmp, high, low, yT)
                norm_rows_out(nc, k, yT, io["final_norm_g"], io["out_y"])


def kernel(**inputs):
    import numpy as _np
    import concourse.bacc as _bacc
    from concourse.bass_utils import run_bass_kernel_spmd as _run

    nc = _bacc.Bacc("TRN2", target_bir_lowering=False, num_devices=1)
    tokens = [_np.reshape(inputs[name], (-1, D)) for name in ("x_prompt", "x_sample")]
    named = dict(inputs, x=_np.concatenate(tokens), mem=inputs["mem_prompt"])
    io, arrays = {}, {}
    for name, shape in SHAPES.items():
        arrays["in_" + name] = _np.ascontiguousarray(_np.reshape(named[name], shape))
        io[name] = nc.dram_tensor("in_" + name, shape, F32, kind="ExternalInput").ap()
    for name, shape in OUTS.items():
        io[name] = nc.dram_tensor(name, shape, F32, kind="ExternalOutput").ap()
    build(nc, io)
    r = _run(nc, [arrays], core_ids=[0]).results[0]
    return (r["out_y"][:TP].reshape(1, TP, D), r["out_y"][TP:].reshape(NB, TS, D),
            r["out_mem_k"].reshape(1, 1, M, MH, D // MH), r["out_mem_v"].reshape(1, 1, M, MH, D // MH),
            r["out_conv_p"].reshape(1, 1, CK - 1, D), r["out_gconv_p"].reshape(1, 1, GK - 1, 3 * D),
            r["out_gdn_p"].reshape(1, 1, H, P, P), r["out_conv_s"].reshape(1, NB, CK - 1, D),
            r["out_gconv_s"].reshape(1, NB, GK - 1, 3 * D), r["out_gdn_s"].reshape(1, NB, H, P, P))
```
